# Optimizing a Trainium2 kernel written in Bass

```python
import math
import jax, jax.numpy as jnp
from jax import lax
import numpy as np

D_MODEL = 1024
BATCH = 1
SEQ = 1024
DEPTH = 1

HEAD_DIM = 64
N_Q_HEADS = 8
N_KV_HEADS = 2
GQ = N_Q_HEADS // N_KV_HEADS
WINDOW = 128
BLOCK = 128
ROPE_THETA = 10000.0
D_A = N_Q_HEADS * HEAD_DIM
D_KV = N_KV_HEADS * HEAD_DIM

CHUNK = 128
N_GROUPS = 4
D_B = D_MODEL // 2
GROUP_W = D_B // N_GROUPS

EPS = 1e-6
NEG = -1e30

SPLIT_SIZES = [D_A, D_KV, D_KV, D_A,
               D_B, D_B, D_B,
               2 * D_MODEL]
SPLIT_IDX = [int(s) for s in np.cumsum(SPLIT_SIZES)[:-1]]
D_IN = int(sum(SPLIT_SIZES))


def _rms(x, g):
    xf = x.astype(jnp.float32)
    y = xf * lax.rsqrt(jnp.mean(xf * xf, axis=-1, keepdims=True) + EPS)
    return (y * g.astype(jnp.float32)).astype(x.dtype)

def _layernorm(x, g, b):
    xf = x.astype(jnp.float32)
    mu = jnp.mean(xf, axis=-1, keepdims=True)
    var = jnp.mean(jnp.square(xf - mu), axis=-1, keepdims=True)
    y = (xf - mu) * lax.rsqrt(var + EPS)
    return (y * g.astype(jnp.float32) + b.astype(jnp.float32)).astype(x.dtype)

def _rope(t, positions):
    half = HEAD_DIM // 2
    inv_freq = ROPE_THETA ** (-jnp.arange(half, dtype=jnp.float32) / half)
    ang = positions.astype(jnp.float32)[..., None] * inv_freq
    cos = jnp.cos(ang)[:, :, None, :]
    sin = jnp.sin(ang)[:, :, None, :]
    tf = t.astype(jnp.float32)
    t1, t2 = tf[..., :half], tf[..., half:]
    out = jnp.concatenate([t1 * cos - t2 * sin, t2 * cos + t1 * sin], axis=-1)
    return out.astype(t.dtype)

def _band(t):
    b, s, h, d = t.shape
    tb = t.reshape(b, s // BLOCK, BLOCK, h, d)
    prev = jnp.pad(tb[:, :-1], ((0, 0), (1, 0), (0, 0), (0, 0), (0, 0)))
    return jnp.concatenate([prev, tb], axis=2)

def _swa_with_sinks(q, k, v, sinks):
    b, s = q.shape[:2]
    nb = s // BLOCK
    qb = q.reshape(b, nb, BLOCK, N_KV_HEADS, GQ, HEAD_DIM)
    kb, vb = _band(k), _band(v)
    scores = jnp.einsum('bnqkgd,bnjkd->bnkgqj', qb, kb).astype(jnp.float32)
    scores = scores * (1.0 / math.sqrt(HEAD_DIM))
    qi = jnp.arange(BLOCK)[:, None]
    kj = jnp.arange(2 * BLOCK)[None, :]
    rel = qi + BLOCK - kj
    in_win = (rel >= 0) & (rel < WINDOW)
    blk = jnp.arange(nb)[:, None, None]
    valid = in_win[None] & ((blk > 0) | (kj[None] >= BLOCK))
    scores = jnp.where(valid[None, :, None, None], scores, NEG)
    sink = sinks.astype(jnp.float32).reshape(N_KV_HEADS, GQ)[None, None, :, :, None, None]
    sink = jnp.broadcast_to(sink, scores.shape[:-1] + (1,))
    probs = jax.nn.softmax(jnp.concatenate([scores, sink], axis=-1), axis=-1)[..., :-1]
    out = jnp.einsum('bnkgqj,bnjkd->bnqkgd', probs.astype(v.dtype), vb)
    return out.reshape(b, s, N_Q_HEADS * HEAD_DIM)

def _chunked_spatial_gating(u, v, ln_g, ln_b, w_s, b_s):
    b, s, _ = v.shape
    nc = s // CHUNK
    vn = _layernorm(v, ln_g, ln_b).reshape(b, nc, CHUNK, N_GROUPS, GROUP_W)
    causal = jnp.tril(jnp.ones((CHUNK, CHUNK), dtype=bool))
    w = jnp.where(causal[None], w_s, jnp.zeros((), w_s.dtype))
    sv = jnp.einsum('gts,bnsgc->bntgc', w, vn) + b_s.T[None, None, :, :, None]
    return u * sv.reshape(b, s, D_B)

def first_inputs(seed: int = 0) -> dict:
    key = jax.random.key(seed)
    ks = jax.random.split(key, 18)
    f32 = jnp.float32
    nrm = lambda k, shape, s: jax.random.normal(k, shape, f32) * s
    x = jax.random.normal(ks[0], (BATCH, SEQ, D_MODEL), f32)
    c = jax.random.normal(ks[1], (BATCH, D_MODEL), f32)
    positions = jnp.broadcast_to(jnp.arange(SEQ, dtype=jnp.int32), (BATCH, SEQ))
    return {
        "x": x,
        "c": c,
        "positions": positions,
        "w_ada": nrm(ks[2], (DEPTH, D_MODEL, 3 * D_MODEL), 0.5 * D_MODEL ** -0.5),
        "b_ada": nrm(ks[3], (DEPTH, 3 * D_MODEL), 0.02),
        "g_pre": 1.0 + nrm(ks[4], (DEPTH, D_MODEL), 0.05),
        "g_post": 1.0 + nrm(ks[5], (DEPTH, D_MODEL), 0.05),
        "w_in": nrm(ks[6], (DEPTH, D_MODEL, D_IN), D_MODEL ** -0.5),
        "sinks": nrm(ks[7], (DEPTH, N_Q_HEADS), 1.0),
        "ln_v_g": 1.0 + nrm(ks[8], (DEPTH, D_B), 0.05),
        "ln_v_b": nrm(ks[9], (DEPTH, D_B), 0.02),
        "w_s": nrm(ks[10], (DEPTH, N_GROUPS, CHUNK, CHUNK), CHUNK ** -0.5),
        "b_s": 1.0 + nrm(ks[11], (DEPTH, N_GROUPS, CHUNK), 0.1),
        "w_proj_a": nrm(ks[12], (DEPTH, D_A, D_MODEL), D_A ** -0.5),
        "w_proj_b": nrm(ks[13], (DEPTH, D_B, D_MODEL), D_B ** -0.5),
        "w_out": nrm(ks[14], (DEPTH, D_MODEL, D_MODEL), D_MODEL ** -0.5),
    }

def first_block(x, c, positions, w_ada, b_ada, g_pre, g_post, w_in, sinks,
              ln_v_g, ln_v_b, w_s, b_s, w_proj_a, w_proj_b, w_out):
    b, s, _ = x.shape
    c_act = jax.nn.silu(c)
    for l in range(DEPTH):
        ada = (c_act @ w_ada[l] + b_ada[l])[:, None, :]
        shift, scale, gate = jnp.split(ada, 3, axis=-1)
        h = _rms(x, g_pre[l]) * (1.0 + scale) + shift

        proj = h @ w_in[l]
        q, k, v, z_a, u_b, v_b, z_b, g_logits = jnp.split(proj, SPLIT_IDX, axis=-1)

        q = _rope(q.reshape(b, s, N_Q_HEADS, HEAD_DIM), positions)
        k = _rope(k.reshape(b, s, N_KV_HEADS, HEAD_DIM), positions)
        v = v.reshape(b, s, N_KV_HEADS, HEAD_DIM)
        y_a = _swa_with_sinks(q, k, v, sinks[l]) * jax.nn.silu(z_a)

        y_b = _chunked_spatial_gating(jax.nn.gelu(u_b, approximate=False),
                                      jax.nn.gelu(v_b, approximate=False),
                                      ln_v_g[l], ln_v_b[l], w_s[l], b_s[l])
        y_b = y_b * jax.nn.silu(z_b)

        gates = jax.nn.sigmoid(g_logits)
        gate_a, gate_b = jnp.split(gates, 2, axis=-1)
        merged = gate_a * (y_a @ w_proj_a[l]) + gate_b * (y_b @ w_proj_b[l])
        y = merged @ w_out[l]

        x = x + gate * _rms(y, g_post[l])
    return x


DEPTH_2 = 2

PLE_DIM = 256
N_MIXERS = 2

GLA_HEADS = 4
GLA_KEY_DIM = D_MODEL // 2
GLA_VAL_DIM = D_MODEL
GLA_DK = GLA_KEY_DIM // GLA_HEADS
GLA_DV = GLA_VAL_DIM // GLA_HEADS
GLA_GATE_RANK = 16
GLA_GATE_NORMALIZER = 16.0
GLA_CHUNK = 64
GLA_IN = 2 * GLA_KEY_DIM + 2 * GLA_VAL_DIM + GLA_GATE_RANK

FOX_HEADS = 16
FOX_WIDTH = D_MODEL
FOX_HD = FOX_WIDTH // FOX_HEADS
FOX_BLOCK = 128
FOX_IN = 4 * FOX_WIDTH + FOX_HEADS

N_GLA = (DEPTH_2 + 1) // 2
N_FOX = DEPTH_2 // 2


def rms_norm(x, g):
    xf = x.astype(jnp.float32)
    y = xf * lax.rsqrt(jnp.mean(xf * xf, axis=-1, keepdims=True) + EPS)
    return (y * g.astype(jnp.float32)).astype(x.dtype)

def to_heads(t, n_heads):
    b, s, w = t.shape
    return t.reshape(b, s, n_heads, w // n_heads).transpose(0, 2, 1, 3)

def gla_chunked(q, k, v, log_a):
    b_, h_, s_, dk = q.shape
    dv = v.shape[-1]
    n = s_ // GLA_CHUNK
    q = q.reshape(b_, h_, n, GLA_CHUNK, dk)
    k = k.reshape(b_, h_, n, GLA_CHUNK, dk)
    v = v.reshape(b_, h_, n, GLA_CHUNK, dv)
    cum = jnp.cumsum(log_a.reshape(b_, h_, n, GLA_CHUNK, dk), axis=3)
    q_in = q * jnp.exp(cum)
    k_in = k * jnp.exp(-cum)
    causal = jnp.tril(jnp.ones((GLA_CHUNK, GLA_CHUNK), dtype=bool))
    attn = jnp.where(causal, jnp.einsum('bhncd,bhnjd->bhncj', q_in, k_in), 0.0)
    o_intra = jnp.einsum('bhncj,bhnjv->bhncv', attn, v)
    cum_last = cum[:, :, :, -1:, :]
    k_dec = k * jnp.exp(cum_last - cum)
    decay_chunk = jnp.exp(cum_last[:, :, :, 0, :])

    def step(state, inp):
        k_n, v_n, d_n = inp
        new_state = state * d_n[..., None] + jnp.einsum('bhcd,bhcv->bhdv', k_n, v_n)
        return new_state, state

    xs = (jnp.moveaxis(k_dec, 2, 0), jnp.moveaxis(v, 2, 0), jnp.moveaxis(decay_chunk, 2, 0))
    init = jnp.zeros((b_, h_, dk, dv), jnp.float32)
    _, states = lax.scan(step, init, xs)
    o_inter = jnp.einsum('bhncd,nbhdv->bhncv', q_in, states)
    return (o_intra + o_inter).reshape(b_, h_, s_, dv)

def gla_mixer(h, w_in, w_a2, b_a, o_gain, w_out):
    b_, s_, _ = h.shape
    proj = h @ w_in
    q, k, v, g, a_lr = jnp.split(
        proj, [GLA_KEY_DIM, 2 * GLA_KEY_DIM, 2 * GLA_KEY_DIM + GLA_VAL_DIM, 2 * GLA_KEY_DIM + 2 * GLA_VAL_DIM], axis=-1)
    log_a = jax.nn.log_sigmoid((a_lr @ w_a2).astype(jnp.float32) + b_a.astype(jnp.float32)) / GLA_GATE_NORMALIZER
    qh = to_heads(q, GLA_HEADS).astype(jnp.float32) * (GLA_DK ** -0.5)
    kh = to_heads(k, GLA_HEADS).astype(jnp.float32)
    vh = to_heads(v, GLA_HEADS).astype(jnp.float32)
    ah = to_heads(log_a, GLA_HEADS)
    o = gla_chunked(qh, kh, vh, ah).astype(h.dtype)
    o = rms_norm(o.transpose(0, 2, 1, 3), o_gain).reshape(b_, s_, GLA_VAL_DIM)
    return (o * jax.nn.silu(g)) @ w_out

def fox_attention(q, k, v, log_f):
    b_, h_, s_, d = q.shape
    nq = s_ // FOX_BLOCK
    c = jnp.cumsum(log_f, axis=-1)
    q_blocks = jnp.moveaxis(q.reshape(b_, h_, nq, FOX_BLOCK, d), 2, 0)
    c_blocks = jnp.moveaxis(c.reshape(b_, h_, nq, FOX_BLOCK), 2, 0)
    starts = jnp.arange(nq, dtype=jnp.int32) * FOX_BLOCK
    key_pos = jnp.arange(s_, dtype=jnp.int32)
    scale = FOX_HD ** -0.5

    def block(args):
        qb, cb, start = args
        q_pos = start + jnp.arange(FOX_BLOCK, dtype=jnp.int32)
        logits = (jnp.einsum('bhqd,bhkd->bhqk', qb, k).astype(jnp.float32) * scale
                  + cb[..., :, None] - c[..., None, :])
        mask = key_pos[None, :] <= q_pos[:, None]
        probs = jax.nn.softmax(jnp.where(mask, logits, -jnp.inf), axis=-1)
        return jnp.einsum('bhqk,bhkd->bhqd', probs.astype(v.dtype), v)

    out = lax.map(block, (q_blocks, c_blocks, starts))
    return jnp.moveaxis(out, 0, 2).reshape(b_, h_, s_, d)

def fox_mixer(h, w_in, b_f, q_gain, k_gain, w_out):
    b_, s_, _ = h.shape
    proj = h @ w_in
    q, k, v, g, f_logit = jnp.split(proj, [FOX_WIDTH, 2 * FOX_WIDTH, 3 * FOX_WIDTH, 4 * FOX_WIDTH], axis=-1)
    log_f = jax.nn.log_sigmoid(f_logit.astype(jnp.float32) + b_f.astype(jnp.float32))
    qh = rms_norm(to_heads(q, FOX_HEADS), q_gain)
    kh = rms_norm(to_heads(k, FOX_HEADS), k_gain)
    vh = to_heads(v, FOX_HEADS)
    o = fox_attention(qh, kh, vh, log_f.transpose(0, 2, 1))
    o = o.transpose(0, 2, 1, 3).reshape(b_, s_, FOX_WIDTH)
    return (o * jax.nn.silu(g)) @ w_out

def second_inputs(seed: int = 0) -> dict:
    key = jax.random.key(seed)
    ks = jax.random.split(key, 20)
    f32 = jnp.float32
    nrm = lambda k, shape, fan_in: jax.random.normal(k, shape, f32) * (fan_in ** -0.5)
    gain = lambda k, shape: 1.0 + 0.02 * jax.random.normal(k, shape, f32)
    return {
        "x": jax.random.normal(ks[0], (BATCH, SEQ, D_MODEL), f32),
        "p": jax.random.normal(ks[1], (DEPTH_2, BATCH, SEQ, PLE_DIM), f32),
        "norm_mixer": gain(ks[2], (DEPTH_2, D_MODEL)),
        "gla_w_in": nrm(ks[3], (N_GLA, D_MODEL, GLA_IN), D_MODEL),
        "gla_w_a2": nrm(ks[4], (N_GLA, GLA_GATE_RANK, GLA_KEY_DIM), GLA_GATE_RANK),
        "gla_b_a": 0.1 * jax.random.normal(ks[5], (N_GLA, GLA_KEY_DIM), f32),
        "gla_o_norm": gain(ks[6], (N_GLA, GLA_DV)),
        "gla_w_out": nrm(ks[7], (N_GLA, GLA_VAL_DIM, D_MODEL), GLA_VAL_DIM),
        "fox_w_in": nrm(ks[8], (N_FOX, D_MODEL, FOX_IN), D_MODEL),
        "fox_b_f": 2.0 + 0.5 * jax.random.normal(ks[9], (N_FOX, FOX_HEADS), f32),
        "fox_q_norm": gain(ks[10], (N_FOX, FOX_HD)),
        "fox_k_norm": gain(ks[11], (N_FOX, FOX_HD)),
        "fox_w_out": nrm(ks[12], (N_FOX, FOX_WIDTH, D_MODEL), FOX_WIDTH),
        "ple_proj": nrm(ks[13], (DEPTH_2, PLE_DIM, D_MODEL), PLE_DIM),
        "ple_gate": nrm(ks[14], (DEPTH_2, D_MODEL, D_MODEL), D_MODEL),
        "ple_norm": gain(ks[15], (DEPTH_2, D_MODEL)),
        "final_norm": gain(ks[16], (D_MODEL,)),
    }

def second_block(x, p, norm_mixer, gla_w_in, gla_w_a2, gla_b_a, gla_o_norm, gla_w_out,
              fox_w_in, fox_b_f, fox_q_norm, fox_k_norm, fox_w_out,
              ple_proj, ple_gate, ple_norm, final_norm):
    h = x
    for i in range(DEPTH_2):
        hn = rms_norm(h, norm_mixer[i])
        j = i // N_MIXERS
        if i % N_MIXERS == 0:
            h = h + gla_mixer(hn, gla_w_in[j], gla_w_a2[j], gla_b_a[j], gla_o_norm[j], gla_w_out[j])
        else:
            h = h + fox_mixer(hn, fox_w_in[j], fox_b_f[j], fox_q_norm[j], fox_k_norm[j], fox_w_out[j])
        h = h + (p[i] @ ple_proj[i]) * jax.nn.sigmoid(rms_norm(h, ple_norm[i]) @ ple_gate[i])
    return rms_norm(h, final_norm)


def setup_inputs(seed=0):
    out = dict(first_inputs(seed))
    for name, value in second_inputs(seed + 1).items():
        if name != "x":
            out[name + "_2"] = value
    return out


def reference(
    x, c, positions, w_ada, b_ada, g_pre, g_post, w_in, sinks, ln_v_g, ln_v_b, w_s, b_s,
    w_proj_a, w_proj_b, w_out, p_2, norm_mixer_2, gla_w_in_2, gla_w_a2_2, gla_b_a_2,
    gla_o_norm_2, gla_w_out_2, fox_w_in_2, fox_b_f_2, fox_q_norm_2, fox_k_norm_2, fox_w_out_2,
    ple_proj_2, ple_gate_2, ple_norm_2, final_norm_2,
):
    x = first_block(
        x, c, positions, w_ada, b_ada, g_pre, g_post, w_in, sinks, ln_v_g, ln_v_b, w_s, b_s,
        w_proj_a, w_proj_b, w_out,
    )
    return second_block(
        x, p_2, norm_mixer_2, gla_w_in_2, gla_w_a2_2, gla_b_a_2, gla_o_norm_2, gla_w_out_2,
        fox_w_in_2, fox_b_f_2, fox_q_norm_2, fox_k_norm_2, fox_w_out_2, ple_proj_2, ple_gate_2,
        ple_norm_2, final_norm_2,
    )


_drawn_inputs = setup_inputs


def setup_inputs(seed=0):
    import zlib

    import numpy as np

    out = dict(_drawn_inputs(seed))
    spreads = {}
    factors = {'g_post': 2.891,
     'sinks': 8.0,
     'ln_v_g': 7.106,
     'ln_v_b': 8.0,
     'norm_mixer_2': 2.978,
     'gla_b_a_2': 2.836,
     'gla_o_norm_2': 6.101,
     'fox_q_norm_2': 8.0,
     'fox_k_norm_2': 8.0,
     'ple_norm_2': 8.0,
     'final_norm_2': 2.728}
    for name, (base, spread) in spreads.items():
        noise = np.random.default_rng([zlib.crc32(name.encode()), seed]).standard_normal(out[name].shape)
        drawn = base * np.exp(spread * noise) if base else spread * noise
        out[name] = __import__('jax').numpy.asarray(drawn.astype(out[name].dtype))
    for name, factor in factors.items():
        out[name] = (out[name] * factor).astype(out[name].dtype)
    return out
```

```python
from contextlib import ExitStack

import numpy as np

import concourse.bass as bass
from concourse import mybir

F32 = mybir.dt.float32
F32R = mybir.dt.float32r
I32 = mybir.dt.int32
ALU = mybir.AluOpType
ACT = mybir.ActivationFunctionType
AX = mybir.AxisListType

P = 128
D = 1024
S = 1024
KC = D // P
NB = S // P
HALF = 512
EPS = 1e-6
NEG = -1e30
SWA_HEADS, SWA_KV, HD = 8, 2, 64
GROUPS = 4
GLA_HEADS, GLA_CHUNK, GLA_RANK = 4, 64, 16
GLA_NORMALIZER = 16.0
FOX_HEADS = 16

T_Q, T_K, T_V, T_G, T_VB, T_ZA, T_U, T_ZB = 0, 4, 5, 6, 22, 26, 30, 34
T_PJ, T_WO, T_LR, T_GLA, T_GO, T_PLE0 = 38, 46, 54, 55, 79, 87
T_F, T_FOX, T_FO, T_PLE1, N_TILES = 95, 96, 128, 136, 144
RAW_SLOTS, W_SLOTS = 2, 4

U_Q, U_K, U_V, U_G, U_VB, U_ZA, U_U, U_ZB = 0, 4, 5, 6, 22, 26, 30, 34
U_PJ, U_WO, U_LR, U_GLA, U_GO, U_PLE0 = 38, 54, 62, 63, 95, 103
U_F, U_FOX, U_FO, U_PLE1, N_UNITS = 119, 120, 152, 160, 176
GLA_UNITS = 8

_COLS = [("g_pre", 8), ("g_post", 8), ("b_ada", 24), ("c", 8), ("norm0", 8), ("norm1", 8), ("ple0", 8),
         ("ple1", 8), ("final", 8), ("o_gain", 2), ("q_gain", 1), ("k_gain", 1), ("b_f", 1),
         ("inv_freq", 1), ("rope_sign", 1), ("eps", 1), ("eps64", 1), ("selector", 16), ("half_pi", 1)]
COL = {}
_at = 0
for _name, _n in _COLS:
    COL[_name] = (_at, _n)
    _at += _n
N_COLS = _at
ROW = {"sinks": (0, 8), "ln_g": (8, 512), "ln_b": (520, 512), "b_s": (1032, 512), "b_a": (1544, 512)}
N_ROWS = 2056
MAT = {n: i for i, n in enumerate(["ident", "ones", "head_ones", "chunk_sum", "chunk_mask", "causal_sum",
                                   "hide_all", "hide_prev", "hide_cur", "causal_w"])}
N_MATS = len(MAT)


def build(nc, xT, pT, pos, cols, rows, mats, w_ada, w_tiles, ws_t, w_a2, ple_w, outT):
    ctx = ExitStack()
    base = (nc.sbuf_base + 31) // 32 * 32
    KB = 1024

    def sb(name, shape, at, dt=F32):
        return nc.alloc_sbuf_tensor_at(name, shape, dt, offset=base + int(at * KB))

    def sem(name):
        return ctx.enter_context(nc.semaphore(name))

    AH = sb("AH", [P, KC, S], 0, F32R)
    AL = sb("AL", [P, KC, S], 32, F32R)
    Y = sb("Y", [P, KC, S], 64)
    RAW = sb("RAW", [P, RAW_SLOTS, D], 96)
    WH = sb("WH", [P, W_SLOTS, D], 104, F32R)
    WL = sb("WL", [P, W_SLOTS, D], 120, F32R)
    CC = 136
    MATS = sb("MATS", [P, N_MATS, P], CC)
    CC += N_MATS * 0.5
    IDR = sb("IDR", [P, P], CC, F32R)
    HIDE = sb("HIDE", [P, 3, P], CC + 0.5, F32R)
    CC += 2
    COLS = sb("COLS", [P, N_COLS], CC)
    SINK = sb("SINK", [P, SWA_HEADS], CC + 0.46875)
    ADA = sb("ADA", [P, 24], CC + 0.5)
    GS = sb("GS", [P, KC], CC + 0.59375)
    GG = sb("GG", [P, KC], CC + 0.625)
    CACT = sb("CACT", [P, KC], CC + 0.65625)
    assert CC + 0.6875 <= 144 and N_COLS * 4 <= 480
    X = sb("X", [P, KC, S], 144)
    SQ = sb("SQ", [P, 2, S], 176)
    TN = sb("TN", [P, 2, S], 184)
    RS = sb("RS", [P, S], 192)
    RC = sb("RC", [P, NB], 206.5)
    AROW = sb("AROW", [P, 2, S], 176)
    COS = sb("COS", [P, S], 196)
    SIN = sb("SIN", [P, S], 200)
    POSI = sb("POSI", [P, S], 64, I32)
    ANG = sb("ANG", [P, S], 68)
    TURN = sb("TURN", [P, S], 72)
    RED = sb("RED", [P, S], 76)
    ABSR = sb("ABSR", [P, S], 80)
    WADA = [sb("WADA_SCALE", [P, KC, D], 0), sb("WADA_SHIFT", [P, KC, D], 32), sb("WADA_GATE", [P, KC, D], 64)]
    Q = sb("Q", [P, 4, S], 144)
    K = sb("K", [P, P + S], 160)
    KSH = sb("KSH", [P, 2, 2 * P], 164.5, F32R)
    KSL = sb("KSL", [P, 2, 2 * P], 166.5, F32R)
    V = sb("V", [P, 1 + NB, P], 169)
    M1 = sb("M1", [P, S], 176)
    M2 = sb("M2", [P, S], 180)
    QSH = sb("QSH", [P, 2, 4, P], 176, F32R)
    QSL = sb("QSL", [P, 2, 4, P], 180, F32R)
    VSH = sb("VSH", [P, 2, 2, P], 184, F32R)
    VSL = sb("VSL", [P, 2, 2, P], 186, F32R)
    PR = sb("PR", [P, 2, 4, 2 * P], 188)
    PTH = sb("PTH", [P, 2, 4 * P], 196, F32R)
    PTL = sb("PTL", [P, 2, 4 * P], 200, F32R)
    SIG = sb("SIG", [P, 2, S], 80)
    NMAX = sb("NMAX", [P, 2, 4], 204)
    NM = sb("NM", [P, 2, 4], 204.0625)
    DEN = sb("DEN", [P, 2, 4], 204.125)
    ESUM = sb("ESUM", [P, 2, 4], 204.1875)
    SDIF = sb("SDIF", [P, 2, 4], 204.25)
    DENS = sb("DENS", [P, 2, 4], 204.3125)
    RDEN = sb("RDEN", [P, 2, 4], 204.375)
    NSINK = sb("NSINK", [P, 8], 204.4375)
    GV = sb("GV", [P, NB, HALF], 144)
    LNT = sb("LNT", [P, 2, HALF], 160)
    VNH = sb("VNH", [P, 2, HALF], 164, F32R)
    VNL = sb("VNL", [P, 2, HALF], 168, F32R)
    WSF = sb("WSF", [P, GROUPS, P], 172)
    WSH = sb("WSH", [P, GROUPS, P], 176, F32R)
    WSL = sb("WSL", [P, GROUPS, P], 178, F32R)
    LNG = sb("LNG", [P, HALF], 180)
    LNB = sb("LNB", [P, HALF], 182)
    BSB = sb("BSB", [P, GROUPS, P], 184)
    BN6 = sb("BN6", [P, NB, 6], 204.5)
    MV = sb("MV", [P, NB, 2], 204.75)
    RSTD = sb("RSTD", [P, NB], 204.8125)
    GU = sb("GU", [P, 2, S], 188)
    GA = sb("GA", [P, 2, S], 144)
    GB = sb("GB", [P, 2, S], 152)
    MB = sb("MB", [P, 2, S], 160)

    gates = nc.dram_tensor("gates", [16, P, S], F32).ap()
    park = nc.dram_tensor("park", [P, KC, S], F32).ap()

    psG = ctx.enter_context(nc.psum_tensor("psG", [P, 4, HALF], F32))
    psA = ctx.enter_context(nc.psum_tensor("psA", [P, 4, HALF], F32))

    def unit(b):
        return psG[:, 2 * b:2 * b + 2, :].rearrange("p a f -> p (a f)")

    def pair(b):
        return psA[:, 2 * b:2 * b + 2, :].rearrange("p a f -> p (a f)")

    def mat(name):
        return MATS[:, MAT[name], :]

    def col(name, j=0):
        return COLS[:, COL[name][0] + j:COL[name][0] + j + 1]

    consts_loaded = sem("consts_loaded")
    x_part = [sem(f"x_part{i}") for i in range(4)]
    x_loaded = sem("x_loaded")
    pos_loaded = sem("pos_loaded")
    ada_loaded = [sem(f"ada_loaded{i}") for i in range(3)]
    raw_loaded = [sem(f"raw_loaded{i}") for i in range(RAW_SLOTS)]
    w_high = sem("w_high")
    w_split = sem("w_split")
    tile_begun = sem("tile_begun")
    psum_full = sem("psum_full")
    psum_free = sem("psum_free")
    a_high = sem("a_high")
    a_ready = sem("a_ready")
    sq_ready = sem("sq_ready")
    sq_used = sem("sq_used")
    rms_ready = sem("rms_ready")
    rc_full = sem("rc_full")
    rc_ready = sem("rc_ready")
    rs_full = sem("rs_full")
    tn_ready = sem("tn_ready")
    dve_step = sem("dve_step")
    act_step = sem("act_step")
    r_ready = sem("r_ready")

    class Chain:

        def __init__(self, eng, s):
            self.eng, self.sem, self.base, self.it, self.per, self.loc = eng, s, 0, 0, 0, 0

        def link(self, ins):
            ins.then_inc(self.sem, 1)
            self.loc += 1
            self.eng.wait_ge(self.sem, self.it * self.per + (self.base + self.loc))

        def loop(self, it, per):
            self.base, self.loc, self.it, self.per = self.base + self.loc, 0, it, per

        def done(self, n):
            assert self.loc == self.per, (self.loc, self.per)
            self.base, self.loc, self.it, self.per = self.base + n * self.per, 0, 0, 0

    block = ctx.enter_context(nc.Block())

    cact_ready = sem("cact_ready")
    ada_row = sem("ada_row")
    ada_copied = sem("ada_copied")
    ada_done = sem("ada_done")
    ada_ready = sem("ada_ready")
    rope_ready = sem("rope_ready")
    rope_angle = sem("rope_angle")
    v_turned = sem("v_turned")
    kv_ready = sem("kv_ready")
    qs_high = sem("qs_high")
    qs_ready = sem("qs_ready")
    s_full = sem("s_full")
    nm_ready = sem("nm_ready")
    exp_done = sem("exp_done")
    prob_ready = sem("prob_ready")
    t_full = sem("t_full")
    pt_high = sem("pt_high")
    pt_ready = sem("pt_ready")
    o_full = sem("o_full")
    o_read = sem("o_read")
    gate_stored = [sem(f"gate_stored{i}") for i in range(2)]
    sgu_loaded = sem("sgu_loaded")
    ws_masked = sem("ws_masked")
    ws_ready = sem("ws_ready")
    ws_high = sem("ws_high")
    ln_stats = sem("ln_stats")
    ln_root = sem("ln_root")
    vn_f32 = sem("vn_f32")
    vn_high = sem("vn_high")
    vn_ready = sem("vn_ready")
    sv_full = sem("sv_full")
    sv_read = sem("sv_read")
    act_out = sem("act_out")
    y_gated = sem("y_gated")
    gab_loaded = [sem(f"gab_loaded{i}") for i in range(2)]
    m_ready = sem("m_ready")
    x_upd = sem("x_upd")

    tile_waited = sem("tile_waited")

    def sp_inputs(sp):
        sp.dma_start(COLS[:, :], cols).then_inc(consts_loaded, 16)
        sp.dma_start(MATS[:, :, :], mats).then_inc(consts_loaded, 16)
        sp.dma_start(SINK[:, :], rows[:, 0:8].to_broadcast([P, 8])).then_inc(consts_loaded, 16)
        sp.dma_start(POSI[:, :], pos.to_broadcast([P, S])).then_inc(pos_loaded, 16)
        for i in range(4):
            sp.dma_start(X[:, 2 * i:2 * i + 2, :], xT[2 * i:2 * i + 2].rearrange("c p s -> p c s")).then_inc(x_part[i], 16)
        for i in range(2):
            sp.dma_start(WADA[i][:, :, :], w_ada[i]).then_inc(ada_loaded[i], 16)

    def sp_stream(sp):
        def load(t, i, first=False):
            if not first:
                sp.wait_ge(w_split, t - 1)
            sp.dma_start(RAW[:, i, :], w_tiles[t]).then_inc(raw_loaded[i], 16)

        load(0, 0, True)
        load(1, 1, True)
        with sp.Fori(1, N_TILES // RAW_SLOTS) as it:
            load(it * 2, 0)
            load(it * 2 + 1, 1)

    def pool_stream(pool):
        def cut(t, turn, i, first=False):
            pool.wait_ge(raw_loaded[i % RAW_SLOTS], turn * 32 + 16 * (i // RAW_SLOTS + 1))
            if not first:
                pool.wait_ge(tile_begun, t - 2)
            pool.sem_inc(tile_waited, 1)
            nc.gpsimd.tensor_scalar(WH[:, i, :], RAW[:, i % RAW_SLOTS, :], 1.0, 0.0, ALU.mult, ALU.add).then_inc(w_high, 1)
            pool.wait_ge(w_high, t + 1)
            nc.gpsimd.tensor_tensor(WL[:, i, :], RAW[:, i % RAW_SLOTS, :], WH[:, i, :].bitcast(F32), ALU.subtract).then_inc(w_split, 1)

        for i in range(W_SLOTS):
            cut(i, 0, i, True)
        with pool.Fori(1, N_TILES // W_SLOTS) as it:
            for i in range(W_SLOTS):
                cut(it * W_SLOTS + i, it, i)

    def three(out, wh, wl, xh, xl, start, stop):
        first = nc.tensor.matmul(out, wh, xh, start=start, stop=False)
        nc.tensor.matmul(out, wh, xl, start=False, stop=False)
        return first, nc.tensor.matmul(out, wl, xh, start=False, stop=stop)

    class Begin:

        def __init__(self, n):
            self.n = n

        def mark(self, ins):
            if self.n:
                ins.then_inc(tile_begun, 1)
                self.n -= 1

    def gemm(pe, t, u, slot, b, halves=(0, 1), kw=range(KC), ka=range(KC), begun=1, fill=None, free=True):
        if 0 in halves:
            pe.wait_ge(w_split, t + 1)
            if free:
                pe.wait_ge(psum_free, u - 1)
        mark = Begin(begun)

        def part(h, w, a, first, last):
            ws = slice(w * P, (w + 1) * P)
            xs = slice(h * HALF, (h + 1) * HALF)
            f, l = three(psG[:, 2 * b + h, :], WH[:, slot, ws], WL[:, slot, ws], AH[:, a, xs], AL[:, a, xs], first, last)
            mark.mark(f)
            return l

        kk = list(zip(kw, ka))
        if fill is None:
            for h in halves:
                for n, (w, a) in enumerate(kk):
                    l = part(h, w, a, n == 0, n == len(kk) - 1)
        else:
            for n, (w, a) in enumerate(kk):
                pe.wait_ge(a_ready, KC * fill + a + 1)
                for h in halves:
                    l = part(h, w, a, n == 0, n == len(kk) - 1)
        if 1 in halves:
            l.then_inc(psum_full, 1)

    def gemm_slices(pe, t, u, slot, b, fill=None, begins=0):
        mark = Begin(1)
        order = [(h, c) for h in range(2) for c in range(KC)] if fill is None else [(h, c) for c in range(KC) for h in range(2)]

        def cut(h, c):
            if (h, c) == order[0]:
                pe.wait_ge(w_split, t + 1)
                pe.wait_ge(psum_free, u - 1)
            if fill is not None and h == 0:
                pe.wait_ge(a_ready, KC * fill + c + 1)
            ws, xs = slice(c * P, (c + 1) * P), slice(h * HALF, (h + 1) * HALF)
            f, l = three(psG[:, 2 * b + h, :], WH[:, slot, ws], WL[:, slot, ws], AH[:, c, xs], AL[:, c, xs], c == 0, c == KC - 1)
            if order.index((h, c)) >= begins:
                mark.mark(f)
            if (h, c) == order[-1]:
                l.then_inc(psum_full, 1)

        for h, c in order:
            yield lambda h=h, c=c: cut(h, c)

    def pe_square(pe, k, j):
        pe.wait_ge(sq_ready, KC * k + j + 1)
        for h in range(2):
            l = nc.tensor.matmul(psA[:, 2 + h, :], mat("ones"), SQ[:, j % 2, h * HALF:(h + 1) * HALF],
                                 start=(j == 0), stop=(j == KC - 1))
        l.then_inc(sq_used, 1)

    def pe_sumsq(pe, k):
        for j in range(KC):
            pe_square(pe, k, j)

    def pe_recip(pe, k):
        pe.wait_ge(rms_ready, k + 1)
        for n in range(NB):
            l = nc.tensor.matmul(psA[:, 2, n:n + 1], RS[:, n * P:(n + 1) * P], mat("ident")[:, 0:1], start=True, stop=True)
        l.then_inc(rc_full, 1)
        pe.wait_ge(rc_ready, k + 1)
        for n in range(NB):
            l = nc.tensor.transpose(psA[:, n // 4, (n % 4) * P:(n % 4 + 1) * P], RC[:, n:n + 1].to_broadcast([P, P]), mat("ident"))
        l.then_inc(rs_full, 1)

    def pe_ada(pe, i):
        if i == 0:
            pe.wait_ge(rc_ready, 1)
        else:
            pe.wait_ge(ada_ready, i)
        pe.wait_ge(ada_loaded[i], 16)
        for h in range(2):
            for c in range(KC):
                l = nc.tensor.matmul(psA[0:1, 2 + h, :], CACT[:, c:c + 1], WADA[i][:, c, h * HALF:(h + 1) * HALF],
                                     start=(c == 0), stop=(c == KC - 1))
        l.then_inc(ada_row, 1)
        pe.wait_ge(ada_copied, i + 1)
        for n in range(KC):
            l = nc.tensor.matmul(psA[:, 2, n:n + 1], AROW[0:1, i % 2, n * P:(n + 1) * P], mat("ones")[0:1, 0:1], start=True, stop=True)
        l.then_inc(ada_done, 1)

    def pe_block1_in(pe):
        pe.wait_ge(consts_loaded, 48)
        pe_sumsq(pe, 0)
        pe_recip(pe, 0)
        pe.wait_ge(cact_ready, 1)
        for i in range(3):
            pe_ada(pe, i)
        for j in range(4):
            gemm(pe, T_Q + j, U_Q + j, j, j % 2, begun=1, fill=0 if j == 0 else None, free=j >= 2)
        gemm(pe, T_K, U_K, T_K % 4, U_K % 2)
        gemm(pe, T_V, U_V, T_V % 4, U_V % 2)
        pe.wait_ge(psum_free, U_V + 1)
        for n in range(NB):
            l = nc.tensor.transpose(psA[:, n // 4, (n % 4) * P:(n % 4 + 1) * P], M2[:, n * P:(n + 1) * P], mat("ident"))
        l.then_inc(v_turned, 1)

    def pe_swa(pe):
        def body(it, first):
            for i in range(4):
                u, n, r = it * 4 + i, it * 2 + i // 2, i % 2
                slot, b = (T_G + i) % 4, i % 2
                rows_ = slice(64 * r, 64 * r + 64)
                if r == 0:
                    pe.wait_ge(qs_ready, n + 1)
                if first and i == 0:
                    pe.wait_ge(kv_ready, 2)
                    pe.wait_ge(r_ready, 2)
                else:
                    pe.wait_ge(prob_ready, u)
                for bank in range(2):
                    hide = HIDE[:, 0:3:2, :] if first and i < 2 else HIDE[:, 1:3, :]
                    nc.tensor.matmul(psA[:, bank, :], IDR[:, :], hide.unsqueeze(1).to_broadcast([P, 2, 2, P]), start=True, stop=False)
                    for j in (2 * bank, 2 * bank + 1):
                        _, l = three(psA[:, bank, (j % 2) * 256:(j % 2 + 1) * 256], QSH[rows_, i // 2, j, :], QSL[rows_, i // 2, j, :],
                                     KSH[rows_, i // 2, :], KSL[rows_, i // 2, :], False, j % 2 == 1)
                l.then_inc(s_full, 1)
                gemm(pe, T_G + u, U_G + u, slot, b, halves=(0,))
                pe.wait_ge(prob_ready, u + 1)
                if not (first and i == 0):
                    pe.wait_ge(o_read, u)
                else:
                    pe.wait_ge(ada_ready, 3)
                for hf in range(2):
                    for j in range(4):
                        l = nc.tensor.transpose(psA[:, 2 + hf, j * P:(j + 1) * P], PR[:, i % 2, j, hf * P:(hf + 1) * P], mat("ident"))
                l.then_inc(t_full, 1)
                gemm(pe, T_G + u, U_G + u, slot, b, halves=(1,), begun=0)
                pe.wait_ge(pt_ready, u + 1)
                for hf in range(2):
                    _, l = three(psA[:, 2, :], VSH[:, i // 2, hf, :], VSL[:, i // 2, hf, :], PTH[:, hf, :], PTL[:, hf, :], hf == 0, hf == 1)
                l.then_inc(o_full, 1)

        body(0, True)
        with pe.Fori(1, 4) as it:
            body(it, False)

    def pe_tokens(pe, t, u, tiles, begun, n_units, b0=None):
        width = len(tiles) * P
        lo, hi = min(tiles), max(tiles) + 1
        side = slice(lo, hi, (hi - lo - 1) // (len(tiles) - 1))
        b0 = u % 2 if b0 is None else b0
        per = HALF // width
        mark = Begin(begun)
        pe.wait_ge(w_split, t + len(tiles))
        for v in range(n_units):
            b = (b0 + v) % 2
            pe.wait_ge(psum_free, u + (v - 1))
            for h in range(2):
                for s in range(per):
                    n = (2 * v + h) * per + s
                    for c in range(KC):
                        blk, ws = slice(n * P, (n + 1) * P), slice(c * P, (c + 1) * P)
                        wh, wl = WH[:, side, ws], WL[:, side, ws]
                        f, l = three(psG[:, 2 * b + h, s * width:(s + 1) * width], AH[:, c, blk], AL[:, c, blk], wh, wl, c == 0, c == KC - 1)
                        mark.mark(f)
            l.then_inc(psum_full, 1)

    def pe_sgu(pe):
        pe.wait_ge(prob_ready, 16)
        nc.tensor.matmul(psA[:, 0, 0:1], mat("ident"), COLS[:, 0:1], start=True, stop=True).then_inc(tile_begun, 1)
        pe_tokens(pe, T_VB, U_VB, [2, 3, 0, 1], 0, 4)
        nc.tensor.matmul(psA[:, 0, 0:1], mat("ident"), COLS[:, 0:1], start=True, stop=True).then_inc(tile_begun, 3)
        for j in range(4):
            gemm(pe, T_ZA + j, U_ZA + j, (T_ZA + j) % 4, j % 2, begun=1)
            if j == 0:
                pe.wait_ge(ws_ready, 1)
            for n in (2 * j, 2 * j + 1):
                pe.wait_ge(vn_ready, n + 1)
                if n >= 2:
                    pe.wait_ge(sv_read, n - 1)
                for g in range(GROUPS):
                    gs = slice(g * P, (g + 1) * P)
                    _, l = three(psA[:, n % 2, gs], VNH[:, n % 2, gs], VNL[:, n % 2, gs], WSH[:, g, :], WSL[:, g, :], True, True)
                l.then_inc(sv_full, 1)

    def pe_tiles(pe, t0, u0, n, it0=0):
        with pe.Fori(0, n // 4) as it:
            for i in range(4):
                gemm(pe, it * 4 + (t0 + i), it * 4 + (u0 + i), (t0 + i) % 4, (u0 + i) % 2)

    def pe_merge(pe):
        def tile(j, i, fill=None):
            gemm(pe, j + T_PJ, j * 2 + U_PJ, (T_PJ + i) % 4, 0, kw=range(4), ka=range(4), fill=fill)
            gemm(pe, j + T_PJ, j * 2 + (U_PJ + 1), (T_PJ + i) % 4, 1, kw=range(4, 8), ka=range(4, 8), begun=0, fill=fill)
        with pe.Fori(0, 2) as it:
            for i in range(4):
                tile(it * 4 + i, i, 1 if i == 0 else None)

    def pe_out(pe, t0, u0, fill, k=None, begun=0):
        for j in range(KC):
            if j >= begun:
                gemm(pe, t0 + j, u0 + j, (t0 + j) % 4, (u0 + j) % 2, fill=fill if j == 0 else None)
            if k is not None and j:
                pe_square(pe, k, j - 1)
        if k is not None:
            pe_square(pe, k, KC - 1)

    def act_fill(act, f, src, ready, j, shift=None):
        act.wait_ge(ready[0], ready[1])
        if shift is None:
            nc.scalar.activation(AH[:, j, :], src, ACT.Copy).then_inc(a_high, 1)
        else:
            nc.scalar.activation(AH[:, j, :], src, ACT.Identity, bias=shift).then_inc(a_high, 1)

    def act_squares(act, k, j, src, ready):
        act.wait_ge(ready[0], ready[1])
        if KC * k + j >= 2:
            act.wait_ge(sq_used, KC * k + j - 1)
        nc.scalar.activation(SQ[:, j % 2, :], src, ACT.Square).then_inc(sq_ready, 1)

    def act_root(act, k):
        act.wait_ge(sq_used, KC * (k + 1))
        nc.scalar.activation(RS[:, :], pair(1), ACT.Sqrt, bias=col("eps"), scale=1.0 / D).then_inc(rms_ready, 1)

    def act_norm_fill(act, k, n_fill, f, shift=None):
        for j in range(KC):
            act_fill(act, f, TN[:, j % 2, :], (tn_ready, KC * n_fill + j + 1), j, None if shift is None else shift(j))

    def act_ada(act, i):
        act.wait_ge(ada_row, i + 1)
        nc.scalar.activation(AROW[0:1, i % 2, :], pair(1)[0:1, :], ACT.Copy).then_inc(ada_copied, 1)

    def act_block1_in(act):
        act.wait_ge(consts_loaded, 48)
        nc.scalar.activation(CACT[:, :], COLS[:, COL["c"][0]:COL["c"][0] + KC], ACT.Silu).then_inc(cact_ready, 1)
        nc.scalar.activation(IDR[:, :], mat("ident"), ACT.Copy).then_inc(r_ready, 1)
        nc.scalar.activation(HIDE[:, :, :], MATS[:, MAT["hide_all"]:MAT["hide_all"] + 3, :], ACT.Copy).then_inc(r_ready, 1)
        for j in range(KC):
            act_squares(act, 0, j, X[:, j, :], (x_part[j // 2], 16))
        act_root(act, 0)
        act.wait_ge(rope_angle, 1)
        nc.scalar.activation(ABSR[:, :], RED[:, :], ACT.Abs).then_inc(act_step, 1)
        act.wait_ge(act_step, 1)
        nc.scalar.activation(COS[:, :], ABSR[:, :], ACT.Sin, bias=col("half_pi"), scale=-1.0).then_inc(rope_ready, 1)
        nc.scalar.activation(SIN[:, :], RED[:, :], ACT.Sin, scale=col("rope_sign")).then_inc(rope_ready, 1)
        act.wait_ge(rope_ready, 2)
        act.dma_start(WADA[2][:, :, :], w_ada[2]).then_inc(ada_loaded[2], 16)
        for i in range(2):
            act_ada(act, i)
        act.wait_ge(ada_ready, 2)
        act_norm_fill(act, 0, 0, 0, lambda j: ADA[:, j:j + 1])
        act_ada(act, 2)
        act.wait_ge(psum_full, U_V + 1)
        act.wait_ge(kv_ready, 1)
        nc.scalar.activation(M2[:, :], unit(U_V % 2), ACT.Copy).then_inc(psum_free, 1)
        act.wait_ge(v_turned, 1)
        nc.scalar.activation(V[:, 1:, :], pair(0).rearrange("p (n f) -> p n f", n=NB), ACT.Copy).then_inc(kv_ready, 1)

    def act_swa(act):
        def body(it, first):
            for i in range(4):
                u, n, r = it * 4 + i, it * 2 + i // 2, i % 2
                rows_ = slice(64 * r, 64 * r + 64)
                if r == 0:
                    if not first:
                        act.wait_ge(o_full, n * 2 - 2)
                    act.wait_ge(kv_ready, 2)
                    nc.scalar.activation(QSH[:, i // 2, :, :], Q[:, :, bass.ds(n * P, P)], ACT.Copy)
                    nc.scalar.activation(VSH[:, i // 2, :, :], V[:, bass.ds(n, 2), :], ACT.Copy)
                    nc.scalar.activation(KSH[:, i // 2, :], K[:, bass.ds(n * P, 2 * P)], ACT.Copy).then_inc(qs_high, 1)
                if first:
                    if i >= 2:
                        act.wait_ge(t_full, i - 1)
                else:
                    act.wait_ge(t_full, u - 1)
                act.wait_ge(nm_ready, u + 1)
                for j in range(4):
                    nc.scalar.activation(PR[:, i % 2, j, :], psA[:, j // 2, (j % 2) * 256:(j % 2 + 1) * 256], ACT.Exp,
                                         bias=NM[:, i % 2, j:j + 1], accum_out=DEN[:, i % 2, j:j + 1])
                nc.scalar.activation(ESUM[:, i % 2, :], SDIF[:, i % 2, :], ACT.Exp).then_inc(exp_done, 1)
                act.wait_ge(t_full, u + 1)
                if not (first and i == 0):
                    act.wait_ge(o_full, u)
                nc.scalar.activation(PTH[:, :, :].rearrange("p a f -> p (a f)"), pair(1), ACT.Copy).then_inc(pt_high, 1)
                if not (first and i < 2):
                    act.wait_ge(gate_stored[i % 2], (it * 2 + i // 2) * 16)
                if first and i == 0:
                    act.wait_ge(ada_ready, 3)
                act.wait_ge(psum_full, u + (U_G + 1))
                nc.scalar.activation(SIG[:, i % 2, :], unit(i % 2), ACT.Sigmoid).then_inc(psum_free, 1)
                act.wait_ge(psum_free, u + (U_G + 1))
                act.dma_start(gates[u], SIG[:, i % 2, :]).then_inc(gate_stored[i % 2], 16)
                act.wait_ge(o_full, u + 1)
                act.wait_ge(kv_ready, 2)
                nc.scalar.activation(Y[rows_, 0:4, bass.ds(n * P, P)], psA[rows_, 2, :].rearrange("p (j f) -> p j f", j=4),
                                     ACT.Copy).then_inc(o_read, 1)

        body(0, True)
        with act.Fori(1, 4) as it:
            body(it, False)

    def act_sgu(act):
        act.wait_ge(o_full, 16)
        act.wait_ge(prob_ready, 16)
        act.dma_start(WSF[:, :, :], ws_t).then_inc(sgu_loaded, 16)
        for name, dst in (("ln_g", LNG[:, :]), ("ln_b", LNB[:, :]), ("b_s", BSB[:, :, :].rearrange("p g f -> p (g f)"))):
            at, n = ROW[name]
            act.dma_start(dst, rows[:, at:at + n].to_broadcast([P, n])).then_inc(sgu_loaded, 16)
        for v in range(4):
            act.wait_ge(psum_full, U_VB + v + 1)
            nc.scalar.activation(GV[:, 2 * v:2 * v + 2, :].rearrange("p a f -> p (a f)"), unit((U_VB + v) % 2), ACT.Gelu).then_inc(psum_free, 1)
        act.wait_ge(ln_stats, 1)
        nc.scalar.activation(RSTD[:, :], MV[:, :, 1], ACT.Sqrt, bias=col("eps")).then_inc(ln_root, 1)
        act.wait_ge(ws_masked, 1)
        nc.scalar.activation(WSH[:, :, :], WSF[:, :, :], ACT.Copy).then_inc(ws_high, 1)
        for j in range(4):
            for n in (2 * j, 2 * j + 1):
                act.wait_ge(vn_f32, n + 1)
                if n >= 2:
                    act.wait_ge(sv_full, n - 1)
                nc.scalar.activation(VNH[:, n % 2, :], LNT[:, n % 2, :], ACT.Copy).then_inc(vn_high, 1)
            act_gate(act, j, ACT.Silu, U_ZA + j)

    def act_gate(act, g, func, u):
        if g >= 2:
            act.wait_ge(y_gated, g - 1)
        act.wait_ge(psum_full, u + 1)
        nc.scalar.activation(GU[:, g % 2, :], unit(u % 2), func).then_inc(psum_free, 1)

    def act_gating(act):
        for j in range(4):
            act_gate(act, 4 + j, ACT.Gelu, U_U + j)
        for j in range(4):
            act_gate(act, 8 + j, ACT.Silu, U_ZB + j)

    def act_merge(act):
        def load(j, b):
            act.dma_start(GA[:, b, :], gates[j]).then_inc(gab_loaded[b], 16)
            act.dma_start(GB[:, b, :], gates[j + KC]).then_inc(gab_loaded[b], 16)
        for b in range(2):
            act.wait_ge(gate_stored[b], 128)
        act.wait_ge(sv_read, NB)
        load(0, 0)
        load(1, 1)
        for j in range(KC):
            act_fill(act, 1, Y[:, j, :], (y_gated, 12), j)
        with act.Fori(1, 4) as it:
            for b in range(2):
                act.wait_ge(m_ready, it * 2 + (b - 1))
                load(it * 2 + b, b)
        for j in range(KC):
            if j == 0:
                act.wait_ge(psum_full, U_WO)
            act_fill(act, 2, Y[:, j, :], (m_ready, j + 1), j)

    def act_project(act, u0, k, f):
        for j in range(KC):
            act_squares(act, k, j, unit((u0 + j) % 2), (psum_full, u0 + j + 1))
            act.wait_ge(a_ready, KC * (f + 1))
            nc.scalar.activation(Y[:, j, :], unit((u0 + j) % 2), ACT.Copy).then_inc(psum_free, 1)
        act_root(act, k)

    def act_block1_out(act):
        act.wait_ge(m_ready, KC)
        act.dma_start(X[:, :, :], xT.rearrange("c p s -> p c s")).then_inc(x_loaded, 16)
        act_project(act, U_WO, 1, 2)

    def act_norm(act, k, n_fill, f, e, shift=None):
        for j in range(KC):
            act_squares(act, k, j, X[:, j, :], (x_upd, KC * e + j + 1))
        act_root(act, k)
        if f is not None:
            act_norm_fill(act, k, n_fill, f, shift)

    chain = Chain(nc.vector, dve_step)
    link = chain.link

    def dve_rope_tables(dve):
        dve.wait_ge(consts_loaded, 48)
        link(nc.vector.tensor_scalar(NSINK[:, :], SINK[:, :], -1.0, None, ALU.mult))
        dve.wait_ge(pos_loaded, 16)
        link(nc.vector.tensor_copy(ANG[:, :], POSI[:, :]))
        link(nc.vector.tensor_scalar(ANG[:, :], ANG[:, :], col("inv_freq"), None, ALU.mult))
        magic = 1.5 * 2.0 ** 23
        link(nc.vector.tensor_scalar(TURN[:, :], ANG[:, :], 1.0 / (2 * np.pi), magic, ALU.mult, ALU.add))
        link(nc.vector.tensor_scalar(TURN[:, :], TURN[:, :], -magic, None, ALU.add))
        hi = 6.28125
        mid = float(np.floor((2 * np.pi - hi) * 2 ** 21) / 2 ** 21)
        lo = float(2 * np.pi - hi - mid)
        link(nc.vector.scalar_tensor_tensor(RED[:, :], TURN[:, :], -hi, ANG[:, :], ALU.mult, ALU.add))
        link(nc.vector.scalar_tensor_tensor(RED[:, :], TURN[:, :], -mid, RED[:, :], ALU.mult, ALU.add))
        link(nc.vector.scalar_tensor_tensor(RED[:, :], TURN[:, :], -lo, RED[:, :], ALU.mult, ALU.add))
        nc.vector.tensor_scalar(RED[:, :], RED[:, :], 3.1415925, -3.1415925, ALU.min, ALU.max).then_inc(rope_angle, 1)

    def dve_ada(dve, i, at):
        dve.wait_ge(ada_done, i + 1)
        b0 = COL["b_ada"][0] + at
        return nc.vector.tensor_tensor(ADA[:, at:at + KC], psA[:, 2, 0:KC], COLS[:, b0:b0 + KC], ALU.add)

    def dve_low(f, j, src):
        nc.vector.wait_ge(a_high, KC * f + j + 1)
        nc.vector.tensor_tensor(AL[:, j, :], src, AH[:, j, :].bitcast(F32), ALU.subtract).then_inc(a_ready, 1)

    def dve_rs(dve, k):
        dve.wait_ge(rc_full, k + 1)
        nc.vector.reciprocal(RC[:, :], psA[:, 2, 0:NB]).then_inc(rc_ready, 1)

    def dve_norm_fill(dve, k, n_fill, f, gain, shift=None):
        if k:
            dve_rs(dve, k)
        dve.wait_ge(rs_full, k + 1)

        def low(j):
            nc.vector.wait_ge(a_high, KC * f + j + 1)
            if shift is None:
                nc.vector.tensor_tensor(AL[:, j, :], TN[:, j % 2, :], AH[:, j, :].bitcast(F32), ALU.subtract).then_inc(a_ready, 1)
            else:
                nc.vector.scalar_tensor_tensor(AL[:, j, :], TN[:, j % 2, :], shift(j), AH[:, j, :].bitcast(F32),
                                               ALU.add, ALU.subtract).then_inc(a_ready, 1)

        for j in range(KC):
            if j >= 2:
                dve.wait_ge(a_ready, KC * f + j - 1)
            nc.vector.scalar_tensor_tensor(TN[:, j % 2, :], X[:, j, :], gain(j), pair(0), ALU.mult, ALU.mult).then_inc(tn_ready, 1)
            if j:
                dve.wait_ge(tn_ready, KC * n_fill + j)
                low(j - 1)
        dve.wait_ge(tn_ready, KC * n_fill + KC)
        low(KC - 1)

    def dve_rotate(dve, u, scale, dst):
        dve.wait_ge(psum_full, u + 1)
        dve.wait_ge(rope_ready, 2)
        nc.vector.scalar_tensor_tensor(M1[:, :], unit(u % 2), scale, COS[:, :], ALU.mult, ALU.mult)
        for q in range(4):
            src, to = slice(32 * q, 32 * q + 32), slice(32 * (q ^ 1), 32 * (q ^ 1) + 32)
            l = nc.vector.scalar_tensor_tensor(M2[to, :], unit(u % 2)[src, :], scale, SIN[src, :], ALU.mult, ALU.mult)
        l.then_inc(psum_free, 1)
        dve.wait_ge(psum_free, u + 1)
        return nc.vector.tensor_tensor(dst, M1[:, :], M2[:, :], ALU.add)

    def dve_block1_in(dve):
        dve_rope_tables(dve)
        dve_rs(dve, 0)
        link(dve_ada(dve, 0, 8))
        g0 = COL["g_pre"][0]
        nc.vector.scalar_tensor_tensor(GS[:, :], ADA[:, 8:16], 1.0, COLS[:, g0:g0 + KC], ALU.add, ALU.mult).then_inc(ada_ready, 1)
        dve_ada(dve, 1, 0).then_inc(ada_ready, 1)
        dve.wait_ge(ada_ready, 2)
        dve_norm_fill(dve, 0, 0, 0, lambda j: GS[:, j:j + 1], lambda j: ADA[:, j:j + 1])
        link(dve_ada(dve, 2, 16))
        g0 = COL["g_post"][0]
        nc.vector.tensor_tensor(GG[:, :], ADA[:, 16:24], COLS[:, g0:g0 + KC], ALU.mult).then_inc(ada_ready, 1)
        dve.wait_ge(a_ready, KC)
        dve.wait_ge(sq_used, KC)
        nc.vector.memset(K[:, 0:P], 0.0)
        link(nc.vector.memset(V[:, 0, :], 0.0))
        for j in range(4):
            link(dve_rotate(dve, U_Q + j, HD ** -0.5, Q[:, j, :]))
        dve_rotate(dve, U_K, 1.0, K[:, P:]).then_inc(kv_ready, 1)

    SWA_STEPS = 4

    def dve_swa(dve):
        def body(it, first):
            for i in range(4):
                u, n, r = it * 4 + i, it * 2 + i // 2, i % 2
                b = i % 2
                if r == 0:
                    dve.wait_ge(qs_high, n + 1)
                    if first and i == 0:
                        dve.wait_ge(kv_ready, 2)
                    nc.vector.tensor_tensor(QSL[:, i // 2, :, :], Q[:, :, bass.ds(n * P, P)], QSH[:, i // 2, :, :].bitcast(F32), ALU.subtract)
                    nc.vector.tensor_tensor(VSL[:, i // 2, :, :], V[:, bass.ds(n, 2), :], VSH[:, i // 2, :, :].bitcast(F32),
                                            ALU.subtract)
                    nc.vector.tensor_tensor(KSL[:, i // 2, :], K[:, bass.ds(n * P, 2 * P)], KSH[:, i // 2, :].bitcast(F32),
                                            ALU.subtract).then_inc(qs_ready, 1)
                dve.wait_ge(s_full, u + 1)
                link(nc.vector.tensor_reduce(NMAX[:, b, :], pair(0).rearrange("p (j k) -> p j k", j=4), AX.X, ALU.max, negate=True))
                link(nc.vector.tensor_tensor(NM[:, b, :], NMAX[:, b, :], NSINK[:, 4 * r:4 * r + 4], ALU.min))
                nc.vector.tensor_tensor(SDIF[:, b, :], NM[:, b, :], SINK[:, 4 * r:4 * r + 4], ALU.add).then_inc(nm_ready, 1)
                dve.wait_ge(exp_done, u + 1)
                link(nc.vector.tensor_tensor(DENS[:, b, :], DEN[:, b, :], ESUM[:, b, :], ALU.add))
                link(nc.vector.reciprocal(RDEN[:, b, :], DENS[:, b, :]))
                nc.vector.tensor_tensor(PR[:, b, :, :], PR[:, b, :, :], RDEN[:, b, :].unsqueeze(2).to_broadcast([P, 4, 2 * P]),
                                        ALU.mult).then_inc(prob_ready, 1)
                dve.wait_ge(pt_high, u + 1)
                nc.vector.tensor_tensor(PTL[:, :, :].rearrange("p a f -> p (a f)"), pair(1),
                                        PTH[:, :, :].rearrange("p a f -> p (a f)").bitcast(F32), ALU.subtract).then_inc(pt_ready, 1)

        chain.loop(0, 4 * SWA_STEPS)
        body(0, True)
        chain.done(1)
        with dve.Fori(1, 4) as it:
            chain.loop(it - 1, 4 * SWA_STEPS)
            body(it, False)
        chain.done(3)

    def dve_gate(dve, g, y, u):
        dve.wait_ge(psum_free, u + 1)
        nc.vector.tensor_tensor(Y[:, y, :], Y[:, y, :], GU[:, g % 2, :], ALU.mult).then_inc(y_gated, 1)

    def dve_sgu(dve):
        dve.wait_ge(sgu_loaded, 64)
        nc.vector.tensor_tensor(WSF[:, :, :], WSF[:, :, :], mat("causal_w").unsqueeze(1).to_broadcast([P, GROUPS, P]),
                                ALU.mult).then_inc(ws_masked, 1)
        for v in range(4):
            dve.wait_ge(psum_free, U_VB + v + 1)
            for n in (2 * v, 2 * v + 1):
                link(nc.vector.bn_stats(BN6[:, n, :], GV[:, n, :]))
                l = nc.vector.bn_aggr(MV[:, n, :], BN6[:, n, :])
                if n < NB - 1:
                    link(l)
        l.then_inc(ln_stats, 1)
        dve.wait_ge(ws_high, 1)
        nc.vector.tensor_tensor(WSL[:, :, :], WSF[:, :, :], WSH[:, :, :].bitcast(F32), ALU.subtract).then_inc(ws_ready, 1)
        dve.wait_ge(ln_root, 1)
        link(nc.vector.reciprocal(RSTD[:, :], RSTD[:, :]))

        def normalise(n):
            t = LNT[:, n % 2, :]
            link(nc.vector.tensor_scalar(t, GV[:, n, :], MV[:, n, 0:1], RSTD[:, n:n + 1], ALU.subtract, ALU.mult))
            link(nc.vector.tensor_tensor(t, t, LNG[:, :], ALU.mult))
            nc.vector.tensor_tensor(t, t, LNB[:, :], ALU.add).then_inc(vn_f32, 1)
            dve.wait_ge(vn_high, n + 1)
            nc.vector.tensor_tensor(VNL[:, n % 2, :], t, VNH[:, n % 2, :].bitcast(F32), ALU.subtract).then_inc(vn_ready, 1)

        def read(n):
            dve.wait_ge(sv_full, n + 1)
            nc.vector.tensor_tensor(Y[:, 4:8, n * P:(n + 1) * P], psA[:, n % 2, :].rearrange("p (g f) -> p g f", g=GROUPS),
                                    BSB[:, :, :], ALU.add).then_inc(sv_read, 1)

        for j in range(4):
            normalise(2 * j)
            normalise(2 * j + 1)
            dve_gate(dve, j, j, U_ZA + j)
            read(2 * j)
            read(2 * j + 1)

    def dve_gating(dve):
        for j in range(4):
            if j == 0:
                dve.wait_ge(sv_read, NB)
            dve_gate(dve, 4 + j, 4 + j, U_U + j)
        for j in range(4):
            dve.wait_ge(y_gated, 5 + j)
            dve_gate(dve, 8 + j, 4 + j, U_ZB + j)

    def dve_merge(dve):
        dve.wait_ge(y_gated, 12)
        for j in range(KC):
            dve_low(1, j, Y[:, j, :])
        with dve.Fori(0, 4) as it:
            for b in range(2):
                j = it * 2 + b
                dve.wait_ge(gab_loaded[b], it * 32 + 32)
                dve.wait_ge(psum_full, j * 2 + (U_PJ + 1))
                nc.vector.tensor_tensor(GA[:, b, :], unit(0), GA[:, b, :], ALU.mult).then_inc(psum_free, 1)
                dve.wait_ge(psum_full, j * 2 + (U_PJ + 2))
                nc.vector.tensor_tensor(MB[:, b, :], unit(1), GB[:, b, :], ALU.mult).then_inc(psum_free, 1)
                dve.wait_ge(psum_free, j * 2 + (U_PJ + 2))
                nc.vector.tensor_tensor(Y[:, bass.ds(j, 1), :].rearrange("p a f -> p (a f)"), GA[:, b, :], MB[:, b, :],
                                        ALU.add).then_inc(m_ready, 1)
        for j in range(KC):
            dve_low(2, j, Y[:, j, :])

    def dve_block1_out(dve):
        dve_rs(dve, 1)
        dve.wait_ge(rs_full, 2)
        dve.wait_ge(x_loaded, 16)
        for j in range(KC):
            if j >= 2:
                dve.wait_ge(x_upd, j - 1)
            link(nc.vector.scalar_tensor_tensor(TN[:, j % 2, :], Y[:, j, :], GG[:, j:j + 1], pair(0), ALU.mult, ALU.mult))
            nc.vector.tensor_tensor(X[:, j, :], X[:, j, :], TN[:, j % 2, :], ALU.add).then_inc(x_upd, 1)

    DK, DV = P, 2 * P
    N_CH = S // GLA_CHUNK
    N_ST = N_CH - 1
    GRP = 2 * P
    QIH, QIL = sb("QIH", [P, S], 144, F32R), sb("QIL", [P, S], 148, F32R)
    KIH, KIL = sb("KIH", [P, S], 152, F32R), sb("KIL", [P, S], 156, F32R)
    GVH, GVL = sb("GVH", [P, NB, DV], 160, F32R), sb("GVL", [P, NB, DV], 168, F32R)
    KD = sb("KD", [P, S], 176)
    E = sb("E", [P, S], 180)
    EN = sb("EN", [P, S], 184)
    ED = sb("ED", [P, S], 188)
    LAH = sb("LAH", [P, NB, P], 192)
    EX = sb("EX", [P, S], 192)
    ALR = sb("ALR", [P, S], 200)
    WA2 = MATS[0:GLA_RANK + 1, 6:10, :].rearrange("p a f -> p (a f)")
    STF = sb("STF", [P, 2, DV], 204)
    LAST = sb("LAST", [P, N_CH], 206)
    STH, STL = sb("STH", [P, 2, DV], 176, F32R), sb("STL", [P, 2, DV], 178, F32R)
    KDTH, KDTL = sb("KDTH", [P, NB, DK], 184, F32R), sb("KDTL", [P, NB, DK], 188, F32R)
    ATF = sb("ATF", [P, S], 192)
    ATH, ATL = sb("ATH", [P, S], 196, F32R), sb("ATL", [P, S], 152, F32R)
    SQO = sb("SQO", [P, 2, HALF], 156)
    RSO = sb("RSO", [P, S], 156)
    PST = sb("PST", [P, 2, S], 196)
    PH, PL = sb("PH", [P, 2, S], 64, F32R), sb("PL", [P, 2, S], 72, F32R)
    PWH, PWL = sb("PWH", [P, 2, S], 80, F32R), sb("PWL", [P, 2, S], 88, F32R)
    SG = sb("SG", [P, 2, S], 184)

    parked = sem("parked")
    x_back = sem("x_back")
    wa_loaded = sem("wa_loaded")
    lr_ones = sem("lr_ones")
    la_log = sem("la_log")
    cum_full = sem("cum_full")
    e_ready = sem("e_ready")
    cd_ready = sem("cd_ready")
    ed_ready = sem("ed_ready")
    qh_ready = sem("qh_ready")
    kf_ready = sem("kf_ready")
    kh_ready = sem("kh_ready")
    qk_ready = sem("qk_ready")
    vh_ready = sem("vh_ready")
    kdt_full = sem("kdt_full")
    kdth_ready = sem("kdth_ready")
    kdt_ready = sem("kdt_ready")
    at_full = sem("at_full")
    atf_ready = sem("atf_ready")
    ath_ready = sem("ath_ready")
    at_ready = sem("at_ready")
    kv_full = sem("kv_full")
    st_upd = sem("st_upd")
    st_high = sem("st_high")
    st_ready = sem("st_ready")
    st_used = sem("st_used")
    og_read = sem("og_read")
    sqo_ready = sem("sqo_ready")
    sqo_used = sem("sqo_used")
    gy_ready = sem("gy_ready")
    ple_loaded = sem("ple_loaded")
    ple_high = sem("ple_high")
    ple_ready = sem("ple_ready")
    sg_used = sem("sg_used")

    achain = Chain(nc.scalar, act_step)
    achain.base = 1
    alink = achain.link

    def gla_units(h):
        first = U_GLA + GLA_UNITS * h
        names = ["k", "v0", "v1", "g0"] + (["next_la", "g1", "sums", "next_q"] if h < GLA_HEADS - 1 else ["g1", "sums"])
        u = {n: first + 2 + i for i, n in enumerate(names)}
        u["la"], u["q"] = (gla_units(h - 1)[n] for n in ("next_la", "next_q")) if h else (first, first + 1)
        return u

    GLA_FILL = [3, 3, 3, 3, 2, 2, 0, 0, 2, 2, 2, 1, 1, 1, 1, 1]
    GLA_CUT_AT = [6, 7, 8, 9, 10, 11]

    def pe_gla(pe):
        gemm(pe, T_LR, U_LR, T_LR % 4, U_LR % 2, fill=3)
        pe.wait_ge(wa_loaded, 32)
        pe.wait_ge(psum_free, U_LR + 1)
        pe_gla_logits(pe, 0)
        gemm(pe, T_GLA, gla_units(0)["q"], T_GLA % 4, gla_units(0)["q"] % 2)
        for h in range(GLA_HEADS):
            pe_gla_head(pe, h)

    def pe_gla_logits(pe, h):
        u = gla_units(h)["la"]
        pe.wait_ge(psum_free, u - 1)
        for n in range(NB):
            l = nc.tensor.matmul(psG[:, 2 * (u % 2) + n // 4, (n % 4) * P:(n % 4 + 1) * P], ALR[0:GLA_RANK + 1, n * P:(n + 1) * P],
                                 WA2[:, h * P:(h + 1) * P], start=True, stop=True)
        l.then_inc(psum_full, 1)

    def pe_gla_head(pe, h):
        u, t = gla_units(h), T_GLA + 6 * h
        more = h + 1 < GLA_HEADS
        pe.wait_ge(psum_free, u["la"] + 1)
        if h:
            pe.wait_ge(og_read, h * 4)
        for n in range(NB):
            l = nc.tensor.matmul(psA[:, 2 + n // 4, (n % 4) * P:(n % 4 + 1) * P], LAH[:, n, :], mat("chunk_sum"), start=True, stop=True)
        l.then_inc(cum_full, 1)
        gemm(pe, t + 1, u["k"], (t + 1) % 4, u["k"] % 2)
        pe_tokens(pe, t + 2, u["v0"], [(t + 2) % 4, (t + 3) % 4], 1, 2)
        pe.wait_ge(psum_free, u["k"] + 1)
        if h:
            pe.wait_ge(st_upd, h * N_ST)
        for n in range(NB):
            l = nc.tensor.transpose(psA[:, n // 4, (n % 4) * P:(n % 4 + 1) * P], KD[:, n * P:(n + 1) * P], mat("ident"))
        l.then_inc(kdt_full, 1)
        pe.wait_ge(qk_ready, h * 2 + 2)
        pe.wait_ge(cd_ready, h + 1)
        for n in range(NB):
            bs = slice(n * P, (n + 1) * P)
            _, l = three(psA[:, 2 + n // 4, (n % 4) * P:(n % 4 + 1) * P], KIH[:, bs], KIL[:, bs], QIH[:, bs], QIL[:, bs], True, True)
        l.then_inc(at_full, 1)
        gemm(pe, t + 4, u["g0"], (t + 4) % 4, u["g0"] % 2, begun=2)
        if more:
            pe_gla_logits(pe, h + 1)
        queue = list(gemm_slices(pe, t + 5, u["g1"], (t + 5) % 4, u["g1"] % 2))
        if more:
            queue += list(gemm_slices(pe, t + 6, u["next_q"], (t + 6) % 4, u["next_q"] % 2))
        else:
            queue += list(gemm_slices(pe, T_GO, U_GO, T_GO % 4, U_GO % 2, 4))

        def kv(c):
            if c >= 2:
                pe.wait_ge(st_upd, h * N_ST + (c - 1))
            n, r = c // 2, slice(64 * (c % 2), 64 * (c % 2) + 64)
            _, l = three(psA[:, c % 2, 0:DV], KDTH[r, n, :], KDTL[r, n, :], GVH[r, n, :], GVL[r, n, :], True, True)
            l.then_inc(kv_full, 1)

        def sums(g):
            pe.wait_ge(sqo_ready, h * 4 + (g + 1))
            if g == 0:
                pe.wait_ge(psum_free, u["sums"] - 1)
            for d in range(2):
                l = nc.tensor.matmul(psG[:, 2 * (u["sums"] % 2) + g // 2, (g % 2) * GRP:(g % 2 + 1) * GRP], mat("ones"),
                                     SQO[:, g % 2, d * GRP:(d + 1) * GRP], start=(d == 0), stop=(d == 1))
            l.then_inc(sqo_used if g < 3 else psum_full, 1)

        pe.wait_ge(kdt_ready, h + 1)
        pe.wait_ge(psum_free, u["v1"] + 1)
        for c in range(2):
            kv(c)
        pe.wait_ge(at_ready, h + 1)
        for c in range(N_CH):
            n, g = c // 2, c // 4
            bank = 2 + g % 2
            if c % 4 == 0 and g >= 2:
                pe.wait_ge(og_read, h * 4 + (g - 1))
            if c % 2 == 0:
                for d in range(2):
                    three(psA[:, bank, d * GRP + (n % 2) * P:d * GRP + (n % 2 + 1) * P], GVH[:, n, d * P:(d + 1) * P], GVL[:, n, d * P:(d + 1) * P],
                          ATH[:, n * P:(n + 1) * P], ATL[:, n * P:(n + 1) * P], c % 4 == 0 and d == 0, False)
            if c + 2 < N_ST:
                kv(c + 2)
            for _ in range(GLA_FILL[c]):
                if queue:
                    queue.pop(0)()
            if c:
                pe.wait_ge(st_ready, h * N_ST + c)
                cs = slice(c * GLA_CHUNK, (c + 1) * GLA_CHUNK)
                for d in range(2):
                    _, l = three(psA[:, bank, d * GRP + (c % 4) * GLA_CHUNK:d * GRP + (c % 4 + 1) * GLA_CHUNK],
                                 STH[:, (c - 1) % 2, d * P:(d + 1) * P], STL[:, (c - 1) % 2, d * P:(d + 1) * P], QIH[:, cs], QIL[:, cs],
                                 False, c % 4 == 3 and d == 1)
                l.then_inc(st_used, 1)
            if c == 8:
                sums(0)
                sums(1)
            elif c == 13:
                sums(2)
        sums(3)
        while queue:
            queue.pop(0)()

    def act_gla_in(act):
        act.wait_ge(x_upd, KC)
        act.dma_start(park, X[:, :, :]).then_inc(parked, 16)
        act.wait_ge(r_ready, 2)
        act.wait_ge(ws_masked, 1)
        act.dma_start(WA2[0:GLA_RANK, :], w_a2).then_inc(wa_loaded, 16)
        at, n = ROW["b_a"]
        act.dma_start(WA2[GLA_RANK:GLA_RANK + 1, :], rows[:, at:at + n]).then_inc(wa_loaded, 16)

    def act_gla(act):
        act.wait_ge(lr_ones, 1)
        act.wait_ge(psum_full, U_LR + 1)
        nc.scalar.activation(ALR[0:GLA_RANK, :], unit(U_LR % 2)[0:GLA_RANK, :], ACT.Copy).then_inc(psum_free, 1)
        act_gla_logits(act, 0)
        for h in range(GLA_HEADS):
            act_gla_head(act, h)

    def act_gla_logits(act, h, steps=(0, 1, 2)):
        if 0 in steps:
            act.wait_ge(psum_full, gla_units(h)["la"] + 1)
            alink(nc.scalar.activation(EX[:, :], unit(gla_units(h)["la"] % 2), ACT.Abs))
        if 1 in steps:
            alink(nc.scalar.activation(EX[:, :], EX[:, :], ACT.Exp, scale=-1.0))
        if 2 in steps:
            nc.scalar.activation(EX[:, :], EX[:, :], ACT.Ln, bias=mat("ones")[:, 0:1]).then_inc(la_log, 1)

    def act_gla_head(act, h):
        u = gla_units(h)
        more = h + 1 < GLA_HEADS

        def buf(x):
            return unit(u[x] % 2)

        act.wait_ge(cum_full, h + 1)
        nc.scalar.activation(E[:, :], pair(1), ACT.Exp)
        nc.scalar.activation(EN[:, :], pair(1), ACT.Exp, scale=-1.0).then_inc(e_ready, 1)
        act.wait_ge(cd_ready, h + 1)
        nc.scalar.activation(ED[:, :], ED[:, :], ACT.Exp).then_inc(ed_ready, 1)
        act.wait_ge(psum_free, u["q"] + 1)
        nc.scalar.activation(QIH[:, :], KD[:, :], ACT.Copy).then_inc(qh_ready, 1)
        act.wait_ge(kf_ready, h + 1)
        nc.scalar.activation(KIH[:, :], EN[:, :], ACT.Copy).then_inc(kh_ready, 1)
        for x in range(2):
            act.wait_ge(psum_full, u["v0"] + x + 1)
            nc.scalar.activation(GVH[:, 4 * x:4 * x + 4, :].rearrange("p n f -> p (n f)"), buf(f"v{x}"), ACT.Copy).then_inc(vh_ready, 1)
        act.wait_ge(kdt_full, h + 1)
        act.wait_ge(qk_ready, h * 2 + 2)
        nc.scalar.activation(KDTH[:, :, :].rearrange("p n f -> p (n f)"), pair(0), ACT.Copy).then_inc(kdth_ready, 1)
        act.wait_ge(atf_ready, h + 1)
        nc.scalar.activation(ATH[:, :], ATF[:, :], ACT.Copy).then_inc(ath_ready, 1)

        def gate(x):
            act.wait_ge(psum_full, u[f"g{x}"] + 1)
            act.wait_ge(psum_free, u[f"g{x}"])
            nc.scalar.activation(Y[:, 2 * h + x, :], buf(f"g{x}"), ACT.Silu).then_inc(psum_free, 1)

        def square(g):
            act.wait_ge(st_used, h * N_ST + (4 * g + 3))
            if g >= 2:
                act.wait_ge(sqo_used, h * 3 + (g - 1))
            nc.scalar.activation(SQO[:, g % 2, :], psA[:, 2 + g % 2, :], ACT.Square).then_inc(sqo_ready, 1)

        gate(0)
        for c in range(N_ST):
            act.wait_ge(st_upd, h * N_ST + (c + 1))
            if c >= 2:
                act.wait_ge(st_used, h * N_ST + (c - 1))
            nc.scalar.activation(STH[:, c % 2, :], STF[:, c % 2, :], ACT.Copy).then_inc(st_high, 1)
            if more and c < 3:
                if c == 0:
                    act.wait_ge(at_ready, h + 1)
                act_gla_logits(act, h + 1, (c,))
            if c == 5:
                gate(1)
            if c % 4 == 3:
                square(c // 4)
            if not more and c in GLA_CUT_AT:
                if c == GLA_CUT_AT[0]:
                    act.wait_ge(psum_full, u["g1"] + 1)
                act_fill(act, 4, Y[:, GLA_CUT_AT.index(c), :], (gy_ready, GLA_CUT_AT.index(c) + 1), GLA_CUT_AT.index(c))
        square(3)
        act.wait_ge(og_read, h * 4 + 4)
        act.wait_ge(psum_full, u["sums"] + 1)
        nc.scalar.activation(RSO[:, :], buf("sums"), ACT.Sqrt, bias=col("eps"), scale=1.0 / DV).then_inc(psum_free, 1)

    def dve_gla(dve):
        dve.wait_ge(parked, 16)
        dve.wait_ge(a_ready, KC * 4)
        nc.vector.memset(ALR[0:GLA_RANK + 1, :], 1.0).then_inc(lr_ones, 1)
        dve_gla_logits(dve, 0)
        for h in range(GLA_HEADS):
            dve_gla_head(dve, h)
        dve_gla_norm(dve, GLA_HEADS - 1)

    def dve_gla_logits(dve, h):
        u = gla_units(h)["la"]
        dve.wait_ge(la_log, h + 1)
        dve.wait_ge(psum_free, u)
        nc.vector.scalar_tensor_tensor(LAH[:, :, :].rearrange("p n f -> p (n f)"), unit(u % 2), 0.0, EX[:, :], ALU.min, ALU.subtract).then_inc(psum_free, 1)

    def dve_gla_norm(dve, h):
        dve.wait_ge(psum_free, gla_units(h)["sums"] + 1)
        link(nc.vector.reciprocal(RSO[:, :], RSO[:, :]))
        for x in range(2):
            y = Y[:, 2 * h + x, :]
            dve.wait_ge(og_read, h * 4 + 4)
            nc.vector.scalar_tensor_tensor(y, y, col("o_gain", x), RSO[:, :], ALU.mult, ALU.mult).then_inc(gy_ready, 1)

    def dve_gla_head(dve, h):
        u = gla_units(h)
        more = h + 1 < GLA_HEADS

        def buf(x):
            return unit(u[x] % 2)

        dve.wait_ge(e_ready, h + 1)
        cum = pair(1).rearrange("p (c t) -> p c t", t=GLA_CHUNK)
        link(nc.vector.tensor_scalar(LAST[:, :], cum[:, :, GLA_CHUNK - 1], 1.0, None, ALU.mult))
        nc.vector.tensor_tensor(ED[:, :].rearrange("p (c t) -> p c t", t=GLA_CHUNK), LAST[:, :].unsqueeze(2).to_broadcast([P, N_CH, GLA_CHUNK]),
                                cum, ALU.subtract).then_inc(cd_ready, 1)
        dve.wait_ge(psum_full, u["q"] + 1)
        nc.vector.scalar_tensor_tensor(KD[:, :], buf("q"), DK ** -0.5, E[:, :], ALU.mult, ALU.mult).then_inc(psum_free, 1)
        dve.wait_ge(qh_ready, h + 1)
        dve.wait_ge(psum_free, u["q"] + 1)
        nc.vector.tensor_tensor(QIL[:, :], KD[:, :], QIH[:, :].bitcast(F32), ALU.subtract).then_inc(qk_ready, 1)
        if h:
            dve_gla_norm(dve, h - 1)
        dve.wait_ge(psum_full, u["k"] + 1)
        nc.vector.tensor_tensor(EN[:, :], buf("k"), EN[:, :], ALU.mult).then_inc(kf_ready, 1)
        dve.wait_ge(ed_ready, h + 1)
        dve.wait_ge(qk_ready, h * 2 + 1)
        nc.vector.tensor_tensor(KD[:, :], buf("k"), ED[:, :], ALU.mult).then_inc(psum_free, 1)
        dve.wait_ge(kh_ready, h + 1)
        nc.vector.tensor_tensor(KIL[:, :], EN[:, :], KIH[:, :].bitcast(F32), ALU.subtract).then_inc(qk_ready, 1)
        for x in range(2):
            dve.wait_ge(vh_ready, h * 2 + (x + 1))
            nc.vector.tensor_tensor(GVL[:, 4 * x:4 * x + 4, :].rearrange("p n f -> p (n f)"), buf(f"v{x}"),
                                    GVH[:, 4 * x:4 * x + 4, :].rearrange("p n f -> p (n f)").bitcast(F32), ALU.subtract).then_inc(psum_free, 1)
        dve.wait_ge(kdth_ready, h + 1)
        nc.vector.tensor_tensor(KDTL[:, :, :].rearrange("p n f -> p (n f)"), pair(0),
                                KDTH[:, :, :].rearrange("p n f -> p (n f)").bitcast(F32), ALU.subtract).then_inc(kdt_ready, 1)
        dve.wait_ge(at_full, h + 1)
        link(nc.vector.tensor_scalar(ATF[:, :], pair(1), 3e38, -3e38, ALU.min, ALU.max))
        nc.vector.tensor_tensor(ATF[:, :].rearrange("p (n f) -> p n f", f=P), ATF[:, :].rearrange("p (n f) -> p n f", f=P),
                                mat("chunk_mask").unsqueeze(1).to_broadcast([P, NB, P]), ALU.mult).then_inc(atf_ready, 1)
        dve.wait_ge(ath_ready, h + 1)
        nc.vector.tensor_tensor(ATL[:, :], ATF[:, :], ATH[:, :].bitcast(F32), ALU.subtract).then_inc(at_ready, 1)

        def update(c):
            dve.wait_ge(kv_full, h * N_ST + (c + 1))
            new = psA[:, c % 2, 0:DV]
            if c == 0:
                nc.vector.tensor_copy(STF[:, 0, :], new).then_inc(st_upd, 1)
                return
            dve.wait_ge(st_upd, h * N_ST + c)
            if c >= 2:
                dve.wait_ge(st_ready, h * N_ST + (c - 1))
            end = (c + 1) * GLA_CHUNK - 1
            nc.vector.scalar_tensor_tensor(STF[:, c % 2, :], STF[:, (c - 1) % 2, :], E[:, end:end + 1], new, ALU.mult, ALU.add).then_inc(st_upd, 1)

        def low(c):
            dve.wait_ge(st_high, h * N_ST + (c + 1))
            nc.vector.tensor_tensor(STL[:, c % 2, :], STF[:, c % 2, :], STH[:, c % 2, :].bitcast(F32), ALU.subtract).then_inc(st_ready, 1)

        def out(g):
            dve.wait_ge(psum_free, u["g1"] + 1)
            dve.wait_ge(sqo_ready, h * 4 + (g + 1))
            y = Y[:, 2 * h:2 * h + 2, g * GRP:(g + 1) * GRP]
            nc.vector.tensor_tensor(y, psA[:, 2 + g % 2, :].rearrange("p (d f) -> p d f", d=2), y, ALU.mult).then_inc(og_read, 1)

        update(0)
        for c in range(N_ST):
            if c + 1 < N_ST:
                update(c + 1)
            low(c)
            if more and c == 3:
                dve_gla_logits(dve, h + 1)
            if c in (6, 7, 11):
                out({6: 0, 7: 1, 11: 2}[c])
            if not more and c in GLA_CUT_AT:
                dve_low(4, GLA_CUT_AT.index(c), Y[:, GLA_CUT_AT.index(c), :])
        out(3)

    def act_mixer_out(act, layer, f, u0, k, y_ready, early):
        for j in range(early, KC):
            act_fill(act, f, Y[:, j, :], y_ready(j), j)
            if j == KC - 1:
                act.dma_start(X[:, :, :], park).then_inc(x_back, 16)
                act.dma_start(PST[:, :, :], pT[layer].rearrange("c p s -> p c s")).then_inc(ple_loaded, 16)
        for j in range(KC):
            act_squares(act, k, j, X[:, j, :], (psum_free, u0 + j + 1))
            if j in (0, 2):
                n = 2 * layer + j // 2
                act.wait_ge(ple_loaded, 16 * (n + 1))
                if j == 0:
                    act.wait_ge(a_ready, KC * (f + 1))
                dst = PWH if j else PH
                nc.scalar.activation(dst[:, :, :], PST[:, :, :], ACT.Copy).then_inc(ple_high, 1)
                if j == 0:
                    act.wait_ge(ple_ready, n + 1)
                    act.dma_start(PST[:, :, :], ple_w[layer].rearrange("c p n -> p c n")).then_inc(ple_loaded, 16)

    def dve_mixer_out(dve, layer, f, u0, n_back, early):
        for j in range(early, KC):
            dve_low(f, j, Y[:, j, :])
        dve.wait_ge(x_back, 16 * n_back)
        for j in range(KC):
            dve.wait_ge(psum_full, u0 + j + 1)
            nc.vector.tensor_tensor(X[:, j, :], X[:, j, :], unit((u0 + j) % 2), ALU.add).then_inc(psum_free, 1)
            if j in (0, 2):
                n = 2 * layer + j // 2
                high, low = (PWH, PWL) if j else (PH, PL)
                dve.wait_ge(ple_high, n + 1)
                nc.vector.tensor_tensor(low[:, :, :], PST[:, :, :], high[:, :, :].bitcast(F32), ALU.subtract).then_inc(ple_ready, 1)

    def pe_ple(pe, layer, t0, u0, f, k):
        for j in range(KC):
            gemm(pe, t0 + j, u0 + 2 * j, (t0 + j) % 4, u0 % 2, fill=f if j == 0 else None)
            pe.wait_ge(ple_ready, 2 * layer + 2)
            b = (u0 + 1) % 2
            pe.wait_ge(psum_free, u0 + 2 * j)
            js = slice(j * P, (j + 1) * P)
            for h in range(2):
                hs = slice(h * HALF, (h + 1) * HALF)
                for c in range(2):
                    _, l = three(psG[:, 2 * b + h, :], PWH[:, c, js], PWL[:, c, js], PH[:, c, hs], PL[:, c, hs], c == 0, c == 1)
            l.then_inc(psum_full, 1)
            if j:
                pe_square(pe, k, j - 1)
        pe_square(pe, k, KC - 1)

    def act_ple(act, layer, u0, k, e):
        for j in range(KC):
            act.wait_ge(psum_full, u0 + 2 * j + 1)
            act.wait_ge(psum_free, u0 + 2 * j)
            nc.scalar.activation(SG[:, j % 2, :], unit(u0 % 2), ACT.Sigmoid).then_inc(psum_free, 1)
            act_squares(act, k, j, X[:, j, :], (x_upd, KC * e + j + 1))

    def dve_ple(dve, layer, u0, e):
        for j in range(KC):
            dve.wait_ge(psum_free, u0 + 2 * j + 1)
            dve.wait_ge(psum_full, u0 + 2 * j + 2)
            nc.vector.tensor_tensor(SG[:, j % 2, :], unit((u0 + 1) % 2), SG[:, j % 2, :], ALU.mult).then_inc(psum_free, 1)
            dve.wait_ge(psum_free, u0 + 2 * j + 2)
            nc.vector.tensor_tensor(X[:, j, :], X[:, j, :], SG[:, j % 2, :], ALU.add).then_inc(x_upd, 1)

    def act_root_fill(act, k, n_fill, f, done):
        act_root(act, k)
        act.wait_ge(psum_full, done)
        act_norm_fill(act, k, n_fill, f)

    PAIRS = FOX_HEADS // 2
    FQH, FQL = sb("FQH", [P, S], 144, F32R), sb("FQL", [P, S], 148, F32R)
    FKH, FKL = sb("FKH", [P, S], 152, F32R), sb("FKL", [P, S], 156, F32R)
    FVH, FVL = sb("FVH", [P, NB, P], 160, F32R), sb("FVL", [P, NB, P], 164, F32R)
    FP = sb("FP", [P, 2, 2, S], 168)
    FTH, FTL = sb("FTH", [P, 2, HALF], 184, F32R), sb("FTL", [P, 2, HALF], 188, F32R)
    CALL = sb("CALL", [P, S], 192, F32R)
    LF = sb("LF", [P, S], 200)
    EXF = sb("EXF", [P, S], 196)
    FSQ = [sb("FSQ_Q", [P, S], 196), sb("FSQ_K", [P, S], 200)]
    FN = [Y[:, KC - 1, :], sb("FN_K", [P, S], 196)[:, :]]
    FREX = sb("FREX", [P, S], 200)
    VF = sb("VF", [P, S], 200)
    SELP = sb("SELP", [P, 2, P], 204, F32R)
    LFT = sb("LFT", [P, NB, FOX_HEADS], 205)
    FREC = sb("FREC", [P, 4 * NB], 205.5)
    NMX, FDEN, FRD = sb("NMX", [P, 4], 206), sb("FDEN", [P, 4], 206.0625), sb("FRD", [P, 4], 206.125)

    PARTS = [(i + 2) // 2 for i in range(NB)]
    AT_PART = [sum(PARTS[:i]) for i in range(NB)]
    N_PARTS, N_S = sum(PARTS), 2 * NB
    FILL = [[4, 5], [2, 5], [3, 3], [2, 4], [1, 4], [1, 1, 2], [1, 1, 3], [1, 1, 1, 3], []]

    FILL_LAST = FILL[:2] + [[2, 2], [2, 2], [2, 2], [1, 1, 2], [1, 1, 2], [1, 1, 1, 1], [1, 1, 1, 1]]

    f_log = sem("f_log")
    f_ready = sem("f_ready")
    f_turned = sem("f_turned")
    f_high = sem("f_high")
    fsq_ready = sem("fsq_ready")
    fsum_full = sem("fsum_full")
    froot_ready = sem("froot_ready")
    frec_ready = sem("frec_ready")
    fqk_high = sem("fqk_high")
    fqk_ready = sem("fqk_ready")
    fn_ready = sem("fn_ready")
    sel_ready = sem("sel_ready")
    fv_turned = sem("fv_turned")
    fv_high = sem("fv_high")
    fv_ready = sem("fv_ready")
    fs_full = sem("fs_full")
    fmax_ready = sem("fmax_ready")
    fexp_done = sem("fexp_done")
    frd_ready = sem("frd_ready")
    fp_ready = sem("fp_ready")
    ft_full = sem("ft_full")
    ft_high = sem("ft_high")
    ft_ready = sem("ft_ready")
    fpv_done = sem("fpv_done")
    fo_read = sem("fo_read")

    def scores(i, r):
        return psA[:, r, 0:(i + 1) * P] if i < 4 else pair(0)[:, 0:(i + 1) * P]

    def fox_buf(x):
        return unit((U_FOX + x) % 2)

    FOX_BEGUN = 2
    FOX_CUT_AT = [0, 1, 2, 3, 4, 5, 6]

    def fox_tile(p, x):
        return p * 4 + (T_FOX + x), p * 4 + (U_FOX + x), (T_FOX + x) % 4, (U_FOX + x) % 2

    def pe_fox_sums(pe, p):
        pe.wait_ge(fsq_ready, p * 2 + 2)
        for x in range(2):
            for n in range(NB):
                at = (x * NB + n) * 2
                l = nc.tensor.matmul(psA[:, 0, at:at + 2], FSQ[x][:, n * P:(n + 1) * P], mat("head_ones")[:, 0:P:HD], start=True, stop=True)
        l.then_inc(fsum_full, 1)

    def pe_fox_spread(pe, p, x):
        pe.wait_ge(frec_ready, p * 3 + (x + 2))
        if x:
            pe.wait_ge(fn_ready, p * 2 + 1)
        for n in range(NB):
            l = nc.tensor.transpose(psA[:, n // 4, (n % 4) * P:(n % 4 + 1) * P], FREX[:, n * P:(n + 1) * P], mat("ident"))
        l.then_inc(fsum_full, 1)

    def pe_fox_in(pe):
        gemm(pe, T_F, U_F, T_F % 4, U_F % 2, fill=6)
        gemm(pe, *fox_tile(0, 0))
        pe.wait_ge(f_ready, 1)
        for n in range(NB):
            l = nc.tensor.transpose(psA[:, 0, n * FOX_HEADS:(n + 1) * FOX_HEADS], LF[0:FOX_HEADS, n * P:(n + 1) * P],
                                    mat("ident")[0:FOX_HEADS, 0:FOX_HEADS])
        l.then_inc(f_turned, 1)
        gemm(pe, *fox_tile(0, 1))
        pe.wait_ge(f_ready, 2)
        for n in range(NB):
            for m in range(n + 1):
                l = nc.tensor.matmul(psA[0:FOX_HEADS, 2 + n // 4, (n % 4) * P:(n % 4 + 1) * P], LFT[:, m, :],
                                     mat("causal_sum" if m == n else "ones"), start=(m == 0), stop=(m == n))
        l.then_inc(f_turned, 1)
        pe_fox_sums(pe, 0)
        for x in range(2):
            pe_fox_spread(pe, 0, x)
        gemm(pe, *fox_tile(0, 2))

    def pe_fox_pair(pe, p, more):
        nxt = p + 1
        queue = list(gemm_slices(pe, *fox_tile(p, 3)))
        if more:
            queue += list(gemm_slices(pe, *fox_tile(nxt, 0))) + list(gemm_slices(pe, *fox_tile(nxt, 1)))
        else:
            one, two = [list(gemm_slices(pe, T_FO + j, U_FO + j, (T_FO + j) % 4, (U_FO + j) % 2, 7, 14 * j)) for j in range(FOX_BEGUN)]
            for c in range(0, 2 * KC, 2):
                queue += one[c:c + 2] + two[c:c + 2]

        plan = FILL if more else FILL_LAST

        def fill(place, n):
            for _ in range(plan[place][n] if n < len(plan[place]) else 0):
                if queue:
                    queue.pop(0)()

        def score(i, r):
            s = 2 * i + r
            if s == 0:
                pe.wait_ge(fqk_ready, p * 2 + 2)
                pe.wait_ge(sel_ready, p + 1)
                pe.wait_ge(f_ready, 4)
            elif i >= 4:
                pe.wait_ge(fexp_done, p * N_S + s)
            elif i:
                pe.wait_ge(fexp_done, p * N_S + (s - 1))
            hs = slice(64 * r, 64 * r + 64)
            out = scores(i, r)
            n = (i + 1) * P
            for at in range(0, n, HALF):
                ks = slice(at, min(at + HALF, n))
                last = ks.stop == n
                three(out[:, ks], FQH[hs, i * P:n], FQL[hs, i * P:n], FKH[hs, ks], FKL[hs, ks], True, False)
                l = nc.tensor.matmul(out[:, ks], SELP[:, r, :], CALL[:, ks], start=False, stop=not last)
                if last:
                    l = nc.tensor.matmul(out[:, i * P:n], IDR[:, :], HIDE[:, 2, :], start=False, stop=True)
            l.then_inc(fs_full, 1)

        def turn(i, x):
            g = AT_PART[i] + x
            if x == 0:
                pe.wait_ge(fp_ready, p * N_S + (2 * i + 2))
            if g == 0:
                pe.wait_ge(fv_ready, p + 1)
            else:
                pe.wait_ge(ft_ready, p * N_PARTS + g)
            for n in range(2 * x, min(2 * x + 2, i + 1)):
                for r in range(2):
                    at = (n % 2) * 2 * P + r * P
                    l = nc.tensor.transpose(psA[:, 2, at:at + P], FP[:, i % 2, r, n * P:(n + 1) * P], mat("ident"))
            l.then_inc(ft_full, 1)

        def weigh(i, x):
            g = AT_PART[i] + x
            pe.wait_ge(ft_ready, p * N_PARTS + (g + 1))
            if x == 0 and i:
                pe.wait_ge(fo_read, p * NB + i)
            for n in range(2 * x, min(2 * x + 2, i + 1)):
                ts = slice((n % 2) * 2 * P, (n % 2 + 1) * 2 * P)
                _, l = three(psA[:, 3, 0:2 * P], FVH[:, n, :], FVL[:, n, :], FTH[:, g % 2, ts], FTL[:, g % 2, ts], n == 0, n == i)
            l.then_inc(fpv_done, 1)

        def ahead(i, r):
            if i + 1 < NB:
                score(i + 1, r)
            elif more and r == 0:
                pe_fox_sums(pe, nxt)
            elif more:
                pe_fox_spread(pe, nxt, 0)

        score(0, 0)
        score(0, 1)
        fill(0, 0)
        pe.wait_ge(psum_free, p * 4 + (U_FOX + 3))
        for n in range(NB):
            l = nc.tensor.transpose(psA[:, 2 + n // 4, (n % 4) * P:(n % 4 + 1) * P], VF[:, n * P:(n + 1) * P], mat("ident"))
        l.then_inc(fv_turned, 1)
        fill(0, 1)
        for i in range(NB):
            turn(i, 0)
            ahead(i, 0)
            fill(i + 1, 0)
            for x in range(PARTS[i]):
                if x + 1 < PARTS[i]:
                    turn(i, x + 1)
                weigh(i, x)
                if x == 0:
                    ahead(i, 1)
                if x == 1 and i + 1 == NB and more:
                    pe_fox_spread(pe, nxt, 1)
                fill(i + 1, x + 1)
        while queue:
            queue.pop(0)()
        if more:
            gemm(pe, *fox_tile(nxt, 2))

    def pe_fox(pe):
        pe_fox_in(pe)
        with pe.Fori(0, PAIRS - 1) as p:
            pe_fox_pair(pe, p, True)
        pe_fox_pair(pe, PAIRS - 1, False)

    def act_fox_square(act, p, x):
        act.wait_ge(psum_full, p * 4 + (U_FOX + x + 1))
        nc.scalar.activation(FSQ[x][:, :], fox_buf(x), ACT.Square).then_inc(fsq_ready, 1)

    def act_fox_root(act, p):
        act.wait_ge(fsum_full, p * 3 + 1)
        nc.scalar.activation(FREC[:, :], psA[:, 0, 0:4 * NB], ACT.Sqrt, bias=col("eps64")).then_inc(froot_ready, 1)

    def act_fox_spread(act, p, x):
        act.wait_ge(fsum_full, p * 3 + (x + 2))
        nc.scalar.activation(FN[x], pair(0), ACT.Copy).then_inc(fn_ready, 1)

    def act_fox_qkv(act, p):
        u = p * 4 + U_FOX
        for r in range(2):
            h = p * 2 + r
            l = nc.scalar.activation(SELP[:, r, :], COLS[:, bass.ds(h + COL["selector"][0], 1)].to_broadcast([P, P]), ACT.Copy)
        l.then_inc(sel_ready, 1)
        for x in range(2):
            act.wait_ge(psum_free, u + (x + 1))
            nc.scalar.activation((FKH if x else FQH)[:, :], FN[x], ACT.Copy, scale=8.0 if x else 1.0).then_inc(fqk_high, 1)
        act.wait_ge(psum_full, u + 3)
        nc.scalar.activation(VF[:, :], fox_buf(2), ACT.Copy).then_inc(psum_free, 1)

    def act_fox_in(act):
        act.wait_ge(x_upd, KC * 2)
        act.dma_start(park, X[:, :, :]).then_inc(parked, 16)

    def act_fox_gates(act):
        act.wait_ge(parked, 32)
        act.wait_ge(psum_full, U_F + 1)
        fs = slice(0, FOX_HEADS)
        alink(nc.scalar.activation(EXF[fs, :], unit(U_F % 2)[fs, :], ACT.Abs, bias=col("b_f")[fs, :]))
        alink(nc.scalar.activation(EXF[fs, :], EXF[fs, :], ACT.Exp, scale=-1.0))
        nc.scalar.activation(EXF[fs, :], EXF[fs, :], ACT.Ln, bias=mat("ones")[fs, 0:1]).then_inc(f_log, 1)
        act.wait_ge(f_turned, 2)
        act.wait_ge(f_ready, 3)
        nc.scalar.activation(CALL[fs, :], pair(1)[fs, :], ACT.Copy).then_inc(f_high, 1)
        for x in range(2):
            act_fox_square(act, 0, x)
        act_fox_root(act, 0)
        for x in range(2):
            act_fox_spread(act, 0, x)
        act_fox_qkv(act, 0)

    def act_fox_pair(act, p, more):
        u, nxt = p * 4 + U_FOX, p + 1

        def exp(i, r):
            s = 2 * i + r
            act.wait_ge(fmax_ready, p * N_S + (s + 1))
            nc.scalar.activation(FP[:, i % 2, r, 0:(i + 1) * P], scores(i, r), ACT.Exp, bias=NMX[:, s % 4:s % 4 + 1],
                                 accum_out=FDEN[:, s % 4:s % 4 + 1]).then_inc(fexp_done, 1)

        def high(i, x):
            g = AT_PART[i] + x
            w = (min(2 * x + 2, i + 1) - 2 * x) * 2 * P
            act.wait_ge(ft_full, p * N_PARTS + (g + 1))
            if g >= 2:
                act.wait_ge(fpv_done, p * N_PARTS + (g - 1))
            nc.scalar.activation(FTH[:, g % 2, 0:w], psA[:, 2, 0:w], ACT.Copy).then_inc(ft_high, 1)

        def ahead(i, r):
            if i + 1 < NB:
                exp(i + 1, r)
            elif more and r == 0:
                act_fox_root(act, nxt)
            elif more:
                act_fox_spread(act, nxt, 0)

        def gate():
            act.wait_ge(psum_full, u + 4)
            act.wait_ge(fv_ready, 1)
            nc.scalar.activation(Y[:, bass.ds(p, 1), :].rearrange("p a f -> p (a f)"), fox_buf(3), ACT.Silu).then_inc(psum_free, 1)

        exp(0, 0)
        exp(0, 1)
        act.wait_ge(fv_turned, p + 1)
        nc.scalar.activation(FVH[:, :, :].rearrange("p n f -> p (n f)"), pair(1), ACT.Copy).then_inc(fv_high, 1)
        for i in range(NB):
            high(i, 0)
            ahead(i, 0)
            for x in range(1, PARTS[i]):
                high(i, x)
                if x == 1:
                    ahead(i, 1)
                if x == 2 and i + 1 == NB and more:
                    act_fox_spread(act, nxt, 1)
            if PARTS[i] == 1:
                ahead(i, 1)
            if i == GATE_AT:
                gate()
            if not more and i in FOX_CUT_AT:
                if i == FOX_CUT_AT[0]:
                    act.wait_ge(psum_full, U_FO)
                j = FOX_CUT_AT.index(i)
                act_fill(act, 7, Y[:, j, :], (fo_read, (j + 1) * NB), j)
            if more and i == SQUARE_AT[0]:
                act_fox_square(act, nxt, 0)
            if more and i == SQUARE_AT[1]:
                act_fox_square(act, nxt, 1)
        if more:
            act_fox_qkv(act, nxt)

    def filled(n):
        done = np.cumsum([sum(f) for f in FILL])
        return int(np.argmax(done >= n)) - 1 if (done >= n).any() else NB - 1

    GATE_AT = filled(16)
    SQUARE_AT = [filled(32), filled(48)]

    def act_fox(act):
        act_fox_gates(act)
        with act.Fori(0, PAIRS - 1) as p:
            act_fox_pair(act, p, True)
        act_fox_pair(act, PAIRS - 1, False)

    def dve_fox_rec(dve, p):
        dve.wait_ge(froot_ready, p + 1)
        nc.vector.reciprocal(FREC[:, :], FREC[:, :]).then_inc(frec_ready, 1)
        dve.wait_ge(frec_ready, p * 3 + 1)
        dve_fox_widen(dve, 0)

    def dve_fox_widen(dve, x):
        nc.vector.tensor_copy(FREX[:, :].rearrange("p (n f) -> p n f", f=HD), FREC[:, x * 2 * NB:(x + 1) * 2 * NB].unsqueeze(2).to_broadcast([P, 2 * NB, HD])).then_inc(frec_ready, 1)

    def dve_fox_norm(dve, p, x):
        dve.wait_ge(fn_ready, p * 2 + (x + 1))
        nc.vector.scalar_tensor_tensor(FN[x], fox_buf(x), col("k_gain" if x else "q_gain"), FN[x], ALU.mult, ALU.mult).then_inc(psum_free, 1)
        if x == 0:
            dve_fox_widen(dve, 1)

    def dve_fox_low(dve, p):
        for x in range(2):
            dve.wait_ge(fqk_high, p * 2 + (x + 1))
            if x:
                l = nc.vector.scalar_tensor_tensor(FKL[:, :], FN[1], 8.0, FKH[:, :].bitcast(F32), ALU.mult, ALU.subtract)
            else:
                l = nc.vector.tensor_tensor(FQL[:, :], FN[0], FQH[:, :].bitcast(F32), ALU.subtract)
            l.then_inc(fqk_ready, 1)

    def dve_fox_gates(dve):
        fs = slice(0, FOX_HEADS)
        dve.wait_ge(f_log, 1)
        nc.vector.tensor_scalar(LF[fs, :], unit(U_F % 2)[fs, :], col("b_f")[fs, :], 0.0, ALU.add, ALU.min).then_inc(psum_free, 1)
        dve.wait_ge(psum_free, U_F + 1)
        nc.vector.tensor_tensor(LF[fs, :], LF[fs, :], EXF[fs, :], ALU.subtract).then_inc(f_ready, 1)
        dve.wait_ge(f_turned, 1)
        nc.vector.tensor_copy(LFT[:, :, :].rearrange("p n h -> p (n h)"), psA[:, 0, 0:NB * FOX_HEADS]).then_inc(f_ready, 1)
        nc.vector.memset(CALL[:, :].bitcast(F32), 0.0).then_inc(f_ready, 1)
        dve.wait_ge(f_high, 1)
        nc.vector.tensor_tensor(CALL[32:32 + FOX_HEADS, :], pair(1)[fs, :], CALL[fs, :].bitcast(F32), ALU.subtract).then_inc(f_ready, 1)
        dve_fox_rec(dve, 0)
        for x in range(2):
            dve_fox_norm(dve, 0, x)
        dve_fox_low(dve, 0)

    def dve_fox_pair(dve, p, more):
        u, nxt = p * 4 + U_FOX, p + 1

        def peak(i, r):
            s = 2 * i + r
            dve.wait_ge(fs_full, p * N_S + (s + 1))
            nc.vector.tensor_reduce(NMX[:, s % 4:s % 4 + 1], scores(i, r), AX.X, ALU.max, negate=True).then_inc(fmax_ready, 1)

        def divide(i, r):
            s = 2 * i + r
            dve.wait_ge(fexp_done, p * N_S + (s + 1))
            nc.vector.reciprocal(FRD[:, s % 4:s % 4 + 1], FDEN[:, s % 4:s % 4 + 1]).then_inc(frd_ready, 1)
            dve.wait_ge(frd_ready, p * N_S + (s + 1))
            probs = FP[:, i % 2, r, 0:(i + 1) * P]
            nc.vector.tensor_scalar(probs, probs, FRD[:, s % 4:s % 4 + 1], None, ALU.mult).then_inc(fp_ready, 1)

        def low(i, x):
            g = AT_PART[i] + x
            w = (min(2 * x + 2, i + 1) - 2 * x) * 2 * P
            dve.wait_ge(ft_high, p * N_PARTS + (g + 1))
            nc.vector.tensor_tensor(FTL[:, g % 2, 0:w], psA[:, 2, 0:w], FTH[:, g % 2, 0:w].bitcast(F32), ALU.subtract).then_inc(ft_ready, 1)

        def out(i):
            dve.wait_ge(fpv_done, p * N_PARTS + (AT_PART[i] + PARTS[i]))
            if i == 0:
                dve.wait_ge(psum_free, u + 4)
            for r in range(2):
                hs = slice(64 * r, 64 * r + 64)
                y = Y[hs, bass.ds(p, 1), i * P:(i + 1) * P].rearrange("p a f -> p (a f)")
                l = nc.vector.tensor_tensor(y, psA[hs, 3, r * P:(r + 1) * P], y, ALU.mult)
            l.then_inc(fo_read, 1)

        peak(0, 0)
        peak(0, 1)
        divide(0, 0)
        divide(0, 1)
        dve.wait_ge(fv_high, p + 1)
        nc.vector.tensor_tensor(FVL[:, :, :].rearrange("p n f -> p (n f)"), pair(1), FVH[:, :, :].rearrange("p n f -> p (n f)").bitcast(F32),
                                ALU.subtract).then_inc(fv_ready, 1)
        for i in range(NB):
            more_blocks = i + 1 < NB
            low(i, 0)
            if more_blocks:
                peak(i + 1, 0)
            elif more:
                dve_fox_rec(dve, nxt)
            if PARTS[i] > 1:
                low(i, 1)
            elif i:
                out(i)
            if more_blocks:
                divide(i + 1, 0)
                peak(i + 1, 1)
            elif more:
                dve_fox_norm(dve, nxt, 0)
            if PARTS[i] > 2:
                low(i, 2)
            if more_blocks:
                divide(i + 1, 1)
            elif more:
                dve_fox_norm(dve, nxt, 1)
            if PARTS[i] > 3:
                low(i, 3)
            if PARTS[i] > 1 or i == 0:
                out(i)
            if not more and i in FOX_CUT_AT:
                dve_low(7, FOX_CUT_AT.index(i), Y[:, FOX_CUT_AT.index(i), :])
        if more:
            dve_fox_low(dve, nxt)

    def dve_fox(dve):
        dve.wait_ge(parked, 32)
        dve_fox_gates(dve)
        with dve.Fori(0, PAIRS - 1) as p:
            dve_fox_pair(dve, p, True)
        dve_fox_pair(dve, PAIRS - 1, False)

    def dve_final(dve, k, n_fill):
        dve_rs(dve, k)
        dve.wait_ge(rs_full, k + 1)
        for j in range(KC):
            if j >= 2:
                dve.wait_ge(out_stored[j % 2], 16 * (j // 2))
            nc.vector.scalar_tensor_tensor(TN[:, j % 2, :], X[:, j, :], col("final", j), pair(0), ALU.mult, ALU.mult).then_inc(tn_ready, 1)

    def sp_out(sp, n_fill):
        for j in range(KC):
            sp.wait_ge(tn_ready, KC * n_fill + j + 1)
            sp.dma_start(outT[j], TN[:, j % 2, :]).then_inc(out_stored[j % 2], 16)
        for b in range(2):
            sp.wait_ge(out_stored[b], 16 * KC // 2)

    out_stored = [sem(f"out_stored{i}") for i in range(2)]

    @block.sync
    def _(sp):
        sp_inputs(sp)
        sp_stream(sp)
        sp_out(sp, 5)

    @block.gpsimd
    def _(pool):
        pool_stream(pool)

    @block.tensor
    def _(pe):
        pe_block1_in(pe)
        pe_swa(pe)
        pe_sgu(pe)
        pe_tiles(pe, T_U, U_U, 8)
        pe_merge(pe)
        pe_out(pe, T_WO, U_WO, 2, 1)
        pe_recip(pe, 1)
        pe_sumsq(pe, 2)
        pe_recip(pe, 2)
        pe_gla(pe)
        pe_out(pe, T_GO, U_GO, 4, 3, 1)
        pe_recip(pe, 3)
        pe_ple(pe, 0, T_PLE0, U_PLE0, 5, 4)
        pe_recip(pe, 4)
        pe_fox(pe)
        pe_out(pe, T_FO, U_FO, 7, 5, FOX_BEGUN)
        pe_recip(pe, 5)
        pe_ple(pe, 1, T_PLE1, U_PLE1, 8, 6)
        pe_recip(pe, 6)

    @block.scalar
    def _(act):
        act_block1_in(act)
        act_swa(act)
        act_sgu(act)
        act_gating(act)
        act_merge(act)
        act_block1_out(act)
        for j in range(KC):
            act_squares(act, 2, j, X[:, j, :], (x_upd, j + 1))
        act_gla_in(act)
        act_root_fill(act, 2, 1, 3, U_LR)
        act_gla(act)
        act_mixer_out(act, 0, 4, U_GO, 3, lambda j: (gy_ready, j + 1), len(GLA_CUT_AT))
        act_root_fill(act, 3, 2, 5, U_PLE0)
        act_ple(act, 0, U_PLE0, 4, 1)
        act_fox_in(act)
        act_root_fill(act, 4, 3, 6, U_F)
        act_fox(act)
        act_mixer_out(act, 1, 7, U_FO, 5, lambda j: (fo_read, (j + 1) * NB), len(FOX_CUT_AT))
        act_root_fill(act, 5, 4, 8, U_PLE1)
        act_ple(act, 1, U_PLE1, 6, 2)
        act_root(act, 6)

    @block.vector
    def _(dve):
        dve_block1_in(dve)
        dve_swa(dve)
        dve_sgu(dve)
        dve_gating(dve)
        dve_merge(dve)
        dve_block1_out(dve)
        dve_norm_fill(dve, 2, 1, 3, lambda j: col("norm0", j))
        dve_gla(dve)
        dve_mixer_out(dve, 0, 4, U_GO, 1, len(GLA_CUT_AT))
        dve_norm_fill(dve, 3, 2, 5, lambda j: col("ple0", j))
        dve_ple(dve, 0, U_PLE0, 1)
        dve_norm_fill(dve, 4, 3, 6, lambda j: col("norm1", j))
        dve_fox(dve)
        dve_mixer_out(dve, 1, 7, U_FO, 2, len(FOX_CUT_AT))
        dve_norm_fill(dve, 5, 4, 8, lambda j: col("ple1", j))
        dve_ple(dve, 1, U_PLE1, 2)
        dve_final(dve, 6, 5)

    ctx.close()




def _tile(w):
    return w.reshape(KC, P, -1).transpose(1, 0, 2).reshape(P, -1)


def _weight_tiles(x):
    w_in, gla, fox = x["w_in"][0], x["gla_w_in_2"][0], x["fox_w_in_2"][0]
    a = SWA_HEADS * HD
    kv = SWA_KV * HD
    at = np.cumsum([0, a, kv, kv, a, HALF, HALF, HALF, 2 * D])
    half = SWA_HEADS // 2

    def paired(w):
        return w.reshape(-1, SWA_HEADS, HD)[:, [h for j in range(half) for h in (j, j + half)]].reshape(w.shape)

    def chunks(w):
        return [w[:, i:i + P] for i in range(0, w.shape[1], P)]

    def padded(w):
        return np.concatenate([w, np.zeros((D, P - w.shape[1]), np.float32)], 1)

    q, k, v, za, u, vb, zb, g = [w_in[:, at[i]:at[i + 1]] for i in range(8)]
    vb = chunks(vb)
    tiles = chunks(paired(q)) + [k, v] + chunks(g) + [vb[i] for i in (2, 3, 0, 1)]
    tiles += chunks(paired(za)) + chunks(u) + chunks(zb)
    pa = paired(x["w_proj_a"][0].T).T
    tiles += chunks(np.concatenate([pa, x["w_proj_b"][0]], 0)) + chunks(x["w_out"][0])
    kd, vd = D // 2, D
    tiles.append(padded(gla[:, 2 * kd + 2 * vd:]))
    for h in range(GLA_HEADS):
        tiles += [gla[:, h * P:(h + 1) * P], gla[:, kd + h * P:kd + (h + 1) * P]]
        for o in (2 * kd, 2 * kd + vd):
            two = chunks(gla[:, o + 2 * h * P:o + 2 * (h + 1) * P])
            tiles += two[::-1] if o == 2 * kd and h % 2 else two
    tiles += chunks(x["gla_w_out_2"][0]) + chunks(x["ple_gate_2"][0])
    tiles.append(padded(fox[:, 4 * D:]))
    for p in range(KC):
        tiles += [fox[:, o * D + p * P:o * D + (p + 1) * P] for o in range(4)]
    tiles += chunks(x["fox_w_out_2"][0]) + chunks(x["ple_gate_2"][1])
    assert len(tiles) == N_TILES
    return np.stack([_tile(t) for t in tiles])


def _columns(x):
    out = np.zeros((P, N_COLS), np.float32)

    def put(name, v, j=0):
        v = np.asarray(v, np.float32).reshape(-1, P).T
        out[:, COL[name][0] + j:COL[name][0] + j + v.shape[1]] = v

    for name, v in (("g_pre", x["g_pre"]), ("g_post", x["g_post"]), ("b_ada", x["b_ada"]), ("c", x["c"]),
                    ("norm0", x["norm_mixer_2"][0]), ("norm1", x["norm_mixer_2"][1]), ("ple0", x["ple_norm_2"][0]),
                    ("ple1", x["ple_norm_2"][1]), ("final", x["final_norm_2"]), ("o_gain", x["gla_o_norm_2"])):
        put(name, v)
    put("q_gain", np.tile(x["fox_q_norm_2"][0], 2))
    put("k_gain", np.tile(x["fox_k_norm_2"][0], 2))
    out[:FOX_HEADS, COL["b_f"][0]] = x["fox_b_f_2"][0]
    f = np.arange(P) % (HD // 2)
    put("inv_freq", np.float32(10000.0) ** (-(f.astype(np.float32)) / np.float32(HD // 2)))
    put("rope_sign", np.where(np.arange(P) % HD < HD // 2, 1.0, -1.0))
    put("eps", np.full(P, EPS))
    put("eps64", np.full(P, HD * EPS))
    r, h = np.arange(P)[:, None], np.arange(FOX_HEADS)[None, :]
    at, n = COL["selector"]
    out[:, at:at + n] = np.where((r == h) | (r == h + 32), -1.0, 0.0)
    put("half_pi", np.full(P, np.pi / 2))
    return out


def _matrices():
    r, c = np.arange(P)[:, None], np.arange(P)[None, :]
    same = r // GLA_CHUNK == c // GLA_CHUNK
    m = {
        "ident": r == c,
        "ones": np.ones((P, P)),
        "head_ones": r // HD == c // HD,
        "hide_all": np.full((P, P), NEG),
        "hide_prev": np.where(c > r, 0.0, NEG),
        "hide_cur": np.where(c <= r, 0.0, NEG),
        "chunk_sum": np.where((r <= c) & same, 1.0 / GLA_NORMALIZER, 0.0),
        "chunk_mask": (r <= c) & same,
        "causal_sum": r <= c,
        "causal_w": r <= c,
    }
    return np.stack([np.asarray(m[n], np.float32) for n in MAT], 1)


def kernel(**inputs):
    import concourse.bacc as bacc
    from concourse.bass_utils import run_bass_kernel_spmd

    x = {k: np.asarray(v) for k, v in inputs.items()}
    rows = np.concatenate([x["sinks"].ravel(), x["ln_v_g"].ravel(), x["ln_v_b"].ravel(), x["b_s"].ravel(),
                           x["gla_b_a_2"].ravel()])[None]
    arrays = {
        "xT": x["x"][0].T.reshape(KC, P, S),
        "pT": x["p_2"][:, 0].transpose(0, 2, 1).reshape(2, 2, P, S),
        "pos": x["positions"].astype(np.int32),
        "cols": _columns(x),
        "rows": rows,
        "mats": _matrices(),
        "w_ada": np.stack([x["w_ada"][0][:, i * D:(i + 1) * D].reshape(KC, P, D).transpose(1, 0, 2) for i in (1, 0, 2)]),
        "w_tiles": _weight_tiles(x),
        "ws_t": x["w_s"][0].transpose(2, 0, 1),
        "w_a2": x["gla_w_a2_2"][0],
        "ple_w": x["ple_proj_2"].reshape(2, 2, P, D),
    }
    arrays = {k: np.ascontiguousarray(v) for k, v in arrays.items()}
    nc = bacc.Bacc("TRN2", target_bir_lowering=False, num_devices=1)
    args = [nc.dram_tensor(k, v.shape, mybir.dt.from_np(v.dtype), kind="ExternalInput").ap() for k, v in arrays.items()]
    out = nc.dram_tensor("outT", (KC, P, S), F32, kind="ExternalOutput").ap()
    build(nc, *args, out)
    r = run_bass_kernel_spmd(nc, [arrays], core_ids=[0])
    return np.ascontiguousarray(r.results[0]["outT"].reshape(D, S).T)[None]
```

```python
from contextlib import ExitStack

import numpy as np

import concourse.bass as bass
from concourse import mybir

F32 = mybir.dt.float32
F32R = mybir.dt.float32r
I32 = mybir.dt.int32
ALU = mybir.AluOpType
ACT = mybir.ActivationFunctionType
AX = mybir.AxisListType

P = 128
D = 1024
S = 1024
KC = D // P
NB = S // P
HALF = 512
EPS = 1e-6
NEG = -1e30
SWA_HEADS, SWA_KV, HD = 8, 2, 64
GROUPS = 4
GLA_HEADS, GLA_CHUNK, GLA_RANK = 4, 64, 16
GLA_NORMALIZER = 16.0
FOX_HEADS = 16

T_Q, T_K, T_V, T_G, T_VB, T_ZA, T_U, T_ZB = 0, 4, 5, 6, 22, 26, 30, 34
T_PJ, T_WO, T_LR, T_GLA, T_GO, T_PLE0 = 38, 46, 54, 55, 79, 87
T_F, T_FOX, T_FO, T_PLE1, N_TILES = 95, 96, 128, 136, 144
RAW_SLOTS, W_SLOTS = 2, 4

U_Q, U_K, U_V, U_G, U_VB, U_ZA, U_U, U_ZB = 0, 4, 5, 6, 22, 26, 30, 34
U_PJ, U_WO, U_LR, U_GLA, U_GO, U_PLE0 = 38, 54, 62, 63, 95, 103
U_F, U_FOX, U_FO, U_PLE1, N_UNITS = 119, 120, 152, 160, 176
GLA_UNITS = 8

PE_NORM = 2
PE_CHUNKS = 4

_COLS = [("g_pre", 8), ("g_post", 8), ("b_ada", 24), ("c", 8), ("norm0", 8), ("norm1", 8), ("ple0", 8),
         ("ple1", 8), ("final", 8), ("o_gain", 2), ("q_gain", 1), ("k_gain", 1), ("b_f", 1),
         ("inv_freq", 1), ("rope_sign", 1), ("eps", 1), ("eps64", 1), ("selector", 16), ("half_pi", 1)]
COL = {}
_at = 0
for _name, _n in _COLS:
    COL[_name] = (_at, _n)
    _at += _n
N_COLS = _at
ROW = {"sinks": (0, 8), "ln_g": (8, 512), "ln_b": (520, 512), "b_s": (1032, 512), "b_a": (1544, 512)}
N_ROWS = 2056
MAT = {n: i for i, n in enumerate(["ident", "ones", "head_ones", "chunk_sum", "chunk_mask", "causal_sum",
                                   "hide_all", "hide_prev", "hide_cur", "causal_w"])}
N_MATS = len(MAT)


def build(nc, xT, pT, pos, cols, rows, mats, w_ada, w_tiles, ws_t, w_a2, ple_w, outT):
    ctx = ExitStack()
    base = (nc.sbuf_base + 31) // 32 * 32
    KB = 1024

    def sb(name, shape, at, dt=F32):
        return nc.alloc_sbuf_tensor_at(name, shape, dt, offset=base + int(at * KB))

    def sem(name):
        return ctx.enter_context(nc.semaphore(name))

    AH = sb("AH", [P, KC, S], 0, F32R)
    AL = sb("AL", [P, KC, S], 32, F32R)
    Y = sb("Y", [P, KC, S], 64)
    RAW = sb("RAW", [P, RAW_SLOTS, D], 96)
    WH = sb("WH", [P, W_SLOTS, D], 104, F32R)
    WL = sb("WL", [P, W_SLOTS, D], 120, F32R)
    CC = 136
    MATS = sb("MATS", [P, N_MATS, P], CC)
    CC += N_MATS * 0.5
    IDR = sb("IDR", [P, P], CC, F32R)
    HIDE = sb("HIDE", [P, 3, P], CC + 0.5, F32R)
    CC += 2
    COLS = sb("COLS", [P, N_COLS], CC)
    SINK = sb("SINK", [P, SWA_HEADS], CC + 0.46875)
    ADA = sb("ADA", [P, 24], CC + 0.5)
    GS = sb("GS", [P, KC], CC + 0.59375)
    GG = sb("GG", [P, KC], CC + 0.625)
    CACT = sb("CACT", [P, KC], CC + 0.65625)
    assert CC + 0.6875 <= 144 and N_COLS * 4 <= 480
    X = sb("X", [P, KC, S], 144)
    SQ = sb("SQ", [P, 2, S], 176)
    SQL = sb("SQL", [P, 2, S], 196)
    TN = sb("TN", [P, 2, S], 184)
    RS = sb("RS", [P, S], 192)
    SPARE = sb("SPARE", [P, 1], 206.25)
    RC = sb("RC", [P, NB], 206.5)
    ASUM = [sb("ASUM_SCALE", [P, D], 176), sb("ASUM_SHIFT", [P, D], 180), sb("ASUM_GATE", [P, D], 188)]
    COS = sb("COS", [P, S], 196)
    SIN = sb("SIN", [P, S], 200)
    POSI = sb("POSI", [P, S], 64, I32)
    ANG = sb("ANG", [P, S], 68)
    TURN = sb("TURN", [P, S], 72)
    RED = sb("RED", [P, S], 76)
    ABSR = sb("ABSR", [P, S], 80)
    WADA = [sb("WADA_SCALE", [P, KC, D], 0), sb("WADA_SHIFT", [P, KC, D], 32), sb("WADA_GATE", [P, KC, D], 64)]
    Q = sb("Q", [P, 4, S], 144)
    K = sb("K", [P, P + S], 160)
    KSH = sb("KSH", [P, 2, 2 * P], 164.5, F32R)
    KSL = sb("KSL", [P, 2, 2 * P], 166.5, F32R)
    V = sb("V", [P, 1 + NB, P], 169)
    M1 = sb("M1", [P, S], 176)
    M2 = sb("M2", [P, S], 180)
    QSH = sb("QSH", [P, 2, 4, P], 176, F32R)
    QSL = sb("QSL", [P, 2, 4, P], 180, F32R)
    VSH = sb("VSH", [P, 2, 2, P], 184, F32R)
    VSL = sb("VSL", [P, 2, 2, P], 186, F32R)
    PR = sb("PR", [P, 2, 4, 2 * P], 188)
    PTH = sb("PTH", [P, 2, 4 * P], 196, F32R)
    PTL = sb("PTL", [P, 2, 4 * P], 200, F32R)
    SIG = sb("SIG", [P, 2, S], 80)
    NMAX = sb("NMAX", [P, 2, 4], 204)
    NM = sb("NM", [P, 2, 4], 204.0625)
    DEN = sb("DEN", [P, 2, 4], 204.125)
    ESUM = sb("ESUM", [P, 2, 4], 204.1875)
    SDIF = sb("SDIF", [P, 2, 4], 204.25)
    DENS = sb("DENS", [P, 2, 4], 204.3125)
    RDEN = sb("RDEN", [P, 2, 4], 204.375)
    NSINK = sb("NSINK", [P, 8], 204.4375)
    GV = sb("GV", [P, NB, HALF], 144)
    LNT = sb("LNT", [P, 2, HALF], 160)
    VNH = sb("VNH", [P, 2, HALF], 164, F32R)
    VNL = sb("VNL", [P, 2, HALF], 168, F32R)
    WSF = sb("WSF", [P, GROUPS, P], 172)
    WSH = sb("WSH", [P, GROUPS, P], 176, F32R)
    WSL = sb("WSL", [P, GROUPS, P], 178, F32R)
    LNG = sb("LNG", [P, HALF], 180)
    LNB = sb("LNB", [P, HALF], 182)
    BSB = sb("BSB", [P, GROUPS, P], 184)
    BN6 = sb("BN6", [P, NB, 6], 204.5)
    MV = sb("MV", [P, NB, 2], 204.75)
    RSTD = sb("RSTD", [P, NB], 204.8125)
    GU = sb("GU", [P, 2, S], 188)
    GA = sb("GA", [P, 2, S], 144)
    GB = sb("GB", [P, 2, S], 152)
    MB = sb("MB", [P, 2, S], 160)

    gates = nc.dram_tensor("gates", [16, P, S], F32).ap()
    park = nc.dram_tensor("park", [P, KC, S], F32).ap()

    psG = ctx.enter_context(nc.psum_tensor("psG", [P, 4, HALF], F32))
    psA = ctx.enter_context(nc.psum_tensor("psA", [P, 4, HALF], F32))

    def unit(b):
        return psG[:, 2 * b:2 * b + 2, :].rearrange("p a f -> p (a f)")

    def pair(b):
        return psA[:, 2 * b:2 * b + 2, :].rearrange("p a f -> p (a f)")

    def mat(name):
        return MATS[:, MAT[name], :]

    def col(name, j=0):
        return COLS[:, COL[name][0] + j:COL[name][0] + j + 1]

    consts_loaded = sem("consts_loaded")
    x_part = [sem(f"x_part{i}") for i in range(4)]
    x_loaded = sem("x_loaded")
    pos_loaded = sem("pos_loaded")
    ada_loaded = [sem(f"ada_loaded{i}") for i in range(3)]
    raw_loaded = [sem(f"raw_loaded{i}") for i in range(RAW_SLOTS)]
    w_high = sem("w_high")
    w_split = sem("w_split")
    tile_begun = sem("tile_begun")
    psum_full = sem("psum_full")
    a_free = sem("a_free")
    psum_free = sem("psum_free")
    a_high = sem("a_high")
    a_ready = sem("a_ready")
    sq_ready = sem("sq_ready")
    sq_used = sem("sq_used")
    sum_full = sem("sum_full")
    rms_ready = sem("rms_ready")
    sq_late = sem("sq_late")
    sum_added = sem("sum_added")
    rc_ready = sem("rc_ready")
    rs_full = sem("rs_full")
    tn_ready = sem("tn_ready")
    dve_step = sem("dve_step")
    act_step = sem("act_step")
    r_ready = sem("r_ready")

    class Chain:

        def __init__(self, eng, s):
            self.eng, self.sem, self.base, self.it, self.per, self.loc = eng, s, 0, 0, 0, 0

        def link(self, ins):
            ins.then_inc(self.sem, 1)
            self.loc += 1
            self.eng.wait_ge(self.sem, self.it * self.per + (self.base + self.loc))

        def loop(self, it, per):
            self.base, self.loc, self.it, self.per = self.base + self.loc, 0, it, per

        def done(self, n):
            assert self.loc == self.per, (self.loc, self.per)
            self.base, self.loc, self.it, self.per = self.base + n * self.per, 0, 0, 0

    block = ctx.enter_context(nc.Block())

    cact_ready = sem("cact_ready")
    ada_sum = sem("ada_sum")
    ada_done = sem("ada_done")
    ada_ready = sem("ada_ready")
    rope_ready = sem("rope_ready")
    rope_angle = sem("rope_angle")
    v_turned = sem("v_turned")
    kv_ready = sem("kv_ready")
    qs_high = sem("qs_high")
    qs_ready = sem("qs_ready")
    s_full = sem("s_full")
    nm_ready = sem("nm_ready")
    exp_done = sem("exp_done")
    prob_ready = sem("prob_ready")
    t_full = sem("t_full")
    pt_high = sem("pt_high")
    pt_ready = sem("pt_ready")
    o_full = sem("o_full")
    o_read = sem("o_read")
    gate_stored = [sem(f"gate_stored{i}") for i in range(2)]
    sgu_loaded = sem("sgu_loaded")
    ws_masked = sem("ws_masked")
    ws_ready = sem("ws_ready")
    ws_high = sem("ws_high")
    ln_stats = sem("ln_stats")
    ln_root = sem("ln_root")
    vn_f32 = sem("vn_f32")
    vn_high = sem("vn_high")
    vn_ready = sem("vn_ready")
    sv_full = sem("sv_full")
    sv_read = sem("sv_read")
    act_out = sem("act_out")
    y_gated = sem("y_gated")
    gab_loaded = [sem(f"gab_loaded{i}") for i in range(2)]
    m_ready = sem("m_ready")
    x_upd = sem("x_upd")

    tile_waited = sem("tile_waited")

    def sp_inputs(sp):
        sp.dma_start(COLS[:, :], cols).then_inc(consts_loaded, 16)
        sp.dma_start(MATS[:, :, :], mats).then_inc(consts_loaded, 16)
        sp.dma_start(SINK[:, :], rows[:, 0:8].to_broadcast([P, 8])).then_inc(consts_loaded, 16)
        sp.dma_start(POSI[:, :], pos.to_broadcast([P, S])).then_inc(pos_loaded, 16)
        for i in range(4):
            sp.dma_start(X[:, 2 * i:2 * i + 2, :], xT[2 * i:2 * i + 2].rearrange("c p s -> p c s")).then_inc(x_part[i], 16)
        for i in range(2):
            sp.dma_start(WADA[i][:, :, :], w_ada[i]).then_inc(ada_loaded[i], 16)

    def sp_stream(sp):
        def load(t, i, first=False):
            if not first:
                sp.wait_ge(w_split, t - 1)
            sp.dma_start(RAW[:, i, :], w_tiles[t]).then_inc(raw_loaded[i], 16)

        load(0, 0, True)
        load(1, 1, True)
        with sp.Fori(1, N_TILES // RAW_SLOTS) as it:
            load(it * 2, 0)
            load(it * 2 + 1, 1)

    def pool_stream(pool):
        def cut(t, turn, i, first=False):
            pool.wait_ge(raw_loaded[i % RAW_SLOTS], turn * 32 + 16 * (i // RAW_SLOTS + 1))
            if not first:
                pool.wait_ge(tile_begun, t - 2)
            pool.sem_inc(tile_waited, 1)
            nc.gpsimd.tensor_scalar(WH[:, i, :], RAW[:, i % RAW_SLOTS, :], 1.0, 0.0, ALU.mult, ALU.add).then_inc(w_high, 1)
            pool.wait_ge(w_high, t + 1)
            nc.gpsimd.tensor_tensor(WL[:, i, :], RAW[:, i % RAW_SLOTS, :], WH[:, i, :].bitcast(F32), ALU.subtract).then_inc(w_split, 1)

        for i in range(W_SLOTS):
            cut(i, 0, i, True)
        with pool.Fori(1, N_TILES // W_SLOTS) as it:
            for i in range(W_SLOTS):
                cut(it * W_SLOTS + i, it, i)

    def three(out, wh, wl, xh, xl, start, stop):
        first = nc.tensor.matmul(out, wh, xh, start=start, stop=False)
        nc.tensor.matmul(out, wh, xl, start=False, stop=False)
        return first, nc.tensor.matmul(out, wl, xh, start=False, stop=stop)

    class Begin:

        def __init__(self, n):
            self.n = n

        def mark(self, ins):
            if self.n:
                ins.then_inc(tile_begun, 1)
                self.n -= 1

    def gemm(pe, t, u, slot, b, halves=(0, 1), kw=range(KC), ka=range(KC), begun=1, fill=None, free=True, release=False):
        if 0 in halves:
            pe.wait_ge(w_split, t + 1)
            if free:
                pe.wait_ge(psum_free, u - 1)
        mark = Begin(begun)

        def part(h, w, a, first, last):
            ws = slice(w * P, (w + 1) * P)
            xs = slice(h * HALF, (h + 1) * HALF)
            f, l = three(psG[:, 2 * b + h, :], WH[:, slot, ws], WL[:, slot, ws], AH[:, a, xs], AL[:, a, xs], first, last)
            mark.mark(f)
            return l

        kk = list(zip(kw, ka))
        if fill is None and not release:
            for h in halves:
                for n, (w, a) in enumerate(kk):
                    l = part(h, w, a, n == 0, n == len(kk) - 1)
        else:
            for n, (w, a) in enumerate(kk):
                if fill is not None:
                    pe.wait_ge(a_ready, KC * fill + a + 1)
                for h in halves:
                    l = part(h, w, a, n == 0, n == len(kk) - 1)
                if release and n < KC - 1:
                    l.then_inc(a_free, 1)
        if 1 in halves:
            l.then_inc(psum_full, 1)

    def gemm_slices(pe, t, u, slot, b, fill=None, begins=0, free=True):
        mark = Begin(1)
        order = [(h, c) for h in range(2) for c in range(KC)] if fill is None else [(h, c) for c in range(KC) for h in range(2)]

        def cut(h, c):
            if (h, c) == order[0]:
                pe.wait_ge(w_split, t + 1)
                if free:
                    pe.wait_ge(psum_free, u - 1)
            if fill is not None and h == 0:
                pe.wait_ge(a_ready, KC * fill + c + 1)
            ws, xs = slice(c * P, (c + 1) * P), slice(h * HALF, (h + 1) * HALF)
            f, l = three(psG[:, 2 * b + h, :], WH[:, slot, ws], WL[:, slot, ws], AH[:, c, xs], AL[:, c, xs], c == 0, c == KC - 1)
            if order.index((h, c)) >= begins:
                mark.mark(f)
            if (h, c) == order[-1]:
                l.then_inc(psum_full, 1)

        for h, c in order:
            yield lambda h=h, c=c: cut(h, c)

    LAG = 4

    def side_by_side(first, second, fill, free=True):
        one = list(gemm_slices(nc.tensor, *first, fill, 0, free))
        two = list(gemm_slices(nc.tensor, *second, fill, 2 * (KC - LAG), free))
        for n in range(KC + LAG):
            behind = n - LAG
            for cut in one[2 * n:2 * n + 2] + (two[2 * behind:2 * behind + 2] if behind >= 0 else []):
                cut()

    def sq_base(k):
        return (KC - 1) * k - (KC - 1 - PE_CHUNKS if k > PE_NORM else 0)

    def pe_sums(src, at):
        for n in range(NB):
            l = nc.tensor.matmul(psA[:, 2, at + n:at + n + 1], src[:, n * P:(n + 1) * P], mat("ones")[:, 0:1], start=True, stop=True)
        return l

    def pe_squares(pe):
        for j in range(PE_CHUNKS):
            pe.wait_ge(sq_ready, KC * PE_NORM + j + 1)
            pe_sums(SQ[:, j % 2, :], NB * j).then_inc(sq_used, 1)
        pe.wait_ge(sq_late, KC - 1 - PE_CHUNKS)
        pe_sums(RS, NB * PE_CHUNKS).then_inc(sum_full, 1)

    def pe_sum(pe, k):
        pe.wait_ge(sq_used, sq_base(k + 1))
        pe_sums(RS, 0).then_inc(sum_full, 1)

    def pe_recip(pe, k):
        pe.wait_ge(rc_ready, k + 1)
        for n in range(NB):
            l = nc.tensor.transpose(psA[:, n // 4, (n % 4) * P:(n % 4 + 1) * P], RC[:, n:n + 1].to_broadcast([P, P]), mat("ident"))
        l.then_inc(rs_full, 1)

    ADA_DIRECT = [2, 2, 0]

    def ada_out(i):
        return psA[:, 2 + i % 2, 0:KC], psA[:, 2 + i % 2, KC:2 * KC]

    def pe_ada_direct(pe, i):
        if i == 0:
            pe.wait_ge(rc_ready, 1)
        pe.wait_ge(ada_loaded[i], 16)
        for n in range(KC):
            for c in range(ADA_DIRECT[i]):
                nc.tensor.matmul(ada_out(i)[1][:, n:n + 1], WADA[i][:, c, n * P:(n + 1) * P], CACT[:, c:c + 1],
                                 start=(c == 0), stop=(c == ADA_DIRECT[i] - 1))

    def pe_ada(pe, i):
        pe.wait_ge(ada_sum, i + 1)
        if i == 2:
            pe.wait_ge(ada_ready, 1)
        for n in range(KC):
            l = nc.tensor.matmul(ada_out(i)[0][:, n:n + 1], ASUM[i][:, n * P:(n + 1) * P], mat("ones")[:, 0:1], start=True, stop=True)
        l.then_inc(ada_done, 1)

    def pe_block1_in(pe):
        pe.wait_ge(consts_loaded, 48)
        pe_sum(pe, 0)
        pe_recip(pe, 0)
        pe.wait_ge(cact_ready, 1)
        for i in range(2):
            pe_ada_direct(pe, i)
            pe_ada(pe, i)
        side_by_side(*((T_Q + j, U_Q + j, j, j) for j in range(2)), 0, free=False)
        for j in range(2, 4):
            gemm(pe, T_Q + j, U_Q + j, j, j % 2)
        gemm(pe, T_K, U_K, T_K % 4, U_K % 2)
        gemm(pe, T_V, U_V, T_V % 4, U_V % 2)
        pe_ada(pe, 2)
        pe.wait_ge(psum_free, U_V + 1)
        for n in range(NB):
            l = nc.tensor.transpose(psA[:, n // 4, (n % 4) * P:(n % 4 + 1) * P], M2[:, n * P:(n + 1) * P], mat("ident"))
        l.then_inc(v_turned, 1)

    def pe_swa(pe):
        def body(it, first, last=False):
            for i in range(4):
                u, n, r = it * 4 + i, it * 2 + i // 2, i % 2
                rows_ = slice(64 * r, 64 * r + 64)
                if r == 0:
                    pe.wait_ge(qs_ready, n + 1)
                if first and i == 0:
                    pe.wait_ge(kv_ready, 2)
                    pe.wait_ge(r_ready, 2)
                else:
                    pe.wait_ge(prob_ready, u)
                for bank in range(2):
                    hide = HIDE[:, 0:3:2, :] if first and i < 2 else HIDE[:, 1:3, :]
                    nc.tensor.matmul(psA[:, bank, :], IDR[:, :], hide.unsqueeze(1).to_broadcast([P, 2, 2, P]), start=True, stop=False)
                    for j in (2 * bank, 2 * bank + 1):
                        _, l = three(psA[:, bank, (j % 2) * 256:(j % 2 + 1) * 256], QSH[rows_, i // 2, j, :], QSL[rows_, i // 2, j, :],
                                     KSH[rows_, i // 2, :], KSL[rows_, i // 2, :], False, j % 2 == 1)
                l.then_inc(s_full, 1)
                gemm(pe, T_G + u, U_G + u, (T_G + i) % 4, i % 2, halves=(1,), begun=0)
                pe.wait_ge(prob_ready, u + 1)
                if not (first and i == 0):
                    pe.wait_ge(o_read, u)
                else:
                    pe.wait_ge(ada_ready, 3)
                for hf in range(2):
                    for j in range(4):
                        l = nc.tensor.transpose(psA[:, 2 + hf, j * P:(j + 1) * P], PR[:, i % 2, j, hf * P:(hf + 1) * P], mat("ident"))
                l.then_inc(t_full, 1)
                if not (last and i == 3):
                    gemm(pe, u + (T_G + 1), u + (U_G + 1), (T_G + i + 1) % 4, (i + 1) % 2, halves=(0,))
                pe.wait_ge(pt_ready, u + 1)
                for hf in range(2):
                    _, l = three(psA[:, 2, :], VSH[:, i // 2, hf, :], VSL[:, i // 2, hf, :], PTH[:, hf, :], PTL[:, hf, :], hf == 0, hf == 1)
                l.then_inc(o_full, 1)

        gemm(pe, T_G, U_G, T_G % 4, 0, halves=(0,))
        body(0, True)
        with pe.Fori(1, 3) as it:
            body(it, False)
        body(3, False, True)

    def pe_tokens(pe, t, u, tiles, begun, n_units, b0=None):
        width = len(tiles) * P
        lo, hi = min(tiles), max(tiles) + 1
        side = slice(lo, hi, (hi - lo - 1) // (len(tiles) - 1))
        b0 = u % 2 if b0 is None else b0
        per = HALF // width
        mark = Begin(begun)
        pe.wait_ge(w_split, t + len(tiles))
        for v in range(n_units):
            b = (b0 + v) % 2
            pe.wait_ge(psum_free, u + (v - 1))
            for h in range(2):
                for s in range(per):
                    n = (2 * v + h) * per + s
                    for c in range(KC):
                        blk, ws = slice(n * P, (n + 1) * P), slice(c * P, (c + 1) * P)
                        wh, wl = WH[:, side, ws], WL[:, side, ws]
                        f, l = three(psG[:, 2 * b + h, s * width:(s + 1) * width], AH[:, c, blk], AL[:, c, blk], wh, wl, c == 0, c == KC - 1)
                        mark.mark(f)
            l.then_inc(psum_full, 1)

    def pe_sgu(pe):
        pe.wait_ge(prob_ready, 16)
        nc.tensor.matmul(psA[:, 0, 0:1], mat("ident"), COLS[:, 0:1], start=True, stop=True).then_inc(tile_begun, 1)
        pe_tokens(pe, T_VB, U_VB, [2, 3, 0, 1], 0, 4)
        nc.tensor.matmul(psA[:, 0, 0:1], mat("ident"), COLS[:, 0:1], start=True, stop=True).then_inc(tile_begun, 3)
        for j in range(4):
            gemm(pe, T_ZA + j, U_ZA + j, (T_ZA + j) % 4, j % 2, begun=1)
            if j == 0:
                pe.wait_ge(ws_ready, 1)
            for n in (2 * j, 2 * j + 1):
                pe.wait_ge(vn_ready, n + 1)
                if n >= 2:
                    pe.wait_ge(sv_read, n - 1)
                for g in range(GROUPS):
                    gs = slice(g * P, (g + 1) * P)
                    _, l = three(psA[:, n % 2, gs], VNH[:, n % 2, gs], VNL[:, n % 2, gs], WSH[:, g, :], WSL[:, g, :], True, True)
                l.then_inc(sv_full, 1)

    def pe_gating(pe):
        for j in range(8):
            gemm(pe, T_U + j, U_U + j, (T_U + j) % 4, (U_U + j) % 2, release=j == 7)

    def act_replace(act, turn, j):
        if j < KC - 1:
            act.wait_ge(a_free, (KC - 1) * turn + j + 1)

    def pe_merge(pe):
        def tile(j, i, fill=None):
            gemm(pe, j + T_PJ, j * 2 + U_PJ, (T_PJ + i) % 4, 0, kw=range(4), ka=range(4), fill=fill)
            gemm(pe, j + T_PJ, j * 2 + (U_PJ + 1), (T_PJ + i) % 4, 1, kw=range(4, 8), ka=range(4, 8), begun=0, fill=fill)
        with pe.Fori(0, 2) as it:
            for i in range(4):
                tile(it * 4 + i, i, 1 if i == 0 else None)

    def pe_out(pe, t0, u0, fill, begun=0, release=False):
        for j in range(begun, KC):
            gemm(pe, t0 + j, u0 + j, (t0 + j) % 4, (u0 + j) % 2, fill=fill if j == 0 else None, release=release and j == KC - 1)

    def act_table(f):
        nc.scalar.activation(SPARE[:, :], mat("ones")[:, 0:1], f)

    def act_fill(act, f, src, ready, j, shift=None):
        act.wait_ge(ready[0], ready[1])
        if shift is None:
            nc.scalar.activation(AH[:, j, :], src, ACT.Copy).then_inc(a_high, 1)
        else:
            nc.scalar.activation(AH[:, j, :], src, ACT.Identity, bias=shift).then_inc(a_high, 1)

    def act_squares(act, k, j, src, ready):
        act.wait_ge(ready[0], ready[1])
        own = j == (PE_CHUNKS if k == PE_NORM else 0)
        late = j - PE_CHUNKS - 1 if k == PE_NORM else -1
        if own and k:
            act.wait_ge(sum_full, k)
        elif late >= 2:
            act.wait_ge(sq_late, late - 1)
        elif late < 0 and not own and (j >= 3 or k):
            act.wait_ge(sq_used, sq_base(k) + max(j - (1 if k == PE_NORM else 2), 0))
        dst = RS[:, :] if own else SQL[:, late % 2, :] if late >= 0 else SQ[:, j % 2, :]
        nc.scalar.activation(dst, src, ACT.Square).then_inc(sq_ready, 1)

    def act_root(act, k):
        if k == PE_NORM:
            act.wait_ge(sum_added, 1)
        else:
            act.wait_ge(sum_full, k + 1)
        sums = RC[:, :] if k == PE_NORM else psA[:, 2, 0:NB]
        nc.scalar.activation(RC[:, :], sums, ACT.Sqrt, bias=col("eps"), scale=1.0 / D).then_inc(rms_ready, 1)

    def act_norm_fill(act, k, n_fill, f, shift=None):
        for j in range(KC):
            act_fill(act, f, TN[:, j % 2, :], (tn_ready, KC * n_fill + j + 1), j, None if shift is None else shift(j))

    def act_block1_in(act):
        act.wait_ge(consts_loaded, 48)
        nc.scalar.activation(CACT[:, :], COLS[:, COL["c"][0]:COL["c"][0] + KC], ACT.Silu).then_inc(cact_ready, 1)
        nc.scalar.activation(IDR[:, :], mat("ident"), ACT.Copy).then_inc(r_ready, 1)
        nc.scalar.activation(HIDE[:, :, :], MATS[:, MAT["hide_all"]:MAT["hide_all"] + 3, :], ACT.Copy).then_inc(r_ready, 1)
        for j in range(KC):
            act_squares(act, 0, j, X[:, j, :], (x_part[j // 2], 16))
        act_root(act, 0)
        act.wait_ge(rope_angle, 1)
        nc.scalar.activation(ABSR[:, :], RED[:, :], ACT.Abs).then_inc(act_step, 1)
        act.wait_ge(act_step, 1)
        nc.scalar.activation(COS[:, :], ABSR[:, :], ACT.Sin, bias=col("half_pi"), scale=-1.0).then_inc(rope_ready, 1)
        nc.scalar.activation(SIN[:, :], RED[:, :], ACT.Sin, scale=col("rope_sign")).then_inc(rope_ready, 1)
        act.wait_ge(rope_ready, 2)
        act.dma_start(WADA[2][:, :, :], w_ada[2]).then_inc(ada_loaded[2], 16)
        act.wait_ge(ada_ready, 2)
        act_norm_fill(act, 0, 0, 0, lambda j: ADA[:, j:j + 1])
        act.wait_ge(psum_full, U_V + 1)
        act.wait_ge(kv_ready, 1)
        nc.scalar.activation(M2[:, :], unit(U_V % 2), ACT.Copy).then_inc(psum_free, 1)
        act.wait_ge(v_turned, 1)
        nc.scalar.activation(V[:, 1:, :], pair(0).rearrange("p (n f) -> p n f", n=NB), ACT.Copy).then_inc(kv_ready, 1)

    def act_swa(act):
        def cut(n, b):
            nc.scalar.activation(QSH[:, b, :, :], Q[:, :, bass.ds(n * P, P)], ACT.Copy)
            nc.scalar.activation(VSH[:, b, :, :], V[:, bass.ds(n, 2), :], ACT.Copy)
            nc.scalar.activation(KSH[:, b, :], K[:, bass.ds(n * P, 2 * P)], ACT.Copy).then_inc(qs_high, 1)

        def body(it, first, last=False):
            for i in range(4):
                u, n, r = it * 4 + i, it * 2 + i // 2, i % 2
                rows_ = slice(64 * r, 64 * r + 64)
                if first:
                    if i >= 2:
                        act.wait_ge(t_full, i - 1)
                else:
                    act.wait_ge(t_full, u - 1)
                act.wait_ge(nm_ready, u + 1)
                for j in range(4):
                    nc.scalar.activation(PR[:, i % 2, j, :], psA[:, j // 2, (j % 2) * 256:(j % 2 + 1) * 256], ACT.Exp,
                                         bias=NM[:, i % 2, j:j + 1], accum_out=DEN[:, i % 2, j:j + 1])
                nc.scalar.activation(ESUM[:, i % 2, :], SDIF[:, i % 2, :], ACT.Exp).then_inc(exp_done, 1)
                if r == 1 and not (last and i == 3):
                    if not (first and i == 1):
                        act.wait_ge(o_full, n * 2)
                    act.wait_ge(kv_ready, 2)
                    cut(n + 1, (i // 2 + 1) % 2)
                act.wait_ge(t_full, u + 1)
                if not (first and i == 0):
                    act.wait_ge(o_full, u)
                nc.scalar.activation(PTH[:, :, :].rearrange("p a f -> p (a f)"), pair(1), ACT.Copy).then_inc(pt_high, 1)
                if not (first and i < 2):
                    act.wait_ge(gate_stored[i % 2], (it * 2 + i // 2) * 16)
                if first and i == 0:
                    act.wait_ge(ada_ready, 3)
                act.wait_ge(psum_full, u + (U_G + 1))
                nc.scalar.activation(SIG[:, i % 2, :], unit(i % 2), ACT.Sigmoid).then_inc(psum_free, 1)
                act.wait_ge(psum_free, u + (U_G + 1))
                act.dma_start(gates[u], SIG[:, i % 2, :]).then_inc(gate_stored[i % 2], 16)
                act.wait_ge(o_full, u + 1)
                act.wait_ge(kv_ready, 2)
                nc.scalar.activation(Y[rows_, 0:4, bass.ds(n * P, P)], psA[rows_, 2, :].rearrange("p (j f) -> p j f", j=4),
                                     ACT.Copy).then_inc(o_read, 1)
                if not (last and i == 3):
                    act_table(ACT.Exp)

        act.wait_ge(kv_ready, 2)
        cut(0, 0)
        body(0, True)
        with act.Fori(1, 3) as it:
            body(it, False)
        body(3, False, True)

    def act_sgu(act):
        act.wait_ge(o_full, 16)
        act.wait_ge(prob_ready, 16)
        act.dma_start(WSF[:, :, :], ws_t).then_inc(sgu_loaded, 16)
        for name, dst in (("ln_g", LNG[:, :]), ("ln_b", LNB[:, :]), ("b_s", BSB[:, :, :].rearrange("p g f -> p (g f)"))):
            at, n = ROW[name]
            act.dma_start(dst, rows[:, at:at + n].to_broadcast([P, n])).then_inc(sgu_loaded, 16)
        for v in range(4):
            act.wait_ge(psum_full, U_VB + v + 1)
            nc.scalar.activation(GV[:, 2 * v:2 * v + 2, :].rearrange("p a f -> p (a f)"), unit((U_VB + v) % 2), ACT.Gelu).then_inc(psum_free, 1)
        act.wait_ge(ln_stats, 1)
        nc.scalar.activation(RSTD[:, :], MV[:, :, 1], ACT.Sqrt, bias=col("eps")).then_inc(ln_root, 1)
        act.wait_ge(ws_masked, 1)
        nc.scalar.activation(WSH[:, :, :], WSF[:, :, :], ACT.Copy).then_inc(ws_high, 1)
        for j in range(4):
            for n in (2 * j, 2 * j + 1):
                act.wait_ge(vn_f32, n + 1)
                if n >= 2:
                    act.wait_ge(sv_full, n - 1)
                nc.scalar.activation(VNH[:, n % 2, :], LNT[:, n % 2, :], ACT.Copy).then_inc(vn_high, 1)
            act_gate(act, j, ACT.Silu, U_ZA + j)

    def act_gate(act, g, func, u):
        if g >= 2:
            act.wait_ge(y_gated, g - 1)
        act.wait_ge(psum_full, u + 1)
        nc.scalar.activation(GU[:, g % 2, :], unit(u % 2), func).then_inc(psum_free, 1)

    def act_gating(act):
        for j in range(4):
            act_gate(act, 4 + j, ACT.Gelu, U_U + j)
        for j in range(4):
            if j == 3:
                for c in range(KC - 1):
                    act_replace(act, 0, c)
                    act_fill(act, 1, Y[:, c, :], (y_gated, c + 1 if c < 4 else c + 5), c)
            act_gate(act, 8 + j, ACT.Silu, U_ZB + j)

    def act_merge(act):
        def load(j, b):
            act.dma_start(GA[:, b, :], gates[j]).then_inc(gab_loaded[b], 16)
            act.dma_start(GB[:, b, :], gates[j + KC]).then_inc(gab_loaded[b], 16)
        for b in range(2):
            act.wait_ge(gate_stored[b], 128)
        act.wait_ge(sv_read, NB)
        load(0, 0)
        load(1, 1)
        act_fill(act, 1, Y[:, KC - 1, :], (y_gated, 12), KC - 1)
        with act.Fori(1, 4) as it:
            for b in range(2):
                act.wait_ge(m_ready, it * 2 + (b - 1))
                load(it * 2 + b, b)
        for j in range(KC):
            if j in (0, KC // 2):
                act.wait_ge(psum_full, U_WO - 1 + j // 4)
            act_fill(act, 2, Y[:, j, :], (m_ready, j + 1), j)

    def act_project(act, u0, k, f):
        for j in range(KC):
            act_squares(act, k, j, unit((u0 + j) % 2), (psum_full, u0 + j + 1))
            act.wait_ge(a_ready, KC * (f + 1))
            nc.scalar.activation(Y[:, j, :], unit((u0 + j) % 2), ACT.Copy).then_inc(psum_free, 1)
        act_root(act, k)

    def act_block1_out(act):
        act.wait_ge(m_ready, KC)
        act.dma_start(X[:, :, :], xT.rearrange("c p s -> p c s")).then_inc(x_loaded, 16)
        act_project(act, U_WO, 1, 2)

    chain = Chain(nc.vector, dve_step)
    link = chain.link

    def dve_rope_tables(dve):
        dve.wait_ge(consts_loaded, 48)
        link(nc.vector.tensor_scalar(NSINK[:, :], SINK[:, :], -1.0, None, ALU.mult))
        dve.wait_ge(pos_loaded, 16)
        link(nc.vector.tensor_copy(ANG[:, :], POSI[:, :]))
        link(nc.vector.tensor_scalar(ANG[:, :], ANG[:, :], col("inv_freq"), None, ALU.mult))
        magic = 1.5 * 2.0 ** 23
        link(nc.vector.tensor_scalar(TURN[:, :], ANG[:, :], 1.0 / (2 * np.pi), magic, ALU.mult, ALU.add))
        link(nc.vector.tensor_scalar(TURN[:, :], TURN[:, :], -magic, None, ALU.add))
        hi = 6.28125
        mid = float(np.floor((2 * np.pi - hi) * 2 ** 21) / 2 ** 21)
        lo = float(2 * np.pi - hi - mid)
        link(nc.vector.scalar_tensor_tensor(RED[:, :], TURN[:, :], -hi, ANG[:, :], ALU.mult, ALU.add))
        link(nc.vector.scalar_tensor_tensor(RED[:, :], TURN[:, :], -mid, RED[:, :], ALU.mult, ALU.add))
        link(nc.vector.scalar_tensor_tensor(RED[:, :], TURN[:, :], -lo, RED[:, :], ALU.mult, ALU.add))
        nc.vector.tensor_scalar(RED[:, :], RED[:, :], 3.1415925, -3.1415925, ALU.min, ALU.max).then_inc(rope_angle, 1)

    def dve_ada_sum(dve, i, chunks):
        for c in chunks:
            if c == ADA_DIRECT[i]:
                dve.wait_ge(cact_ready, 1)
                dve.wait_ge(ada_loaded[i], 16)
                l = nc.vector.tensor_scalar(ASUM[i][:, :], WADA[i][:, c, :], CACT[:, c:c + 1], None, ALU.mult)
            else:
                l = nc.vector.scalar_tensor_tensor(ASUM[i][:, :], WADA[i][:, c, :], CACT[:, c:c + 1], ASUM[i][:, :], ALU.mult, ALU.add)
            if c < KC - 1:
                link(l)
        if KC - 1 in chunks:
            l.then_inc(ada_sum, 1)

    def dve_ada(dve, i, at):
        dve.wait_ge(ada_done, i + 1)
        b0 = COL["b_ada"][0] + at
        summed, direct = ada_out(i)
        l = nc.vector.tensor_tensor(ADA[:, at:at + KC], summed, COLS[:, b0:b0 + KC], ALU.add)
        if ADA_DIRECT[i]:
            link(l)
            l = nc.vector.tensor_tensor(ADA[:, at:at + KC], direct, ADA[:, at:at + KC], ALU.add)
        return l

    def dve_low(f, j, src):
        nc.vector.wait_ge(a_high, KC * f + j + 1)
        nc.vector.tensor_tensor(AL[:, j, :], src, AH[:, j, :].bitcast(F32), ALU.subtract).then_inc(a_ready, 1)

    def dve_square(dve, k, j):
        dve.wait_ge(sq_ready, KC * k + j + 1)
        if j >= 2:
            dve.wait_ge(sq_used, sq_base(k) + j - 1)
        nc.vector.tensor_tensor(RS[:, :], RS[:, :], SQ[:, j % 2, :], ALU.add).then_inc(sq_used, 1)

    def dve_rs(dve, k):
        if k == PE_NORM:
            dve.wait_ge(sum_full, k + 1)
            nc.vector.tensor_reduce(RC[:, :], psA[:, 2, 0:(PE_CHUNKS + 1) * NB].rearrange("p (j n) -> p n j", n=NB), AX.X, ALU.add).then_inc(sum_added, 1)
        dve.wait_ge(rms_ready, k + 1)
        nc.vector.reciprocal(RC[:, :], RC[:, :]).then_inc(rc_ready, 1)

    def dve_norm_fill(dve, k, n_fill, f, gain, shift=None):
        if k:
            dve_rs(dve, k)
        dve.wait_ge(rs_full, k + 1)

        def low(j):
            nc.vector.wait_ge(a_high, KC * f + j + 1)
            if shift is None:
                nc.vector.tensor_tensor(AL[:, j, :], TN[:, j % 2, :], AH[:, j, :].bitcast(F32), ALU.subtract).then_inc(a_ready, 1)
            else:
                nc.vector.scalar_tensor_tensor(AL[:, j, :], TN[:, j % 2, :], shift(j), AH[:, j, :].bitcast(F32),
                                               ALU.add, ALU.subtract).then_inc(a_ready, 1)

        for j in range(KC):
            if j >= 2:
                dve.wait_ge(a_ready, KC * f + j - 1)
            nc.vector.scalar_tensor_tensor(TN[:, j % 2, :], X[:, j, :], gain(j), pair(0), ALU.mult, ALU.mult).then_inc(tn_ready, 1)
            if j:
                dve.wait_ge(tn_ready, KC * n_fill + j)
                low(j - 1)
        dve.wait_ge(tn_ready, KC * n_fill + KC)
        low(KC - 1)

    def dve_rotate(dve, u, scale, dst):
        dve.wait_ge(psum_full, u + 1)
        dve.wait_ge(rope_ready, 2)
        nc.vector.scalar_tensor_tensor(M1[:, :], unit(u % 2), scale, COS[:, :], ALU.mult, ALU.mult)
        for q in range(4):
            src, to = slice(32 * q, 32 * q + 32), slice(32 * (q ^ 1), 32 * (q ^ 1) + 32)
            l = nc.vector.scalar_tensor_tensor(M2[to, :], unit(u % 2)[src, :], scale, SIN[src, :], ALU.mult, ALU.mult)
        l.then_inc(psum_free, 1)
        dve.wait_ge(psum_free, u + 1)
        return nc.vector.tensor_tensor(dst, M1[:, :], M2[:, :], ALU.add)

    def dve_block1_in(dve):
        dve_rope_tables(dve)
        for j in range(1, KC):
            dve_square(dve, 0, j)
        dve_rs(dve, 0)
        for i in range(2):
            dve_ada_sum(dve, i, range(ADA_DIRECT[i], KC))
        link(dve_ada(dve, 0, 8))
        g0 = COL["g_pre"][0]
        nc.vector.scalar_tensor_tensor(GS[:, :], ADA[:, 8:16], 1.0, COLS[:, g0:g0 + KC], ALU.add, ALU.mult).then_inc(ada_ready, 1)
        dve_ada(dve, 1, 0).then_inc(ada_ready, 1)
        dve.wait_ge(ada_ready, 2)
        dve_norm_fill(dve, 0, 0, 0, lambda j: GS[:, j:j + 1], lambda j: ADA[:, j:j + 1])
        dve.wait_ge(a_ready, KC)
        dve.wait_ge(sq_used, KC - 1)
        nc.vector.memset(K[:, 0:P], 0.0)
        link(nc.vector.memset(V[:, 0, :], 0.0))
        share = [0, 0, 2, 4, 6, KC]
        for j in range(4):
            dve_ada_sum(dve, 2, range(share[j], share[j + 1]))
            link(dve_rotate(dve, U_Q + j, HD ** -0.5, Q[:, j, :]))
        dve_ada_sum(dve, 2, range(share[4], share[5]))
        dve_rotate(dve, U_K, 1.0, K[:, P:]).then_inc(kv_ready, 1)
        link(dve_ada(dve, 2, 16))
        g0 = COL["g_post"][0]
        nc.vector.tensor_tensor(GG[:, :], ADA[:, 16:24], COLS[:, g0:g0 + KC], ALU.mult).then_inc(ada_ready, 1)

    SWA_STEPS = 4

    def dve_swa(dve):
        def cut(n, b):
            dve.wait_ge(qs_high, n + 1)
            nc.vector.tensor_tensor(QSL[:, b, :, :], Q[:, :, bass.ds(n * P, P)], QSH[:, b, :, :].bitcast(F32), ALU.subtract)
            nc.vector.tensor_tensor(VSL[:, b, :, :], V[:, bass.ds(n, 2), :], VSH[:, b, :, :].bitcast(F32), ALU.subtract)
            nc.vector.tensor_tensor(KSL[:, b, :], K[:, bass.ds(n * P, 2 * P)], KSH[:, b, :].bitcast(F32),
                                    ALU.subtract).then_inc(qs_ready, 1)

        def body(it, last=False):
            for i in range(4):
                u, n, r = it * 4 + i, it * 2 + i // 2, i % 2
                b = i % 2
                dve.wait_ge(s_full, u + 1)
                link(nc.vector.tensor_reduce(NMAX[:, b, :], pair(0).rearrange("p (j k) -> p j k", j=4), AX.X, ALU.max, negate=True))
                link(nc.vector.tensor_tensor(NM[:, b, :], NMAX[:, b, :], NSINK[:, 4 * r:4 * r + 4], ALU.min))
                nc.vector.tensor_tensor(SDIF[:, b, :], NM[:, b, :], SINK[:, 4 * r:4 * r + 4], ALU.add).then_inc(nm_ready, 1)
                dve.wait_ge(exp_done, u + 1)
                link(nc.vector.tensor_tensor(DENS[:, b, :], DEN[:, b, :], ESUM[:, b, :], ALU.add))
                link(nc.vector.reciprocal(RDEN[:, b, :], DENS[:, b, :]))
                nc.vector.tensor_tensor(PR[:, b, :, :], PR[:, b, :, :], RDEN[:, b, :].unsqueeze(2).to_broadcast([P, 4, 2 * P]),
                                        ALU.mult).then_inc(prob_ready, 1)
                if r == 1 and not (last and i == 3):
                    cut(n + 1, (i // 2 + 1) % 2)
                dve.wait_ge(pt_high, u + 1)
                nc.vector.tensor_tensor(PTL[:, :, :].rearrange("p a f -> p (a f)"), pair(1),
                                        PTH[:, :, :].rearrange("p a f -> p (a f)").bitcast(F32), ALU.subtract).then_inc(pt_ready, 1)

        dve.wait_ge(kv_ready, 2)
        cut(0, 0)
        chain.loop(0, 4 * SWA_STEPS)
        body(0)
        chain.done(1)
        with dve.Fori(1, 3) as it:
            chain.loop(it - 1, 4 * SWA_STEPS)
            body(it)
        chain.done(2)
        chain.loop(0, 4 * SWA_STEPS)
        body(3, True)
        chain.done(1)

    def dve_gate(dve, g, y, u):
        dve.wait_ge(psum_free, u + 1)
        nc.vector.tensor_tensor(Y[:, y, :], Y[:, y, :], GU[:, g % 2, :], ALU.mult).then_inc(y_gated, 1)

    def dve_sgu(dve):
        dve.wait_ge(sgu_loaded, 64)
        nc.vector.tensor_tensor(WSF[:, :, :], WSF[:, :, :], mat("causal_w").unsqueeze(1).to_broadcast([P, GROUPS, P]),
                                ALU.mult).then_inc(ws_masked, 1)
        for v in range(4):
            dve.wait_ge(psum_free, U_VB + v + 1)
            for n in (2 * v, 2 * v + 1):
                link(nc.vector.bn_stats(BN6[:, n, :], GV[:, n, :]))
                l = nc.vector.bn_aggr(MV[:, n, :], BN6[:, n, :])
                if n < NB - 1:
                    link(l)
        l.then_inc(ln_stats, 1)
        dve.wait_ge(ws_high, 1)
        nc.vector.tensor_tensor(WSL[:, :, :], WSF[:, :, :], WSH[:, :, :].bitcast(F32), ALU.subtract).then_inc(ws_ready, 1)
        dve.wait_ge(ln_root, 1)
        link(nc.vector.reciprocal(RSTD[:, :], RSTD[:, :]))

        def normalise(n):
            t = LNT[:, n % 2, :]
            link(nc.vector.tensor_scalar(t, GV[:, n, :], MV[:, n, 0:1], RSTD[:, n:n + 1], ALU.subtract, ALU.mult))
            link(nc.vector.tensor_tensor(t, t, LNG[:, :], ALU.mult))
            nc.vector.tensor_tensor(t, t, LNB[:, :], ALU.add).then_inc(vn_f32, 1)
            dve.wait_ge(vn_high, n + 1)
            nc.vector.tensor_tensor(VNL[:, n % 2, :], t, VNH[:, n % 2, :].bitcast(F32), ALU.subtract).then_inc(vn_ready, 1)

        def read(n):
            dve.wait_ge(sv_full, n + 1)
            nc.vector.tensor_tensor(Y[:, 4:8, n * P:(n + 1) * P], psA[:, n % 2, :].rearrange("p (g f) -> p g f", g=GROUPS),
                                    BSB[:, :, :], ALU.add).then_inc(sv_read, 1)

        for j in range(4):
            normalise(2 * j)
            normalise(2 * j + 1)
            dve_gate(dve, j, j, U_ZA + j)
            read(2 * j)
            read(2 * j + 1)

    def dve_gating(dve):
        for j in range(4):
            if j == 0:
                dve.wait_ge(sv_read, NB)
            dve_gate(dve, 4 + j, 4 + j, U_U + j)
        for j in range(4):
            if j == 3:
                for c in range(KC - 1):
                    dve_low(1, c, Y[:, c, :])
            dve.wait_ge(y_gated, 5 + j)
            dve_gate(dve, 8 + j, 4 + j, U_ZB + j)

    def dve_merge(dve):
        dve.wait_ge(y_gated, 12)
        dve_low(1, KC - 1, Y[:, KC - 1, :])

        def merge(it, b, ahead=0):
            j = it * 2 + b
            dve.wait_ge(gab_loaded[b], it * 32 + 32)
            dve.wait_ge(psum_full, j * 2 + (U_PJ + 1))
            nc.vector.tensor_tensor(GA[:, b, :], unit(0), GA[:, b, :], ALU.mult).then_inc(psum_free, 1)
            for c in range(ahead):
                dve_low(2, c, Y[:, c, :])
            dve.wait_ge(psum_full, j * 2 + (U_PJ + 2))
            nc.vector.tensor_tensor(MB[:, b, :], unit(1), GB[:, b, :], ALU.mult).then_inc(psum_free, 1)
            dve.wait_ge(psum_free, j * 2 + (U_PJ + 2))
            nc.vector.tensor_tensor(Y[:, bass.ds(j, 1), :].rearrange("p a f -> p (a f)"), GA[:, b, :], MB[:, b, :],
                                    ALU.add).then_inc(m_ready, 1)

        with dve.Fori(0, 3) as it:
            for b in range(2):
                merge(it, b)
        merge(3, 0)
        merge(3, 1, KC // 2)
        for j in range(KC // 2, KC):
            dve_low(2, j, Y[:, j, :])

    def dve_block1_out(dve):
        def late(j):
            n = j - PE_CHUNKS - 1
            dve.wait_ge(sq_ready, KC * PE_NORM + j + 1)
            if n:
                dve.wait_ge(sq_late, n)
            nc.vector.tensor_tensor(RS[:, :], RS[:, :], SQL[:, n % 2, :], ALU.add).then_inc(sq_late, 1)

        for j in range(1, KC):
            dve_square(dve, 1, j)
        dve_rs(dve, 1)
        dve.wait_ge(rs_full, 2)
        dve.wait_ge(x_loaded, 16)
        for j in range(KC):
            if j >= 2:
                dve.wait_ge(x_upd, j - 1)
            link(nc.vector.scalar_tensor_tensor(TN[:, j % 2, :], Y[:, j, :], GG[:, j:j + 1], pair(0), ALU.mult, ALU.mult))
            nc.vector.tensor_tensor(X[:, j, :], X[:, j, :], TN[:, j % 2, :], ALU.add).then_inc(x_upd, 1)
            if j > PE_CHUNKS + 1:
                late(j - 1)
        late(KC - 1)

    DK, DV = P, 2 * P
    N_CH = S // GLA_CHUNK
    N_ST = N_CH - 1
    GRP = 2 * P
    QIH, QIL = sb("QIH", [P, S], 144, F32R), sb("QIL", [P, S], 148, F32R)
    KIH, KIL = sb("KIH", [P, S], 152, F32R), sb("KIL", [P, S], 156, F32R)
    GVH, GVL = sb("GVH", [P, NB, DV], 160, F32R), sb("GVL", [P, NB, DV], 168, F32R)
    KD = sb("KD", [P, S], 176)
    E = sb("E", [P, S], 180)
    EN = sb("EN", [P, S], 184)
    ED = sb("ED", [P, S], 188)
    LAH = sb("LAH", [P, NB, P], 192)
    EX = sb("EX", [P, S], 192)
    ALR = sb("ALR", [P, S], 200)
    WA2 = MATS[0:GLA_RANK + 1, 6:10, :].rearrange("p a f -> p (a f)")
    STF = sb("STF", [P, 2, DV], 204)
    LAST = sb("LAST", [P, N_CH], 206)
    STH, STL = sb("STH", [P, 2, DV], 176, F32R), sb("STL", [P, 2, DV], 178, F32R)
    KDTH, KDTL = sb("KDTH", [P, NB, DK], 184, F32R), sb("KDTL", [P, NB, DK], 188, F32R)
    ATF = sb("ATF", [P, S], 192)
    ATH, ATL = sb("ATH", [P, S], 196, F32R), sb("ATL", [P, S], 152, F32R)
    SQO = sb("SQO", [P, 2, HALF], 156)
    RSO = [sb("RSO", [P, S], 156)] * (GLA_HEADS - 1) + [sb("RSO_LAST", [P, S], 192)]
    PST = sb("PST", [P, 2, S], 196)
    PH, PL = sb("PH", [P, 2, S], 64, F32R), sb("PL", [P, 2, S], 72, F32R)
    PWH, PWL = sb("PWH", [P, 2, S], 80, F32R), sb("PWL", [P, 2, S], 88, F32R)
    RSB = sb("RSB", [P, S], 196)
    SG = sb("SG", [P, 2, S], 184)

    parked = sem("parked")
    x_early = sem("x_early")
    x_late = sem("x_late")
    wa_loaded = sem("wa_loaded")
    lr_ones = sem("lr_ones")
    la_log = sem("la_log")
    cum_full = sem("cum_full")
    e_ready = sem("e_ready")
    cd_ready = sem("cd_ready")
    ed_ready = sem("ed_ready")
    qh_ready = sem("qh_ready")
    kf_ready = sem("kf_ready")
    kh_ready = sem("kh_ready")
    qk_ready = sem("qk_ready")
    vh_ready = sem("vh_ready")
    kdt_full = sem("kdt_full")
    kdth_ready = sem("kdth_ready")
    kdt_ready = sem("kdt_ready")
    at_full = sem("at_full")
    atf_ready = sem("atf_ready")
    ath_ready = sem("ath_ready")
    at_ready = sem("at_ready")
    kv_full = sem("kv_full")
    st_upd = sem("st_upd")
    st_high = sem("st_high")
    st_ready = sem("st_ready")
    st_used = sem("st_used")
    og_read = sem("og_read")
    sqo_ready = sem("sqo_ready")
    sqo_used = sem("sqo_used")
    rso_half = sem("rso_half")
    gy_ready = sem("gy_ready")
    ple_loaded = sem("ple_loaded")
    ple_high = sem("ple_high")
    ple_ready = sem("ple_ready")
    rsb_ready = sem("rsb_ready")
    sg_ready = sem("sg_ready")

    achain = Chain(nc.scalar, act_step)
    achain.base = 1
    alink = achain.link

    def gla_units(h):
        first = U_GLA + GLA_UNITS * h
        names = ["k", "v0", "v1", "g0"] + (["next_la", "g1", "sums", "next_q"] if h < GLA_HEADS - 1 else ["g1", "sums"])
        u = {n: first + 2 + i for i, n in enumerate(names)}
        u["la"], u["q"] = (gla_units(h - 1)[n] for n in ("next_la", "next_q")) if h else (first, first + 1)
        return u

    GLA_FILL = [3, 3, 3, 3, 2, 2, 0, 0, 2, 2, 2, 1, 1, 1, 1, 1]
    GLA_BEGUN = 2
    GLA_CUT_AT = [6, 7, 8, 9, 10, 11]

    def pe_gla(pe):
        gemm(pe, T_LR, U_LR, T_LR % 4, U_LR % 2, fill=3)
        pe.wait_ge(wa_loaded, 32)
        pe.wait_ge(psum_free, U_LR + 1)
        pe_gla_logits(pe, 0)
        gemm(pe, T_GLA, gla_units(0)["q"], T_GLA % 4, gla_units(0)["q"] % 2)
        for h in range(GLA_HEADS):
            pe_gla_head(pe, h)

    def pe_gla_logits(pe, h):
        u = gla_units(h)["la"]
        pe.wait_ge(psum_free, u - 1)
        for n in range(NB):
            l = nc.tensor.matmul(psG[:, 2 * (u % 2) + n // 4, (n % 4) * P:(n % 4 + 1) * P], ALR[0:GLA_RANK + 1, n * P:(n + 1) * P],
                                 WA2[:, h * P:(h + 1) * P], start=True, stop=True)
        l.then_inc(psum_full, 1)

    def pe_gla_head(pe, h):
        u, t = gla_units(h), T_GLA + 6 * h
        more = h + 1 < GLA_HEADS
        pe.wait_ge(psum_free, u["la"] + 1)
        if h:
            pe.wait_ge(og_read, h * 4)
        for n in range(NB):
            l = nc.tensor.matmul(psA[:, 2 + n // 4, (n % 4) * P:(n % 4 + 1) * P], LAH[:, n, :], mat("chunk_sum"), start=True, stop=True)
        l.then_inc(cum_full, 1)
        gemm(pe, t + 1, u["k"], (t + 1) % 4, u["k"] % 2)
        pe_tokens(pe, t + 2, u["v0"], [(t + 2) % 4, (t + 3) % 4], 1, 2)
        pe.wait_ge(psum_free, u["k"] + 1)
        if h:
            pe.wait_ge(st_upd, h * N_ST)
        for n in range(NB):
            l = nc.tensor.transpose(psA[:, n // 4, (n % 4) * P:(n % 4 + 1) * P], KD[:, n * P:(n + 1) * P], mat("ident"))
        l.then_inc(kdt_full, 1)
        pe.wait_ge(qk_ready, h * 2 + 2)
        pe.wait_ge(cd_ready, h + 1)
        for n in range(NB):
            bs = slice(n * P, (n + 1) * P)
            _, l = three(psA[:, 2 + n // 4, (n % 4) * P:(n % 4 + 1) * P], KIH[:, bs], KIL[:, bs], QIH[:, bs], QIL[:, bs], True, True)
        l.then_inc(at_full, 1)
        gemm(pe, t + 4, u["g0"], (t + 4) % 4, u["g0"] % 2, begun=2)
        if more:
            pe_gla_logits(pe, h + 1)
        queue = list(gemm_slices(pe, t + 5, u["g1"], (t + 5) % 4, u["g1"] % 2))
        if more:
            queue += list(gemm_slices(pe, t + 6, u["next_q"], (t + 6) % 4, u["next_q"] % 2))
        else:
            n = 2 * len(GLA_CUT_AT)
            one, two = [list(gemm_slices(pe, T_GO + j, U_GO + j, (T_GO + j) % 4, (U_GO + j) % 2, 4, 14 * j)) for j in range(GLA_BEGUN)]
            queue += one[:n] + two[:n] + one[n:] + two[n:]

        def kv(c):
            if c >= 2:
                pe.wait_ge(st_upd, h * N_ST + (c - 1))
            n, r = c // 2, slice(64 * (c % 2), 64 * (c % 2) + 64)
            _, l = three(psA[:, c % 2, 0:DV], KDTH[r, n, :], KDTL[r, n, :], GVH[r, n, :], GVL[r, n, :], True, True)
            l.then_inc(kv_full, 1)

        def sums(g):
            pe.wait_ge(sqo_ready, h * 4 + (g + 1))
            if g == 0:
                pe.wait_ge(psum_free, u["sums"] - 1)
            for d in range(2):
                l = nc.tensor.matmul(psG[:, 2 * (u["sums"] % 2) + g // 2, (g % 2) * GRP:(g % 2 + 1) * GRP], mat("ones"),
                                     SQO[:, g % 2, d * GRP:(d + 1) * GRP], start=(d == 0), stop=(d == 1))
            l.then_inc(sqo_used if g < 3 else psum_full, 1)

        pe.wait_ge(kdt_ready, h + 1)
        pe.wait_ge(psum_free, u["v1"] + 1)
        for c in range(2):
            kv(c)
        pe.wait_ge(at_ready, h + 1)
        for c in range(N_CH):
            n, g = c // 2, c // 4
            bank = 2 + g % 2
            if c % 4 == 0 and g >= 2:
                pe.wait_ge(og_read, h * 4 + (g - 1))
            if c % 2 == 0:
                for d in range(2):
                    three(psA[:, bank, d * GRP + (n % 2) * P:d * GRP + (n % 2 + 1) * P], GVH[:, n, d * P:(d + 1) * P], GVL[:, n, d * P:(d + 1) * P],
                          ATH[:, n * P:(n + 1) * P], ATL[:, n * P:(n + 1) * P], c % 4 == 0 and d == 0, False)
            if c + 2 < N_ST:
                kv(c + 2)
            for _ in range(GLA_FILL[c]):
                if queue:
                    queue.pop(0)()
            if c:
                pe.wait_ge(st_ready, h * N_ST + c)
                cs = slice(c * GLA_CHUNK, (c + 1) * GLA_CHUNK)
                for d in range(2):
                    _, l = three(psA[:, bank, d * GRP + (c % 4) * GLA_CHUNK:d * GRP + (c % 4 + 1) * GLA_CHUNK],
                                 STH[:, (c - 1) % 2, d * P:(d + 1) * P], STL[:, (c - 1) % 2, d * P:(d + 1) * P], QIH[:, cs], QIL[:, cs],
                                 False, c % 4 == 3 and d == 1)
                l.then_inc(st_used, 1)
            if c == 8:
                sums(0)
                sums(1)
            elif c == 13:
                sums(2)
        sums(3)
        while queue:
            queue.pop(0)()

    def act_gla_in(act):
        act.wait_ge(x_upd, KC)
        act.dma_start(park, X[:, :, :]).then_inc(parked, 16)
        act.wait_ge(r_ready, 2)
        act.wait_ge(ws_masked, 1)
        act.dma_start(WA2[0:GLA_RANK, :], w_a2).then_inc(wa_loaded, 16)
        at, n = ROW["b_a"]
        act.dma_start(WA2[GLA_RANK:GLA_RANK + 1, :], rows[:, at:at + n]).then_inc(wa_loaded, 16)

    def act_gla(act):
        act.wait_ge(lr_ones, 1)
        act.wait_ge(psum_full, U_LR + 1)
        nc.scalar.activation(ALR[0:GLA_RANK, :], unit(U_LR % 2)[0:GLA_RANK, :], ACT.Copy).then_inc(psum_free, 1)
        act_gla_logits(act, 0)
        for h in range(GLA_HEADS):
            act_gla_head(act, h)

    def act_gla_logits(act, h, steps=(0, 1, 2)):
        if 0 in steps:
            act.wait_ge(psum_full, gla_units(h)["la"] + 1)
            alink(nc.scalar.activation(EX[:, :], unit(gla_units(h)["la"] % 2), ACT.Abs))
        if 1 in steps:
            alink(nc.scalar.activation(EX[:, :], EX[:, :], ACT.Exp, scale=-1.0))
        if 2 in steps:
            nc.scalar.activation(EX[:, :], EX[:, :], ACT.Ln, bias=mat("ones")[:, 0:1]).then_inc(la_log, 1)

    def act_gla_head(act, h):
        u = gla_units(h)
        more = h + 1 < GLA_HEADS

        def buf(x):
            return unit(u[x] % 2)

        act.wait_ge(cum_full, h + 1)
        nc.scalar.activation(E[:, :], pair(1), ACT.Exp)
        nc.scalar.activation(EN[:, :], pair(1), ACT.Exp, scale=-1.0).then_inc(e_ready, 1)
        act.wait_ge(cd_ready, h + 1)
        nc.scalar.activation(ED[:, :], ED[:, :], ACT.Exp).then_inc(ed_ready, 1)
        act.wait_ge(psum_free, u["q"] + 1)
        nc.scalar.activation(QIH[:, :], KD[:, :], ACT.Copy).then_inc(qh_ready, 1)
        act.wait_ge(kf_ready, h + 1)
        nc.scalar.activation(KIH[:, :], EN[:, :], ACT.Copy).then_inc(kh_ready, 1)
        for x in range(2):
            act.wait_ge(psum_full, u["v0"] + x + 1)
            nc.scalar.activation(GVH[:, 4 * x:4 * x + 4, :].rearrange("p n f -> p (n f)"), buf(f"v{x}"), ACT.Copy).then_inc(vh_ready, 1)
        act.wait_ge(kdt_full, h + 1)
        act.wait_ge(qk_ready, h * 2 + 2)
        nc.scalar.activation(KDTH[:, :, :].rearrange("p n f -> p (n f)"), pair(0), ACT.Copy).then_inc(kdth_ready, 1)
        act.wait_ge(atf_ready, h + 1)
        nc.scalar.activation(ATH[:, :], ATF[:, :], ACT.Copy).then_inc(ath_ready, 1)

        def gate(x):
            act.wait_ge(psum_full, u[f"g{x}"] + 1)
            act.wait_ge(psum_free, u[f"g{x}"])
            nc.scalar.activation(Y[:, 2 * h + x, :], buf(f"g{x}"), ACT.Silu).then_inc(psum_free, 1)

        def square(g):
            act.wait_ge(st_used, h * N_ST + (4 * g + 3))
            if g >= 2:
                act.wait_ge(sqo_used, h * 3 + (g - 1))
            nc.scalar.activation(SQO[:, g % 2, :], psA[:, 2 + g % 2, :], ACT.Square).then_inc(sqo_ready, 1)

        gate(0)
        for c in range(N_ST):
            act.wait_ge(st_upd, h * N_ST + (c + 1))
            if c >= 2:
                act.wait_ge(st_used, h * N_ST + (c - 1))
            nc.scalar.activation(STH[:, c % 2, :], STF[:, c % 2, :], ACT.Copy).then_inc(st_high, 1)
            if more and c < 3:
                if c == 0:
                    act.wait_ge(at_ready, h + 1)
                act_gla_logits(act, h + 1, (c,))
            if c == 5:
                gate(1)
            if c % 4 == 3:
                square(c // 4)
            if not more and c in GLA_CUT_AT:
                if c == GLA_CUT_AT[0]:
                    act.wait_ge(psum_full, u["g1"] + 1)
                act_fill(act, 4, Y[:, GLA_CUT_AT.index(c), :], (gy_ready, GLA_CUT_AT.index(c) + 1), GLA_CUT_AT.index(c))
        def root(ts):
            return nc.scalar.activation(RSO[h][:, ts], buf("sums")[:, ts], ACT.Sqrt, bias=col("eps"), scale=1.0 / DV)

        if not more:
            act.wait_ge(sqo_used, h * 3 + 2)
            root(slice(0, HALF)).then_inc(rso_half, 1)
        square(3)
        if not more:
            act_early(act, 0)
        act.wait_ge(psum_full, u["sums"] + 1)
        if more:
            act.wait_ge(og_read, h * 4 + 4)
        root(slice(0 if more else HALF, S)).then_inc(psum_free, 1)

    def dve_gla_in(dve):
        nc.vector.memset(ALR[0:GLA_RANK + 1, :], 1.0).then_inc(lr_ones, 1)

    def dve_gla(dve):
        dve.wait_ge(parked, 16)
        dve.wait_ge(a_ready, KC * 4)
        dve_gla_logits(dve, 0)
        for h in range(GLA_HEADS):
            dve_gla_head(dve, h)
        dve_gla_norm(dve, GLA_HEADS - 1)

    def dve_gla_logits(dve, h):
        u = gla_units(h)["la"]
        dve.wait_ge(la_log, h + 1)
        dve.wait_ge(psum_free, u)
        nc.vector.scalar_tensor_tensor(LAH[:, :, :].rearrange("p n f -> p (n f)"), unit(u % 2), 0.0, EX[:, :], ALU.min, ALU.subtract).then_inc(psum_free, 1)

    def dve_gla_norm(dve, h):
        dve.wait_ge(psum_free, gla_units(h)["sums"] + 1)
        ts = slice(0 if h < GLA_HEADS - 1 else HALF, S)
        link(nc.vector.reciprocal(RSO[h][:, ts], RSO[h][:, ts]))
        for x in range(2):
            y = Y[:, 2 * h + x, :]
            dve.wait_ge(og_read, h * 4 + 4)
            nc.vector.scalar_tensor_tensor(y, y, col("o_gain", x), RSO[h][:, :], ALU.mult, ALU.mult).then_inc(gy_ready, 1)

    def dve_gla_head(dve, h):
        u = gla_units(h)
        more = h + 1 < GLA_HEADS

        def buf(x):
            return unit(u[x] % 2)

        dve.wait_ge(e_ready, h + 1)
        cum = pair(1).rearrange("p (c t) -> p c t", t=GLA_CHUNK)
        link(nc.vector.tensor_scalar(LAST[:, :], cum[:, :, GLA_CHUNK - 1], 1.0, None, ALU.mult))
        nc.vector.tensor_tensor(ED[:, :].rearrange("p (c t) -> p c t", t=GLA_CHUNK), LAST[:, :].unsqueeze(2).to_broadcast([P, N_CH, GLA_CHUNK]),
                                cum, ALU.subtract).then_inc(cd_ready, 1)
        dve.wait_ge(psum_full, u["q"] + 1)
        nc.vector.scalar_tensor_tensor(KD[:, :], buf("q"), DK ** -0.5, E[:, :], ALU.mult, ALU.mult).then_inc(psum_free, 1)
        dve.wait_ge(qh_ready, h + 1)
        dve.wait_ge(psum_free, u["q"] + 1)
        nc.vector.tensor_tensor(QIL[:, :], KD[:, :], QIH[:, :].bitcast(F32), ALU.subtract).then_inc(qk_ready, 1)
        dve.wait_ge(psum_full, u["k"] + 1)
        nc.vector.tensor_tensor(EN[:, :], buf("k"), EN[:, :], ALU.mult).then_inc(kf_ready, 1)
        dve.wait_ge(ed_ready, h + 1)
        dve.wait_ge(qk_ready, h * 2 + 1)
        nc.vector.tensor_tensor(KD[:, :], buf("k"), ED[:, :], ALU.mult).then_inc(psum_free, 1)
        if h:
            dve_gla_norm(dve, h - 1)
            dve.wait_ge(gy_ready, 2 * h)
        dve.wait_ge(kh_ready, h + 1)
        nc.vector.tensor_tensor(KIL[:, :], EN[:, :], KIH[:, :].bitcast(F32), ALU.subtract).then_inc(qk_ready, 1)
        for x in range(2):
            dve.wait_ge(vh_ready, h * 2 + (x + 1))
            nc.vector.tensor_tensor(GVL[:, 4 * x:4 * x + 4, :].rearrange("p n f -> p (n f)"), buf(f"v{x}"),
                                    GVH[:, 4 * x:4 * x + 4, :].rearrange("p n f -> p (n f)").bitcast(F32), ALU.subtract).then_inc(psum_free, 1)
        dve.wait_ge(kdth_ready, h + 1)
        nc.vector.tensor_tensor(KDTL[:, :, :].rearrange("p n f -> p (n f)"), pair(0),
                                KDTH[:, :, :].rearrange("p n f -> p (n f)").bitcast(F32), ALU.subtract).then_inc(kdt_ready, 1)
        dve.wait_ge(at_full, h + 1)
        link(nc.vector.tensor_scalar(ATF[:, :], pair(1), 3e38, -3e38, ALU.min, ALU.max))
        nc.vector.tensor_tensor(ATF[:, :].rearrange("p (n f) -> p n f", f=P), ATF[:, :].rearrange("p (n f) -> p n f", f=P),
                                mat("chunk_mask").unsqueeze(1).to_broadcast([P, NB, P]), ALU.mult).then_inc(atf_ready, 1)
        dve.wait_ge(ath_ready, h + 1)
        nc.vector.tensor_tensor(ATL[:, :], ATF[:, :], ATH[:, :].bitcast(F32), ALU.subtract).then_inc(at_ready, 1)

        def update(c):
            dve.wait_ge(kv_full, h * N_ST + (c + 1))
            new = psA[:, c % 2, 0:DV]
            if c == 0:
                nc.vector.tensor_copy(STF[:, 0, :], new).then_inc(st_upd, 1)
                return
            dve.wait_ge(st_upd, h * N_ST + c)
            if c >= 2:
                dve.wait_ge(st_ready, h * N_ST + (c - 1))
            end = (c + 1) * GLA_CHUNK - 1
            nc.vector.scalar_tensor_tensor(STF[:, c % 2, :], STF[:, (c - 1) % 2, :], E[:, end:end + 1], new, ALU.mult, ALU.add).then_inc(st_upd, 1)

        def low(c):
            dve.wait_ge(st_high, h * N_ST + (c + 1))
            nc.vector.tensor_tensor(STL[:, c % 2, :], STF[:, c % 2, :], STH[:, c % 2, :].bitcast(F32), ALU.subtract).then_inc(st_ready, 1)

        def out(g):
            dve.wait_ge(psum_free, u["g1"] + 1)
            dve.wait_ge(sqo_ready, h * 4 + (g + 1))
            y = Y[:, 2 * h:2 * h + 2, g * GRP:(g + 1) * GRP]
            nc.vector.tensor_tensor(y, psA[:, 2 + g % 2, :].rearrange("p (d f) -> p d f", d=2), y, ALU.mult).then_inc(og_read, 1)

        update(0)
        for c in range(N_ST):
            if c + 1 < N_ST:
                update(c + 1)
            low(c)
            if more and c == 3:
                dve_gla_logits(dve, h + 1)
            if c in (6, 7, 11):
                out({6: 0, 7: 1, 11: 2}[c])
            if not more and c in GLA_CUT_AT:
                dve_low(4, GLA_CUT_AT.index(c), Y[:, GLA_CUT_AT.index(c), :])
        if not more:
            dve.wait_ge(rso_half, 1)
            link(nc.vector.reciprocal(RSO[h][:, 0:HALF], RSO[h][:, 0:HALF]))
        out(3)

    X_EARLY = [[slice(0, 3), slice(4, 8)], [slice(0, 4)]]
    X_LATE = [slice(3, 4), slice(4, 8)]

    def act_early(act, layer):
        for cs in X_EARLY[layer]:
            act.dma_start(X[:, cs, :], park[:, cs, :]).then_inc(x_early, 16)
        act.dma_start(PST[:, :, :], pT[layer].rearrange("c p s -> p c s")).then_inc(ple_loaded, 16)

    def act_mixer_out(act, layer, f, u0, k, y_ready, early):
        for j in range(early, KC):
            act_fill(act, f, Y[:, j, :], y_ready(j), j)
            if j == KC - 1:
                late = X_LATE[layer]
                act.dma_start(X[:, late, :], park[:, late, :]).then_inc(x_late, 16)
        for j in range(KC):
            if j == KC - 1:
                for c in range(SCALED_EARLY):
                    act_scaled(act, layer, f + 1, u0, c)
            act_squares(act, k, j, X[:, j, :], (psum_free, u0 + j + 1))
            if j in (0, 2):
                n = 2 * layer + j // 2
                act.wait_ge(ple_loaded, 16 * (n + 1))
                if j == 0:
                    act.wait_ge(a_ready, KC * (f + 1))
                dst = PWH if j else PH
                nc.scalar.activation(dst[:, :, :], PST[:, :, :], ACT.Copy).then_inc(ple_high, 1)
                if j == 0:
                    act.wait_ge(ple_ready, n + 1)
                    act.dma_start(PST[:, :, :], ple_w[layer].rearrange("c p n -> p c n")).then_inc(ple_loaded, 16)

        for j in range(SCALED_EARLY, KC):
            act_scaled(act, layer, f + 1, u0, j)
        act_root(act, k)
        act.wait_ge(rs_full, k + 1)
        act.wait_ge(ple_ready, 2 * layer + 2)
        nc.scalar.activation(RSB[:, :], pair(0), ACT.Copy).then_inc(rsb_ready, 1)

    SCALED_EARLY = 6

    def act_scaled(act, layer, f, u0, j):
        act.wait_ge(psum_free, u0 + j + 1)
        act_replace(act, layer + 1, j)
        nc.scalar.activation(AH[:, j, :], X[:, j, :], ACT.Copy, scale=col(f"ple{layer}", j)).then_inc(a_high, 1)

    def dve_scaled(dve, layer, f, j):
        dve.wait_ge(a_high, KC * f + j + 1)
        nc.vector.scalar_tensor_tensor(AL[:, j, :], X[:, j, :], col(f"ple{layer}", j), AH[:, j, :].bitcast(F32),
                                       ALU.mult, ALU.subtract).then_inc(a_ready, 1)

    def dve_mixer_out(dve, layer, f, u0, k, early):
        for j in range(early, KC):
            dve_low(f, j, Y[:, j, :])
        for j in range(KC):
            if j == X_LATE[layer].start:
                dve.wait_ge(x_late, 16 * (layer + 1))
            elif j == 0:
                dve.wait_ge(x_early, 16 * sum(len(e) for e in X_EARLY[:layer + 1]))
            if j == KC - 1:
                for c in range(SCALED_EARLY):
                    dve_scaled(dve, layer, f + 1, c)
            dve.wait_ge(psum_full, u0 + j + 1)
            nc.vector.tensor_tensor(X[:, j, :], X[:, j, :], unit((u0 + j) % 2), ALU.add).then_inc(psum_free, 1)
            if j >= 2:
                dve_square(dve, k, j - 1)
            if j in (0, 2):
                n = 2 * layer + j // 2
                high, low = (PWH, PWL) if j else (PH, PL)
                dve.wait_ge(ple_high, n + 1)
                nc.vector.tensor_tensor(low[:, :, :], PST[:, :, :], high[:, :, :].bitcast(F32), ALU.subtract).then_inc(ple_ready, 1)
        dve_square(dve, k, KC - 1)
        for j in range(SCALED_EARLY, KC):
            dve_scaled(dve, layer, f + 1, j)
        dve_rs(dve, k)

    def pe_ple(pe, layer, t0, u0, f, k):
        for j in range(KC):
            if j == 0:
                for n, cut in enumerate(gemm_slices(pe, t0, u0, t0 % 4, u0 % 2, f)):
                    if n == 2 * SCALED_EARLY:
                        pe_sum(pe, k)
                    cut()
                pe_recip(pe, k)
            else:
                gemm(pe, t0 + j, u0 + 2 * j, (t0 + j) % 4, u0 % 2)
            pe.wait_ge(ple_ready, 2 * layer + 2)
            b = (u0 + 1) % 2
            pe.wait_ge(psum_free, u0 + 2 * j)
            js = slice(j * P, (j + 1) * P)
            for h in range(2):
                hs = slice(h * HALF, (h + 1) * HALF)
                for c in range(2):
                    _, l = three(psG[:, 2 * b + h, :], PWH[:, c, js], PWL[:, c, js], PH[:, c, hs], PL[:, c, hs], c == 0, c == 1)
            l.then_inc(psum_full, 1)

    def act_ple(act, layer, u0, k, e):
        for j in range(KC):
            act.wait_ge(psum_free, u0 + 2 * j + 1)
            nc.scalar.activation(SG[:, j % 2, :], SG[:, j % 2, :], ACT.Sigmoid).then_inc(sg_ready, 1)
            act_squares(act, k, j, X[:, j, :], (x_upd, KC * e + j + 1))

    def dve_ple(dve, layer, u0, k, e):
        dve.wait_ge(rsb_ready, layer + 1)
        for j in range(KC):
            dve.wait_ge(psum_full, u0 + 2 * j + 1)
            if j >= 2:
                dve.wait_ge(x_upd, KC * e + j - 1)
            nc.vector.tensor_tensor(SG[:, j % 2, :], unit(u0 % 2), RSB[:, :], ALU.mult).then_inc(psum_free, 1)
            dve.wait_ge(sg_ready, KC * layer + j + 1)
            dve.wait_ge(psum_full, u0 + 2 * j + 2)
            nc.vector.tensor_tensor(SG[:, j % 2, :], unit((u0 + 1) % 2), SG[:, j % 2, :], ALU.mult).then_inc(psum_free, 1)
            dve.wait_ge(psum_free, u0 + 2 * j + 2)
            nc.vector.tensor_tensor(X[:, j, :], X[:, j, :], SG[:, j % 2, :], ALU.add).then_inc(x_upd, 1)
            if j >= 2:
                dve_square(dve, k, j - 1)
        dve_square(dve, k, KC - 1)

    def act_root_fill(act, k, n_fill, f, done):
        act_root(act, k)
        act.wait_ge(psum_full, done)
        act_norm_fill(act, k, n_fill, f)

    PAIRS = FOX_HEADS // 2
    FQH, FQL = sb("FQH", [P, S], 144, F32R), sb("FQL", [P, S], 148, F32R)
    FKH, FKL = sb("FKH", [P, S], 152, F32R), sb("FKL", [P, S], 156, F32R)
    FVH, FVL = sb("FVH", [P, NB, P], 160, F32R), sb("FVL", [P, NB, P], 164, F32R)
    FP = sb("FP", [P, 2, 2, S], 168)
    FTH, FTL = sb("FTH", [P, 2, HALF], 184, F32R), sb("FTL", [P, 2, HALF], 188, F32R)
    CALL = sb("CALL", [P, S], 192, F32R)
    LF = sb("LF", [P, S], 200)
    EXF = sb("EXF", [P, S], 196)
    FSQ = [sb("FSQ_Q", [P, S], 196), sb("FSQ_K", [P, S], 200)]
    FN = [Y[:, KC - 1, :], sb("FN_K", [P, S], 196)[:, :]]
    FREX = sb("FREX", [P, S], 200)
    VF = sb("VF", [P, S], 200)
    SELP = sb("SELP", [P, 2, P], 204, F32R)
    LFT = sb("LFT", [P, NB, FOX_HEADS], 205)
    FREC = sb("FREC", [P, 2, 2 * NB], 205.5)
    NMX, FDEN, FRD = sb("NMX", [P, 4], 206), sb("FDEN", [P, 4], 206.0625), sb("FRD", [P, 4], 206.125)

    PARTS = [(i + 2) // 2 for i in range(NB)]
    AT_PART = [sum(PARTS[:i]) for i in range(NB)]
    N_PARTS, N_S = sum(PARTS), 2 * NB
    FILL = [[3, 3, 5], [3, 4], [2, 2], [2, 4], [1, 3], [1, 0, 2], [2, 0, 2], [1, 2, 1, 1], [1, 1, 2]]

    FILL_LAST = [[2, 3, 4], [2, 5], [1, 2], [2, 2], [2, 2], [1, 1, 2], [1, 1, 2], [2, 1, 0, 1], [1, 2, 1, 1]]

    f_min = sem("f_min")
    f_log = sem("f_log")
    f_ready = sem("f_ready")
    f_turned = sem("f_turned")
    f_high = sem("f_high")
    fsq_ready = sem("fsq_ready")
    fsum_full = sem("fsum_full")
    froot_ready = sem("froot_ready")
    frec_ready = sem("frec_ready")
    fqk_high = sem("fqk_high")
    fqk_ready = sem("fqk_ready")
    fn_ready = sem("fn_ready")
    sel_ready = sem("sel_ready")
    fv_turned = sem("fv_turned")
    fv_high = sem("fv_high")
    fv_ready = sem("fv_ready")
    fs_full = sem("fs_full")
    fmax_ready = sem("fmax_ready")
    fexp_done = sem("fexp_done")
    frd_ready = sem("frd_ready")
    fp_ready = sem("fp_ready")
    ft_full = sem("ft_full")
    ft_high = sem("ft_high")
    ft_ready = sem("ft_ready")
    fpv_done = sem("fpv_done")
    fo_read = sem("fo_read")

    def scores(i, r):
        return psA[:, r, 0:(i + 1) * P] if i < 4 else pair(0)[:, 0:(i + 1) * P]

    def fox_buf(x):
        return unit((U_FOX + x) % 2)

    FOX_BEGUN = 2
    FOX_CUT_AT = [0, 1, 2, 3, 4, 5, 6]

    def fox_tile(p, x):
        return p * 4 + (T_FOX + x), p * 4 + (U_FOX + x), (T_FOX + x) % 4, (U_FOX + x) % 2

    def pe_fox_sums(pe, p, x):
        pe.wait_ge(fsq_ready, p * 2 + (x + 1))
        if x:
            pe.wait_ge(fn_ready, p * 2 + 1)
        for n in range(NB):
            l = nc.tensor.matmul(psA[:, 0, 2 * n:2 * n + 2], FSQ[x][:, n * P:(n + 1) * P], mat("head_ones")[:, 0:P:HD], start=True, stop=True)
        l.then_inc(fsum_full, 1)

    def pe_fox_spread(pe, p, x):
        pe.wait_ge(frec_ready, p * 4 + (2 * x + 2))
        for n in range(NB):
            l = nc.tensor.transpose(psA[:, n // 4, (n % 4) * P:(n % 4 + 1) * P], FREX[:, n * P:(n + 1) * P], mat("ident"))
        l.then_inc(fsum_full, 1)

    def pe_fox_v(pe, p):
        v = list(gemm_slices(pe, *fox_tile(p, 2)))
        for n, cut in enumerate(v):
            if n == 4:
                pe_fox_sums(pe, p, 1)
            if n == 10:
                pe_fox_spread(pe, p, 1)
            cut()

    def pe_fox_in(pe):
        side_by_side((T_F, U_F, T_F % 4, U_F % 2), fox_tile(0, 0), 6)
        gemm(pe, *fox_tile(0, 1))
        pe.wait_ge(f_ready, 1)
        for n in range(NB):
            l = nc.tensor.transpose(psA[:, 0, n * FOX_HEADS:(n + 1) * FOX_HEADS], LF[0:FOX_HEADS, n * P:(n + 1) * P],
                                    mat("ident")[0:FOX_HEADS, 0:FOX_HEADS])
        l.then_inc(f_turned, 1)
        pe.wait_ge(f_ready, 2)
        pe_fox_sums(pe, 0, 0)
        for n in range(NB):
            for m in range(n + 1):
                l = nc.tensor.matmul(psA[0:FOX_HEADS, 2 + n // 4, (n % 4) * P:(n % 4 + 1) * P], LFT[:, m, :],
                                     mat("causal_sum" if m == n else "ones"), start=(m == 0), stop=(m == n))
            if n == NB - 3:
                pe_fox_spread(pe, 0, 0)
        l.then_inc(f_turned, 1)
        pe_fox_v(pe, 0)

    def pe_fox_pair(pe, p, more):
        nxt = p + 1
        queue = list(gemm_slices(pe, *fox_tile(p, 3)))
        if more:
            queue += list(gemm_slices(pe, *fox_tile(nxt, 0))) + list(gemm_slices(pe, *fox_tile(nxt, 1)))
        else:
            one, two = [list(gemm_slices(pe, T_FO + j, U_FO + j, (T_FO + j) % 4, (U_FO + j) % 2, 7, 14 * j)) for j in range(FOX_BEGUN)]
            for c in range(0, 2 * KC, 2):
                queue += one[c:c + 2] + two[c:c + 2]

        plan = FILL if more else FILL_LAST

        def fill(place, n):
            for _ in range(plan[place][n] if n < len(plan[place]) else 0):
                if queue:
                    queue.pop(0)()

        def score(i, r):
            s = 2 * i + r
            if s == 0:
                pe.wait_ge(fqk_ready, p * 2 + 2)
                pe.wait_ge(sel_ready, p + 1)
                pe.wait_ge(f_ready, 4)
            elif i >= 4:
                pe.wait_ge(fexp_done, p * N_S + s)
            elif i:
                pe.wait_ge(fexp_done, p * N_S + (s - 1))
            hs = slice(64 * r, 64 * r + 64)
            out = scores(i, r)
            n = (i + 1) * P
            for at in range(0, n, HALF):
                ks = slice(at, min(at + HALF, n))
                last = ks.stop == n
                three(out[:, ks], FQH[hs, i * P:n], FQL[hs, i * P:n], FKH[hs, ks], FKL[hs, ks], True, False)
                l = nc.tensor.matmul(out[:, ks], SELP[:, r, :], CALL[:, ks], start=False, stop=not last)
                if last:
                    l = nc.tensor.matmul(out[:, i * P:n], IDR[:, :], HIDE[:, 2, :], start=False, stop=True)
            l.then_inc(fs_full, 1)

        def turn(i, x):
            g = AT_PART[i] + x
            if x == 0:
                pe.wait_ge(fp_ready, p * N_S + (2 * i + 2))
            if g == 0:
                pe.wait_ge(fv_ready, p + 1)
            else:
                pe.wait_ge(ft_ready, p * N_PARTS + g)
            for n in range(2 * x, min(2 * x + 2, i + 1)):
                for r in range(2):
                    at = (n % 2) * 2 * P + r * P
                    l = nc.tensor.transpose(psA[:, 2, at:at + P], FP[:, i % 2, r, n * P:(n + 1) * P], mat("ident"))
            l.then_inc(ft_full, 1)

        def weigh(i, x):
            g = AT_PART[i] + x
            pe.wait_ge(ft_ready, p * N_PARTS + (g + 1))
            if x == 0 and i:
                pe.wait_ge(fo_read, p * NB + i)
            for n in range(2 * x, min(2 * x + 2, i + 1)):
                ts = slice((n % 2) * 2 * P, (n % 2 + 1) * 2 * P)
                _, l = three(psA[:, 3, 0:2 * P], FVH[:, n, :], FVL[:, n, :], FTH[:, g % 2, ts], FTL[:, g % 2, ts], n == 0, n == i)
            l.then_inc(fpv_done, 1)

        def ahead(i, r):
            if i + 1 < NB:
                score(i + 1, r)
            elif more and r == 0:
                pe_fox_sums(pe, nxt, 0)
            elif more:
                pe_fox_spread(pe, nxt, 0)

        fill(0, 0)
        score(0, 0)
        score(0, 1)
        fill(0, 1)
        pe.wait_ge(psum_free, p * 4 + (U_FOX + 3))
        for n in range(NB):
            l = nc.tensor.transpose(psA[:, 2 + n // 4, (n % 4) * P:(n % 4 + 1) * P], VF[:, n * P:(n + 1) * P], mat("ident"))
        l.then_inc(fv_turned, 1)
        fill(0, 2)
        for i in range(NB):
            turn(i, 0)
            ahead(i, 0)
            fill(i + 1, 0)
            for x in range(PARTS[i]):
                if x + 1 < PARTS[i]:
                    turn(i, x + 1)
                weigh(i, x)
                if x == 0:
                    ahead(i, 1)
                fill(i + 1, x + 1)
        while queue:
            queue.pop(0)()
        if more:
            pe_fox_v(pe, nxt)

    def pe_fox(pe):
        pe_fox_in(pe)
        with pe.Fori(0, PAIRS - 1) as p:
            pe_fox_pair(pe, p, True)
        pe_fox_pair(pe, PAIRS - 1, False)

    def act_fox_square(act, p, x):
        act.wait_ge(psum_full, p * 4 + (U_FOX + x + 1))
        nc.scalar.activation(FSQ[x][:, :], fox_buf(x), ACT.Square).then_inc(fsq_ready, 1)

    def act_fox_root(act, p, x):
        act.wait_ge(fsum_full, p * 4 + (2 * x + 1))
        nc.scalar.activation(FREC[:, x, :], psA[:, 0, 0:2 * NB], ACT.Sqrt, bias=col("eps64")).then_inc(froot_ready, 1)

    def act_fox_spread(act, p, x):
        act.wait_ge(fsum_full, p * 4 + (2 * x + 2))
        nc.scalar.activation(FN[x], pair(0), ACT.Copy).then_inc(fn_ready, 1)

    def act_fox_high(act, p, x):
        act.wait_ge(psum_free, p * 4 + (U_FOX + x + 1))
        nc.scalar.activation((FKH if x else FQH)[:, :], FN[x], ACT.Copy, scale=8.0 if x else 1.0).then_inc(fqk_high, 1)

    def act_fox_kv(act, p):
        act_fox_square(act, p, 1)
        act_fox_high(act, p, 0)
        act_fox_root(act, p, 1)
        act_fox_spread(act, p, 1)
        for r in range(2):
            l = nc.scalar.activation(SELP[:, r, :], COLS[:, bass.ds(p * 2 + (r + COL["selector"][0]), 1)].to_broadcast([P, P]), ACT.Copy)
        l.then_inc(sel_ready, 1)
        act_fox_high(act, p, 1)
        act.wait_ge(psum_full, p * 4 + (U_FOX + 3))
        nc.scalar.activation(VF[:, :], fox_buf(2), ACT.Copy).then_inc(psum_free, 1)

    def act_fox_in(act):
        act.wait_ge(x_upd, KC * 2)
        act.dma_start(park, X[:, :, :]).then_inc(parked, 16)

    def act_fox_gates(act):
        act.wait_ge(parked, 32)
        fs = slice(0, FOX_HEADS)
        act.wait_ge(f_min, 1)
        nc.scalar.activation(EXF[fs, :], unit(U_F % 2)[fs, :], ACT.Abs, bias=col("b_f")[fs, :]).then_inc(psum_free, 1)
        act.wait_ge(psum_free, U_F + 1)
        alink(nc.scalar.activation(EXF[fs, :], EXF[fs, :], ACT.Exp, scale=-1.0))
        nc.scalar.activation(EXF[fs, :], EXF[fs, :], ACT.Ln, bias=mat("ones")[fs, 0:1]).then_inc(f_log, 1)
        act.wait_ge(f_ready, 1)
        act_fox_square(act, 0, 0)
        act_fox_root(act, 0, 0)
        act_fox_spread(act, 0, 0)
        act.wait_ge(f_turned, 2)
        act.wait_ge(f_ready, 3)
        nc.scalar.activation(CALL[fs, :], pair(1)[fs, :], ACT.Copy).then_inc(f_high, 1)
        act_fox_kv(act, 0)

    def act_fox_pair(act, p, more):
        u, nxt = p * 4 + U_FOX, p + 1

        def exp(i, r):
            s = 2 * i + r
            act.wait_ge(fmax_ready, p * N_S + (s + 1))
            nc.scalar.activation(FP[:, i % 2, r, 0:(i + 1) * P], scores(i, r), ACT.Exp, bias=NMX[:, s % 4:s % 4 + 1],
                                 accum_out=FDEN[:, s % 4:s % 4 + 1]).then_inc(fexp_done, 1)

        def high(i, x):
            g = AT_PART[i] + x
            w = (min(2 * x + 2, i + 1) - 2 * x) * 2 * P
            act.wait_ge(ft_full, p * N_PARTS + (g + 1))
            if g >= 2:
                act.wait_ge(fpv_done, p * N_PARTS + (g - 1))
            nc.scalar.activation(FTH[:, g % 2, 0:w], psA[:, 2, 0:w], ACT.Copy).then_inc(ft_high, 1)

        def ahead(i, r):
            if i + 1 < NB:
                exp(i + 1, r)
            elif more and r == 0:
                act_fox_root(act, nxt, 0)
            elif more:
                act_fox_spread(act, nxt, 0)

        def gate():
            act.wait_ge(psum_full, u + 4)
            act.wait_ge(fv_ready, 1)
            nc.scalar.activation(Y[:, bass.ds(p, 1), :].rearrange("p a f -> p (a f)"), fox_buf(3), ACT.Silu).then_inc(psum_free, 1)

        exp(0, 0)
        exp(0, 1)
        act.wait_ge(fv_turned, p + 1)
        nc.scalar.activation(FVH[:, :, :].rearrange("p n f -> p (n f)"), pair(1), ACT.Copy).then_inc(fv_high, 1)
        for i in range(NB):
            if not more and i == NB - 1:
                act.wait_ge(fs_full, PAIRS * N_S)
                act_early(act, 1)
            high(i, 0)
            ahead(i, 0)
            for x in range(1, PARTS[i]):
                high(i, x)
                if x == (2 if PARTS[i] == 3 else 1):
                    ahead(i, 1)
            if PARTS[i] == 1:
                ahead(i, 1)
            if i == GATE_AT:
                gate()
            if not more and i in FOX_CUT_AT:
                if i == FOX_CUT_AT[0]:
                    act.wait_ge(psum_full, U_FO)
                j = FOX_CUT_AT.index(i)
                act_fill(act, 7, Y[:, j, :], (fo_read, (j + 1) * NB), j)
            if more and i == SQUARE_AT:
                act_fox_square(act, nxt, 0)
        if more:
            act_fox_kv(act, nxt)

    def filled(n):
        done = np.cumsum([sum(f) for f in FILL])
        return int(np.argmax(done >= n)) - 1 if (done >= n).any() else NB - 1

    GATE_AT = filled(16)
    SQUARE_AT = filled(32)

    def act_fox(act):
        act_fox_gates(act)
        with act.Fori(0, PAIRS - 1) as p:
            act_fox_pair(act, p, True)
        act_fox_pair(act, PAIRS - 1, False)

    def dve_fox_rec(dve, p, x):
        dve.wait_ge(froot_ready, p * 2 + (x + 1))
        nc.vector.reciprocal(FREC[:, x, :], FREC[:, x, :]).then_inc(frec_ready, 1)
        dve.wait_ge(frec_ready, p * 4 + (2 * x + 1))
        nc.vector.tensor_copy(FREX[:, :].rearrange("p (n f) -> p n f", f=HD), FREC[:, x, :].unsqueeze(2).to_broadcast([P, 2 * NB, HD])).then_inc(frec_ready, 1)

    def dve_fox_norm(dve, p, x):
        dve.wait_ge(fn_ready, p * 2 + (x + 1))
        nc.vector.scalar_tensor_tensor(FN[x], fox_buf(x), col("k_gain" if x else "q_gain"), FN[x], ALU.mult, ALU.mult).then_inc(psum_free, 1)

    def dve_fox_k(dve, p):
        dve.wait_ge(fqk_high, p * 2 + 1)
        nc.vector.tensor_tensor(FQL[:, :], FN[0], FQH[:, :].bitcast(F32), ALU.subtract).then_inc(fqk_ready, 1)
        dve_fox_rec(dve, p, 1)
        dve_fox_norm(dve, p, 1)
        dve.wait_ge(fqk_high, p * 2 + 2)
        nc.vector.scalar_tensor_tensor(FKL[:, :], FN[1], 8.0, FKH[:, :].bitcast(F32), ALU.mult, ALU.subtract).then_inc(fqk_ready, 1)

    def dve_fox_gates(dve):
        fs = slice(0, FOX_HEADS)
        dve.wait_ge(psum_full, U_F + 1)
        nc.vector.tensor_scalar(LF[fs, :], unit(U_F % 2)[fs, :], col("b_f")[fs, :], 0.0, ALU.add, ALU.min).then_inc(f_min, 1)
        dve.wait_ge(f_min, 1)
        dve.wait_ge(f_log, 1)
        nc.vector.tensor_tensor(LF[fs, :], LF[fs, :], EXF[fs, :], ALU.subtract).then_inc(f_ready, 1)
        dve.wait_ge(f_turned, 1)
        nc.vector.tensor_copy(LFT[:, :, :].rearrange("p n h -> p (n h)"), psA[:, 0, 0:NB * FOX_HEADS]).then_inc(f_ready, 1)
        nc.vector.memset(CALL[:, :].bitcast(F32), 0.0).then_inc(f_ready, 1)
        dve_fox_rec(dve, 0, 0)
        dve_fox_norm(dve, 0, 0)
        dve.wait_ge(f_high, 1)
        nc.vector.tensor_tensor(CALL[32:32 + FOX_HEADS, :], pair(1)[fs, :], CALL[fs, :].bitcast(F32), ALU.subtract).then_inc(f_ready, 1)
        dve_fox_k(dve, 0)

    def dve_fox_pair(dve, p, more):
        u, nxt = p * 4 + U_FOX, p + 1

        def peak(i, r):
            s = 2 * i + r
            dve.wait_ge(fs_full, p * N_S + (s + 1))
            nc.vector.tensor_reduce(NMX[:, s % 4:s % 4 + 1], scores(i, r), AX.X, ALU.max, negate=True).then_inc(fmax_ready, 1)

        def divide(i, r):
            s = 2 * i + r
            dve.wait_ge(fexp_done, p * N_S + (s + 1))
            nc.vector.reciprocal(FRD[:, s % 4:s % 4 + 1], FDEN[:, s % 4:s % 4 + 1]).then_inc(frd_ready, 1)
            dve.wait_ge(frd_ready, p * N_S + (s + 1))
            probs = FP[:, i % 2, r, 0:(i + 1) * P]
            nc.vector.tensor_scalar(probs, probs, FRD[:, s % 4:s % 4 + 1], None, ALU.mult).then_inc(fp_ready, 1)

        def low(i, x):
            g = AT_PART[i] + x
            w = (min(2 * x + 2, i + 1) - 2 * x) * 2 * P
            dve.wait_ge(ft_high, p * N_PARTS + (g + 1))
            nc.vector.tensor_tensor(FTL[:, g % 2, 0:w], psA[:, 2, 0:w], FTH[:, g % 2, 0:w].bitcast(F32), ALU.subtract).then_inc(ft_ready, 1)

        def out(i):
            dve.wait_ge(fpv_done, p * N_PARTS + (AT_PART[i] + PARTS[i]))
            if i == 0:
                dve.wait_ge(psum_free, u + 4)
            for r in range(2):
                hs = slice(64 * r, 64 * r + 64)
                y = Y[hs, bass.ds(p, 1), i * P:(i + 1) * P].rearrange("p a f -> p (a f)")
                l = nc.vector.tensor_tensor(y, psA[hs, 3, r * P:(r + 1) * P], y, ALU.mult)
            l.then_inc(fo_read, 1)

        peak(0, 0)
        peak(0, 1)
        divide(0, 0)
        divide(0, 1)
        dve.wait_ge(fv_high, p + 1)
        nc.vector.tensor_tensor(FVL[:, :, :].rearrange("p n f -> p (n f)"), pair(1), FVH[:, :, :].rearrange("p n f -> p (n f)").bitcast(F32),
                                ALU.subtract).then_inc(fv_ready, 1)
        for i in range(NB):
            more_blocks = i + 1 < NB
            low(i, 0)
            if more_blocks:
                peak(i + 1, 0)
            elif more:
                dve_fox_rec(dve, nxt, 0)
            if PARTS[i] > 1:
                low(i, 1)
            elif i:
                out(i)
            if more_blocks:
                peak(i + 1, 1)
                divide(i + 1, 0)
            elif more:
                dve_fox_norm(dve, nxt, 0)
            if PARTS[i] > 2:
                low(i, 2)
            if more_blocks:
                divide(i + 1, 1)
            if PARTS[i] > 3:
                low(i, 3)
            if PARTS[i] > 1 or i == 0:
                out(i)
            if not more and i in FOX_CUT_AT:
                dve_low(7, FOX_CUT_AT.index(i), Y[:, FOX_CUT_AT.index(i), :])
        if more:
            dve_fox_k(dve, nxt)

    def dve_fox(dve):
        dve.wait_ge(parked, 32)
        dve_fox_gates(dve)
        with dve.Fori(0, PAIRS - 1) as p:
            dve_fox_pair(dve, p, True)
        dve_fox_pair(dve, PAIRS - 1, False)

    def dve_final(dve, k):
        dve_rs(dve, k)
        dve.wait_ge(rs_full, k + 1)
        for j in range(KC):
            nc.vector.scalar_tensor_tensor(X[:, j, :], X[:, j, :], col("final", j), pair(0), ALU.mult, ALU.mult).then_inc(x_final, 1)

    def sp_out(sp):
        for j in range(KC):
            sp.wait_ge(x_final, j + 1)
            sp.dma_start(outT[j], X[:, j, :]).then_inc(out_stored, 16)
        sp.wait_ge(out_stored, 16 * KC)

    x_final = sem("x_final")
    out_stored = sem("out_stored")

    @block.sync
    def _(sp):
        sp_inputs(sp)
        sp_stream(sp)
        sp_out(sp)

    @block.gpsimd
    def _(pool):
        pool_stream(pool)

    @block.tensor
    def _(pe):
        pe_block1_in(pe)
        pe_swa(pe)
        pe_sgu(pe)
        pe_gating(pe)
        pe_merge(pe)
        pe_out(pe, T_WO, U_WO, 2)
        pe_sum(pe, 1)
        pe_recip(pe, 1)
        pe_squares(pe)
        pe_recip(pe, 2)
        pe_gla(pe)
        pe_out(pe, T_GO, U_GO, 4, GLA_BEGUN, True)
        pe_ple(pe, 0, T_PLE0, U_PLE0, 5, 3)
        pe_sum(pe, 4)
        pe_recip(pe, 4)
        pe_fox(pe)
        pe_out(pe, T_FO, U_FO, 7, FOX_BEGUN, True)
        pe_ple(pe, 1, T_PLE1, U_PLE1, 8, 5)
        pe_sum(pe, 6)
        pe_recip(pe, 6)

    @block.scalar
    def _(act):
        act_block1_in(act)
        act_swa(act)
        act_sgu(act)
        act_gating(act)
        act_merge(act)
        act_block1_out(act)
        for j in range(KC):
            act_squares(act, 2, j, X[:, j, :], (x_upd, j + 1))
        act_gla_in(act)
        act_root_fill(act, 2, 1, 3, U_LR)
        act_gla(act)
        act_mixer_out(act, 0, 4, U_GO, 3, lambda j: (gy_ready, j + 1), len(GLA_CUT_AT))
        act_ple(act, 0, U_PLE0, 4, 1)
        act_fox_in(act)
        act_root_fill(act, 4, 2, 6, U_F)
        act_fox(act)
        act_mixer_out(act, 1, 7, U_FO, 5, lambda j: (fo_read, (j + 1) * NB), len(FOX_CUT_AT))
        act_ple(act, 1, U_PLE1, 6, 2)
        act_root(act, 6)

    @block.vector
    def _(dve):
        dve_block1_in(dve)
        dve_swa(dve)
        dve_sgu(dve)
        dve_gating(dve)
        dve_merge(dve)
        dve_block1_out(dve)
        dve_gla_in(dve)
        dve_norm_fill(dve, 2, 1, 3, lambda j: col("norm0", j))
        dve_gla(dve)
        dve_mixer_out(dve, 0, 4, U_GO, 3, len(GLA_CUT_AT))
        dve_ple(dve, 0, U_PLE0, 4, 1)
        dve_norm_fill(dve, 4, 2, 6, lambda j: col("norm1", j))
        dve_fox(dve)
        dve_mixer_out(dve, 1, 7, U_FO, 5, len(FOX_CUT_AT))
        dve_ple(dve, 1, U_PLE1, 6, 2)
        dve_final(dve, 6)

    ctx.close()




def _tile(w):
    return w.reshape(KC, P, -1).transpose(1, 0, 2).reshape(P, -1)


def _weight_tiles(x):
    w_in, gla, fox = x["w_in"][0], x["gla_w_in_2"][0], x["fox_w_in_2"][0]
    a = SWA_HEADS * HD
    kv = SWA_KV * HD
    at = np.cumsum([0, a, kv, kv, a, HALF, HALF, HALF, 2 * D])
    half = SWA_HEADS // 2

    def paired(w):
        return w.reshape(-1, SWA_HEADS, HD)[:, [h for j in range(half) for h in (j, j + half)]].reshape(w.shape)

    def chunks(w):
        return [w[:, i:i + P] for i in range(0, w.shape[1], P)]

    def padded(w):
        return np.concatenate([w, np.zeros((D, P - w.shape[1]), np.float32)], 1)

    q, k, v, za, u, vb, zb, g = [w_in[:, at[i]:at[i + 1]] for i in range(8)]
    vb = chunks(vb)
    tiles = chunks(paired(q)) + [k, v] + chunks(g) + [vb[i] for i in (2, 3, 0, 1)]
    tiles += chunks(paired(za)) + chunks(u) + chunks(zb)
    pa = paired(x["w_proj_a"][0].T).T
    tiles += chunks(np.concatenate([pa, x["w_proj_b"][0]], 0)) + chunks(x["w_out"][0])
    kd, vd = D // 2, D
    tiles.append(padded(gla[:, 2 * kd + 2 * vd:]))
    for h in range(GLA_HEADS):
        tiles += [gla[:, h * P:(h + 1) * P], gla[:, kd + h * P:kd + (h + 1) * P]]
        for o in (2 * kd, 2 * kd + vd):
            two = chunks(gla[:, o + 2 * h * P:o + 2 * (h + 1) * P])
            tiles += two[::-1] if o == 2 * kd and h % 2 else two
    tiles += chunks(x["gla_w_out_2"][0]) + chunks(x["ple_gate_2"][0])
    tiles.append(padded(fox[:, 4 * D:]))
    for p in range(KC):
        tiles += [fox[:, o * D + p * P:o * D + (p + 1) * P] for o in range(4)]
    tiles += chunks(x["fox_w_out_2"][0]) + chunks(x["ple_gate_2"][1])
    assert len(tiles) == N_TILES
    return np.stack([_tile(t) for t in tiles])


def _columns(x):
    out = np.zeros((P, N_COLS), np.float32)

    def put(name, v, j=0):
        v = np.asarray(v, np.float32).reshape(-1, P).T
        out[:, COL[name][0] + j:COL[name][0] + j + v.shape[1]] = v

    for name, v in (("g_pre", x["g_pre"]), ("g_post", x["g_post"]), ("b_ada", x["b_ada"]), ("c", x["c"]),
                    ("norm0", x["norm_mixer_2"][0]), ("norm1", x["norm_mixer_2"][1]), ("ple0", x["ple_norm_2"][0]),
                    ("ple1", x["ple_norm_2"][1]), ("final", x["final_norm_2"]), ("o_gain", x["gla_o_norm_2"])):
        put(name, v)
    put("q_gain", np.tile(x["fox_q_norm_2"][0], 2))
    put("k_gain", np.tile(x["fox_k_norm_2"][0], 2))
    out[:FOX_HEADS, COL["b_f"][0]] = x["fox_b_f_2"][0]
    f = np.arange(P) % (HD // 2)
    put("inv_freq", np.float32(10000.0) ** (-(f.astype(np.float32)) / np.float32(HD // 2)))
    put("rope_sign", np.where(np.arange(P) % HD < HD // 2, 1.0, -1.0))
    put("eps", np.full(P, EPS))
    put("eps64", np.full(P, HD * EPS))
    r, h = np.arange(P)[:, None], np.arange(FOX_HEADS)[None, :]
    at, n = COL["selector"]
    out[:, at:at + n] = np.where((r == h) | (r == h + 32), -1.0, 0.0)
    put("half_pi", np.full(P, np.pi / 2))
    return out


def _matrices():
    r, c = np.arange(P)[:, None], np.arange(P)[None, :]
    same = r // GLA_CHUNK == c // GLA_CHUNK
    m = {
        "ident": r == c,
        "ones": np.ones((P, P)),
        "head_ones": r // HD == c // HD,
        "hide_all": np.full((P, P), NEG),
        "hide_prev": np.where(c > r, 0.0, NEG),
        "hide_cur": np.where(c <= r, 0.0, NEG),
        "chunk_sum": np.where((r <= c) & same, 1.0 / GLA_NORMALIZER, 0.0),
        "chunk_mask": (r <= c) & same,
        "causal_sum": r <= c,
        "causal_w": r <= c,
    }
    return np.stack([np.asarray(m[n], np.float32) for n in MAT], 1)


def kernel(**inputs):
    import concourse.bacc as bacc
    from concourse.bass_utils import run_bass_kernel_spmd

    x = {k: np.asarray(v) for k, v in inputs.items()}
    rows = np.concatenate([x["sinks"].ravel(), x["ln_v_g"].ravel(), x["ln_v_b"].ravel(), x["b_s"].ravel(),
                           x["gla_b_a_2"].ravel()])[None]
    arrays = {
        "xT": x["x"][0].T.reshape(KC, P, S),
        "pT": x["p_2"][:, 0].transpose(0, 2, 1).reshape(2, 2, P, S),
        "pos": x["positions"].astype(np.int32),
        "cols": _columns(x),
        "rows": rows,
        "mats": _matrices(),
        "w_ada": np.stack([x["w_ada"][0][:, i * D:(i + 1) * D].reshape(KC, P, D).transpose(1, 0, 2) for i in (1, 0, 2)]),
        "w_tiles": _weight_tiles(x),
        "ws_t": x["w_s"][0].transpose(2, 0, 1),
        "w_a2": x["gla_w_a2_2"][0],
        "ple_w": x["ple_proj_2"].reshape(2, 2, P, D),
    }
    arrays = {k: np.ascontiguousarray(v) for k, v in arrays.items()}
    nc = bacc.Bacc("TRN2", target_bir_lowering=False, num_devices=1)
    args = [nc.dram_tensor(k, v.shape, mybir.dt.from_np(v.dtype), kind="ExternalInput").ap() for k, v in arrays.items()]
    out = nc.dram_tensor("outT", (KC, P, S), F32, kind="ExternalOutput").ap()
    build(nc, *args, out)
    r = run_bass_kernel_spmd(nc, [arrays], core_ids=[0])
    return np.ascontiguousarray(r.results[0]["outT"].reshape(D, S).T)[None]
```
